# Optimizing a Trainium2 kernel written in Bass

```python
import math
import jax, jax.numpy as jnp
from jax import lax
import numpy as np
import jax
import jax.numpy as jnp

D_MODEL = 1024
BATCH = 1
SEQ = 256
DEPTH = 1

POOL_WINDOWS = (2, 4, 8, 16)
POOL_GROUPS = 4
POOL_GROUP_DIM = 128
POOL_WIDTH = POOL_GROUPS * POOL_GROUP_DIM
ATTN_HEADS = 8
ATTN_HEAD_DIM = 128
ATTN_WIDTH = ATTN_HEADS * ATTN_HEAD_DIM
KV_DIM = ATTN_HEAD_DIM
IDX_HEADS = 4
IDX_DIM = 64
TOPK_MAX = 256
Q_BLOCK = 128
N_BUCKETS = 32
MAX_DISTANCE = 128
N_MEM = 256
MEM_HEADS = 4
MEM_HEAD_DIM = 128
MEM_WIDTH = MEM_HEADS * MEM_HEAD_DIM
D_FF = -(-8 * D_MODEL // (3 * 256)) * 256
EPS = 1e-6

IN_SPLITS = (POOL_WIDTH, ATTN_WIDTH, KV_DIM, KV_DIM, IDX_HEADS * IDX_DIM, IDX_DIM, IDX_HEADS, D_MODEL, D_MODEL)
IN_WIDTH = sum(IN_SPLITS)


def _rmsnorm(x, g):
    xf = x.astype(jnp.float32)
    y = xf * lax.rsqrt(jnp.mean(xf * xf, axis=-1, keepdims=True) + EPS)
    return (y * g.astype(jnp.float32)).astype(x.dtype)

def _t5_bucket(dist):
    n = jnp.maximum(dist, 0)
    max_exact = N_BUCKETS // 2
    nf = jnp.maximum(n, 1).astype(jnp.float32)
    large = max_exact + (jnp.log(nf / max_exact) / math.log(MAX_DISTANCE / max_exact)
                         * (N_BUCKETS - max_exact)).astype(jnp.int32)
    large = jnp.minimum(large, N_BUCKETS - 1)
    return jnp.where(n < max_exact, n, large)

def _pool_mixer(u, pool_w, pool_scale):
    B, S, _ = u.shape
    ug = u.reshape(B, S, POOL_GROUPS, POOL_GROUP_DIM).astype(jnp.float32)
    cs = jnp.concatenate([jnp.zeros((B, 1, POOL_GROUPS, POOL_GROUP_DIM), jnp.float32),
                          jnp.cumsum(ug, axis=1)], axis=1)
    win = jnp.array(POOL_WINDOWS, jnp.int32)
    t1 = jnp.arange(1, S + 1, dtype=jnp.int32)[:, None]
    lo = jnp.maximum(t1 - win[None, :], 0)
    cnt = jnp.minimum(t1, win[None, :]).astype(jnp.float32)
    g_idx = jnp.arange(POOL_GROUPS)[None, :]
    mean = (cs[:, 1:] - cs[:, lo, g_idx, :]) / cnt[None, :, :, None]
    pooled = (mean - ug).astype(u.dtype)
    mixed = jnp.einsum('bsgc,gcd->bsgd', pooled, pool_w)
    return mixed.reshape(B, S, POOL_WIDTH) * pool_scale

def _sparse_attention(q, k, v, q_idx, k_idx, w_idx, rel_bias_table):
    B, S = q.shape[:2]
    n_sel = min(TOPK_MAX, S // 4)
    nb = S // Q_BLOCK
    key_pos = jnp.arange(S, dtype=jnp.int32)
    idx_scale = IDX_DIM ** -0.5
    w_scale = IDX_HEADS ** -0.5
    attn_scale = ATTN_HEAD_DIM ** -0.5

    def blockify(a):
        return a.reshape((B, nb, Q_BLOCK) + a.shape[2:]).swapaxes(0, 1)

    def one_block(args):
        qb, qib, wb, start = args
        q_pos = start + jnp.arange(Q_BLOCK, dtype=jnp.int32)
        dots = jnp.einsum('bthd,bsd->bths', qib, k_idx).astype(jnp.float32) * idx_scale
        score = jnp.einsum('bths,bth->bts', jax.nn.relu(dots), wb.astype(jnp.float32) * w_scale)
        causal = key_pos[None, :] <= q_pos[:, None]
        score = jnp.where(causal[None], score, -jnp.inf)
        _, sel = lax.top_k(score, n_sel)
        valid = sel <= q_pos[None, :, None]
        kg = jax.vmap(lambda kb, ib: kb[ib])(k, sel)
        vg = jax.vmap(lambda vb, ib: vb[ib])(v, sel)
        logits = jnp.einsum('bthd,btkd->bhtk', qb, kg).astype(jnp.float32) * attn_scale
        bias = rel_bias_table[_t5_bucket(q_pos[None, :, None] - sel)]
        logits = logits + jnp.moveaxis(bias, -1, 1).astype(jnp.float32)
        logits = jnp.where(valid[:, None], logits, -jnp.inf)
        p = jax.nn.softmax(logits, axis=-1).astype(vg.dtype)
        return jnp.einsum('bhtk,btkd->bthd', p, vg)

    starts = jnp.arange(nb, dtype=jnp.int32) * Q_BLOCK
    out = lax.map(one_block, (blockify(q), blockify(q_idx), blockify(w_idx), starts))
    return out.swapaxes(0, 1).reshape(B, S, ATTN_HEADS * ATTN_HEAD_DIM)

def _mixer_sublayer(h, w_in, pool_w, pool_scale, w_proj_pool, w_proj_attn, rel_bias_table, w_out):
    B, S, _ = h.shape
    proj = h @ w_in
    offs = np.cumsum(IN_SPLITS)[:-1].tolist()
    u_pool, q, k, v, q_idx, k_idx, w_idx, g_pool, g_attn = jnp.split(proj, offs, axis=-1)
    a = _pool_mixer(u_pool, pool_w, pool_scale) @ w_proj_pool
    att = _sparse_attention(q.reshape(B, S, ATTN_HEADS, ATTN_HEAD_DIM), k, v,
                            q_idx.reshape(B, S, IDX_HEADS, IDX_DIM), k_idx, w_idx,
                            rel_bias_table)
    b = att @ w_proj_attn
    merged = jax.nn.sigmoid(g_pool) * a + jax.nn.sigmoid(g_attn) * b
    return merged @ w_out

def _memory_cross_attention(h, mem, norm_mem_kv, w_q_mem, w_kv_mem, w_o_mem):
    B, S, _ = h.shape
    q = (h @ w_q_mem).reshape(B, S, MEM_HEADS, MEM_HEAD_DIM)
    kv = _rmsnorm(mem, norm_mem_kv) @ w_kv_mem
    k, v = jnp.split(kv, 2, axis=-1)
    k = k.reshape(B, N_MEM, MEM_HEADS, MEM_HEAD_DIM)
    v = v.reshape(B, N_MEM, MEM_HEADS, MEM_HEAD_DIM)
    logits = jnp.einsum('bshd,bmhd->bhsm', q, k).astype(jnp.float32) * MEM_HEAD_DIM ** -0.5
    p = jax.nn.softmax(logits, axis=-1).astype(v.dtype)
    o = jnp.einsum('bhsm,bmhd->bshd', p, v).reshape(B, S, MEM_WIDTH)
    return o @ w_o_mem

def _swiglu(h, w_gate_up, w_down):
    g, u = jnp.split(h @ w_gate_up, 2, axis=-1)
    return (jax.nn.silu(g) * u) @ w_down

def first_inputs(seed: int = 0) -> dict:
    key = jax.random.key(seed)
    ks = jax.random.split(key, 24)
    f32 = jnp.float32

    def w(k, shape, fan_in):
        return jax.random.normal(k, shape, f32) * fan_in ** -0.5

    def gain(k, n):
        return 1.0 + 0.02 * jax.random.normal(k, (n,), f32)

    return {
        "x": jax.random.normal(ks[0], (BATCH, SEQ, D_MODEL), f32),
        "mem": jax.random.normal(ks[1], (BATCH, N_MEM, D_MODEL), f32),
        "norm_mix_pre": gain(ks[2], D_MODEL),
        "norm_mix_post": gain(ks[3], D_MODEL),
        "w_in": w(ks[4], (D_MODEL, IN_WIDTH), D_MODEL),
        "pool_w": w(ks[5], (POOL_GROUPS, POOL_GROUP_DIM, POOL_GROUP_DIM), POOL_GROUP_DIM),
        "pool_scale": gain(ks[6], POOL_WIDTH),
        "w_proj_pool": w(ks[7], (POOL_WIDTH, D_MODEL), POOL_WIDTH),
        "w_proj_attn": w(ks[8], (ATTN_WIDTH, D_MODEL), ATTN_WIDTH),
        "rel_bias_table": 0.5 * jax.random.normal(ks[9], (N_BUCKETS, ATTN_HEADS), f32),
        "w_out": w(ks[10], (D_MODEL, D_MODEL), D_MODEL),
        "norm_mem_pre": gain(ks[11], D_MODEL),
        "norm_mem_kv": gain(ks[12], D_MODEL),
        "norm_mem_post": gain(ks[13], D_MODEL),
        "w_q_mem": w(ks[14], (D_MODEL, MEM_WIDTH), D_MODEL),
        "w_kv_mem": w(ks[15], (D_MODEL, 2 * MEM_WIDTH), D_MODEL),
        "w_o_mem": w(ks[16], (MEM_WIDTH, D_MODEL), MEM_WIDTH),
        "norm_ffn_pre": gain(ks[17], D_MODEL),
        "norm_ffn_post": gain(ks[18], D_MODEL),
        "w_gate_up": w(ks[19], (D_MODEL, 2 * D_FF), D_MODEL),
        "w_down": w(ks[20], (D_FF, D_MODEL), D_FF),
    }

def first_block(x, mem, norm_mix_pre, norm_mix_post, w_in, pool_w, pool_scale, w_proj_pool,
              w_proj_attn, rel_bias_table, w_out, norm_mem_pre, norm_mem_kv, norm_mem_post,
              w_q_mem, w_kv_mem, w_o_mem, norm_ffn_pre, norm_ffn_post, w_gate_up, w_down):
    for _ in range(DEPTH):
        h = _rmsnorm(x, norm_mix_pre)
        x = x + _rmsnorm(_mixer_sublayer(h, w_in, pool_w, pool_scale, w_proj_pool,
                                         w_proj_attn, rel_bias_table, w_out), norm_mix_post)
        h = _rmsnorm(x, norm_mem_pre)
        x = x + _rmsnorm(_memory_cross_attention(h, mem, norm_mem_kv, w_q_mem, w_kv_mem, w_o_mem),
                         norm_mem_post)
        h = _rmsnorm(x, norm_ffn_pre)
        x = x + _rmsnorm(_swiglu(h, w_gate_up, w_down), norm_ffn_post)
    return x


DEPTH_2 = 2

N_A_LAYERS = DEPTH_2 // 2
N_B_LAYERS = DEPTH_2 - N_A_LAYERS
DN_ALPHA = (2.0 * DEPTH_2) ** 0.25
DN_BETA = (8.0 * DEPTH_2) ** -0.25
LN_EPS = 1e-5
FFN_DIM = int(math.ceil(8 * D_MODEL / 3 / 256)) * 256
SGU_HIDDEN = 4 * D_MODEL
SGU_HALF = SGU_HIDDEN // 2
SGU_GROUPS = 8
SGU_GROUP_DIM = SGU_HALF // SGU_GROUPS
SGU_CHUNK = 128
N_HEADS = 16
N_KV_GROUPS = 4
HEADS_PER_GROUP = N_HEADS // N_KV_GROUPS
HEAD_DIM = D_MODEL // N_HEADS
CMP_LEN = 32
CMP_STRIDE = 16
PHI_HIDDEN = 256
SEL_LEN = 64
SEL_TOP_N = 8
N_LOCAL_BLOCKS = 2
WINDOW = 512
NSA_Q_BLOCK = 32
N_KV_SLOTS = 6
REL_BUCKETS = 32
REL_MAX_DIST = 128
NEG = -1e30


def layer_norm(x, g, b):
    xf = x.astype(jnp.float32)
    mu = jnp.mean(xf, axis=-1, keepdims=True)
    var = jnp.mean(jnp.square(xf - mu), axis=-1, keepdims=True)
    y = (xf - mu) * lax.rsqrt(var + LN_EPS)
    return (y * g.astype(jnp.float32) + b.astype(jnp.float32)).astype(x.dtype)

def post_norm(x, sub, g, b):
    return layer_norm(DN_ALPHA * x + sub, g, b)

def swiglu(x, w1, w3, w2):
    return (jax.nn.silu(x @ w1) * (x @ w3)) @ w2

def rel_bucket(dist):
    n = jnp.maximum(dist, 0)
    max_exact = REL_BUCKETS // 2
    nf = jnp.maximum(n, 1).astype(jnp.float32)
    large = max_exact + (jnp.log(nf / max_exact) / math.log(REL_MAX_DIST / max_exact)
                         * (REL_BUCKETS - max_exact)).astype(jnp.int32)
    return jnp.where(n < max_exact, n, jnp.minimum(large, REL_BUCKETS - 1))

def chunked_sgu_mixer(x, w_in, ln_g, ln_b, w_s, b_s, w_out):
    B, S, _ = x.shape
    z = jax.nn.gelu(x @ w_in, approximate=False)
    u, v = jnp.split(z, 2, axis=-1)
    v = layer_norm(v, ln_g, ln_b)
    n_chunks = S // SGU_CHUNK
    v = v.reshape(B, n_chunks, SGU_CHUNK, SGU_GROUPS, SGU_GROUP_DIM)
    causal = jnp.tril(jnp.ones((SGU_CHUNK, SGU_CHUNK), dtype=bool))
    w = jnp.where(causal[None], w_s, jnp.zeros_like(w_s))
    mixed = jnp.einsum('gts,bnsgc->bntgc', w, v) + b_s.T[None, None, :, :, None]
    return (u * mixed.reshape(B, S, SGU_HALF)) @ w_out

def compress(kv, pe, w1, b1, w2):
    B, S, G, Dh = kv.shape
    n_sub = CMP_LEN // CMP_STRIDE
    n_chunks = S // CMP_STRIDE
    n_cmp = n_chunks - n_sub + 1
    chunks = kv.reshape(B, n_chunks, CMP_STRIDE, G, Dh)
    blocks = jnp.concatenate([chunks[:, i:i + n_cmp] for i in range(n_sub)], axis=2)
    blocks = blocks + pe[None, None, :, None, :]
    flat = blocks.transpose(0, 1, 3, 2, 4).reshape(B, n_cmp, G, CMP_LEN * Dh)
    return jax.nn.gelu(flat @ w1 + b1, approximate=False) @ w2

def nsa_shared_kv(h, kv_w, cmp_pe, cmp_w1, cmp_b1, cmp_w2):
    B, S, _ = h.shape
    kv = (h @ kv_w).reshape(B, S, N_KV_SLOTS, N_KV_GROUPS, HEAD_DIM)
    k_cmp = compress(kv[:, :, 0], cmp_pe[0], cmp_w1[0], cmp_b1[0], cmp_w2[0])
    v_cmp = compress(kv[:, :, 1], cmp_pe[1], cmp_w1[1], cmp_b1[1], cmp_w2[1])
    n_sel = S // SEL_LEN
    k_sel = kv[:, :, 2].reshape(B, n_sel, SEL_LEN, N_KV_GROUPS, HEAD_DIM).transpose(0, 3, 1, 2, 4)
    v_sel = kv[:, :, 3].reshape(B, n_sel, SEL_LEN, N_KV_GROUPS, HEAD_DIM).transpose(0, 3, 1, 2, 4)
    pad = ((0, 0), (WINDOW, 0), (0, 0), (0, 0))
    k_win = jnp.pad(kv[:, :, 4], pad)
    v_win = jnp.pad(kv[:, :, 5], pad)
    return (k_cmp, v_cmp, k_sel, v_sel, k_win, v_win)

def masked_softmax(s, mask):
    p = jax.nn.softmax(jnp.where(mask, s, NEG), axis=-1)
    return jnp.where(mask, p, 0.0)

def cmp_to_sel_overlap(n_cmp, n_sel):
    i = np.arange(n_cmp)[:, None]
    j = np.arange(n_sel)[None, :]
    ov = (i * CMP_STRIDE < (j + 1) * SEL_LEN) & (i * CMP_STRIDE + CMP_LEN > j * SEL_LEN)
    return ov.astype(np.float32)

def nsa_mixer(h, shared, w_qg, w_o, rel_table):
    k_cmp, v_cmp, k_sel, v_sel, k_win, v_win = shared
    B, S, _ = h.shape
    G, HG, Dh, QB = N_KV_GROUPS, HEADS_PER_GROUP, HEAD_DIM, NSA_Q_BLOCK
    qg = h @ w_qg
    q = qg[..., :N_HEADS * Dh].reshape(B, S, G, HG, Dh) * (Dh ** -0.5)
    gates = jax.nn.sigmoid(qg[..., N_HEADS * Dh:]).reshape(B, S, G, HG, 3)
    n_qb = S // QB
    n_cmp = k_cmp.shape[1]
    n_sel = k_sel.shape[2]
    n_top = min(SEL_TOP_N, n_sel)
    overlap = jnp.asarray(cmp_to_sel_overlap(n_cmp, n_sel))
    cmp_end = jnp.arange(n_cmp, dtype=jnp.int32) * CMP_STRIDE + (CMP_LEN - 1)
    sel_ids = jnp.arange(n_sel, dtype=jnp.int32)
    b_idx = jnp.arange(B)[:, None, None]
    g_idx = jnp.arange(G)[None, :, None]
    g_idx4 = jnp.arange(G)[None, :, None, None]
    tbl_g = rel_table.reshape(REL_BUCKETS, G, HG)

    def head_bias(dist):
        return rel_table[rel_bucket(dist)].reshape(dist.shape + (G, HG)).transpose(2, 3, 0, 1).astype(jnp.float32)

    def block(args):
        q_b, g_b, q0 = args
        t = q0 + jnp.arange(QB, dtype=jnp.int32)
        dist_c = t[:, None] - cmp_end[None, :]
        mask_c = dist_c >= 0
        s_c = jnp.einsum('bqghd,bngd->bghqn', q_b, k_cmp).astype(jnp.float32) + head_bias(dist_c)
        p_c = masked_softmax(s_c, mask_c)
        o_c = jnp.einsum('bghqn,bngd->bqghd', p_c.astype(v_cmp.dtype), v_cmp)
        imp = jnp.einsum('bghqn,nj->bgqj', p_c, overlap)
        cur = t // SEL_LEN
        valid = sel_ids[None, :] <= cur[:, None]
        forced = valid & ((sel_ids[None, :] == 0) | (sel_ids[None, :] > cur[:, None] - N_LOCAL_BLOCKS))
        imp = jnp.where(forced, -NEG, jnp.where(valid, imp, NEG))
        _, idx = lax.top_k(imp, n_top)
        flat = idx.reshape(B, G, QB * n_top)
        k_g = k_sel[b_idx, g_idx, flat].reshape(B, G, QB, n_top * SEL_LEN, Dh)
        v_g = v_sel[b_idx, g_idx, flat].reshape(B, G, QB, n_top * SEL_LEN, Dh)
        pos = (idx[..., None] * SEL_LEN + jnp.arange(SEL_LEN, dtype=jnp.int32)).reshape(B, G, QB, n_top * SEL_LEN)
        dist_s = t[None, None, :, None] - pos
        mask_s = (dist_s >= 0)[:, :, None]
        bias_s = tbl_g[rel_bucket(dist_s), g_idx4].transpose(0, 1, 4, 2, 3).astype(jnp.float32)
        s_s = jnp.einsum('bqghd,bgqkd->bghqk', q_b, k_g).astype(jnp.float32) + bias_s
        p_s = masked_softmax(s_s, mask_s)
        o_s = jnp.einsum('bghqk,bgqkd->bqghd', p_s.astype(v_g.dtype), v_g)
        k_w = lax.dynamic_slice_in_dim(k_win, q0, WINDOW + QB, axis=1)
        v_w = lax.dynamic_slice_in_dim(v_win, q0, WINDOW + QB, axis=1)
        pos_w = q0 - WINDOW + jnp.arange(WINDOW + QB, dtype=jnp.int32)
        dist_w = t[:, None] - pos_w[None, :]
        mask_w = (dist_w >= 0) & (dist_w < WINDOW) & (pos_w[None, :] >= 0)
        s_w = jnp.einsum('bqghd,bkgd->bghqk', q_b, k_w).astype(jnp.float32) + head_bias(dist_w)
        p_w = masked_softmax(s_w, mask_w)
        o_w = jnp.einsum('bghqk,bkgd->bqghd', p_w.astype(v_w.dtype), v_w)
        return g_b[..., 0:1] * o_c + g_b[..., 1:2] * o_s + g_b[..., 2:3] * o_w

    q_blocks = q.reshape(B, n_qb, QB, G, HG, Dh).swapaxes(0, 1)
    g_blocks = gates.reshape(B, n_qb, QB, G, HG, 3).swapaxes(0, 1)
    starts = jnp.arange(n_qb, dtype=jnp.int32) * QB
    out = lax.map(block, (q_blocks, g_blocks, starts))
    out = out.swapaxes(0, 1).reshape(B, S, N_HEADS * Dh)
    return out @ w_o

def second_inputs(seed: int = 0) -> dict:
    key = jax.random.key(seed)
    ks = jax.random.split(key, 24)
    f32 = jnp.float32

    def nrm(k, shape, scale):
        return jax.random.normal(k, shape, f32) * scale

    kv_scale = jnp.array([1.0, DN_BETA, 1.0, DN_BETA, 1.0, DN_BETA], f32)[None, :, None]
    kv_w = (nrm(ks[13], (D_MODEL, N_KV_SLOTS, N_KV_GROUPS * HEAD_DIM), D_MODEL ** -0.5) * kv_scale)
    return {
        'x': nrm(ks[0], (BATCH, SEQ, D_MODEL), 1.0),
        'rel_table': nrm(ks[1], (REL_BUCKETS, N_HEADS), 0.5),
        'ln_g': 1.0 + nrm(ks[2], (DEPTH_2, 3, D_MODEL), 0.05),
        'ln_b': nrm(ks[3], (DEPTH_2, 3, D_MODEL), 0.02),
        'ffn_w1': nrm(ks[4], (DEPTH_2, 2, D_MODEL, FFN_DIM), D_MODEL ** -0.5),
        'ffn_w3': nrm(ks[5], (DEPTH_2, 2, D_MODEL, FFN_DIM), D_MODEL ** -0.5),
        'ffn_w2': nrm(ks[6], (DEPTH_2, 2, FFN_DIM, D_MODEL), DN_BETA * FFN_DIM ** -0.5),
        'sgu_w_in': nrm(ks[7], (N_A_LAYERS, D_MODEL, SGU_HIDDEN), D_MODEL ** -0.5),
        'sgu_ln_g': 1.0 + nrm(ks[8], (N_A_LAYERS, SGU_HALF), 0.05),
        'sgu_ln_b': nrm(ks[9], (N_A_LAYERS, SGU_HALF), 0.02),
        'sgu_w_s': nrm(ks[10], (N_A_LAYERS, SGU_GROUPS, SGU_CHUNK, SGU_CHUNK), 0.05),
        'sgu_b_s': 1.0 + nrm(ks[11], (N_A_LAYERS, SGU_GROUPS, SGU_CHUNK), 0.05),
        'sgu_w_out': nrm(ks[12], (N_A_LAYERS, SGU_HALF, D_MODEL), DN_BETA * SGU_HALF ** -0.5),
        'kv_w': kv_w.reshape(D_MODEL, N_KV_SLOTS * N_KV_GROUPS * HEAD_DIM),
        'cmp_pe': nrm(ks[14], (2, CMP_LEN, HEAD_DIM), 0.5),
        'cmp_w1': nrm(ks[15], (2, CMP_LEN * HEAD_DIM, PHI_HIDDEN), (CMP_LEN * HEAD_DIM) ** -0.5),
        'cmp_b1': nrm(ks[16], (2, PHI_HIDDEN), 0.02),
        'cmp_w2': nrm(ks[17], (2, PHI_HIDDEN, HEAD_DIM), PHI_HIDDEN ** -0.5),
        'nsa_w_qg': nrm(ks[18], (N_B_LAYERS, D_MODEL, N_HEADS * HEAD_DIM + 3 * N_HEADS), D_MODEL ** -0.5),
        'nsa_w_o': nrm(ks[19], (N_B_LAYERS, N_HEADS * HEAD_DIM, D_MODEL), DN_BETA * (N_HEADS * HEAD_DIM) ** -0.5),
    }

def second_block(x, rel_table, ln_g, ln_b, ffn_w1, ffn_w3, ffn_w2, sgu_w_in, sgu_ln_g, sgu_ln_b, sgu_w_s,
              sgu_b_s, sgu_w_out, kv_w, cmp_pe, cmp_w1, cmp_b1, cmp_w2, nsa_w_qg, nsa_w_o):
    h = x
    shared = None
    for layer in range(DEPTH_2):
        if layer == N_A_LAYERS:
            shared = nsa_shared_kv(h, kv_w, cmp_pe, cmp_w1, cmp_b1, cmp_w2)
        h = post_norm(h, 0.5 * swiglu(h, ffn_w1[layer, 0], ffn_w3[layer, 0], ffn_w2[layer, 0]),
                      ln_g[layer, 0], ln_b[layer, 0])
        if layer < N_A_LAYERS:
            a = layer
            mix = chunked_sgu_mixer(h, sgu_w_in[a], sgu_ln_g[a], sgu_ln_b[a], sgu_w_s[a], sgu_b_s[a], sgu_w_out[a])
        else:
            bl = layer - N_A_LAYERS
            mix = nsa_mixer(h, shared, nsa_w_qg[bl], nsa_w_o[bl], rel_table)
        h = post_norm(h, mix, ln_g[layer, 1], ln_b[layer, 1])
        h = post_norm(h, 0.5 * swiglu(h, ffn_w1[layer, 1], ffn_w3[layer, 1], ffn_w2[layer, 1]),
                      ln_g[layer, 2], ln_b[layer, 2])
    return h


def setup_inputs(seed=0):
    out = dict(first_inputs(seed))
    for name, value in second_inputs(seed + 1).items():
        if name != "x":
            out[name + "_2"] = value
    return out


def reference(
    x, mem, norm_mix_pre, norm_mix_post, w_in, pool_w, pool_scale, w_proj_pool, w_proj_attn,
    rel_bias_table, w_out, norm_mem_pre, norm_mem_kv, norm_mem_post, w_q_mem, w_kv_mem, w_o_mem,
    norm_ffn_pre, norm_ffn_post, w_gate_up, w_down, rel_table_2, ln_g_2, ln_b_2, ffn_w1_2,
    ffn_w3_2, ffn_w2_2, sgu_w_in_2, sgu_ln_g_2, sgu_ln_b_2, sgu_w_s_2, sgu_b_s_2, sgu_w_out_2,
    kv_w_2, cmp_pe_2, cmp_w1_2, cmp_b1_2, cmp_w2_2, nsa_w_qg_2, nsa_w_o_2,
):
    x = first_block(
        x, mem, norm_mix_pre, norm_mix_post, w_in, pool_w, pool_scale, w_proj_pool, w_proj_attn,
        rel_bias_table, w_out, norm_mem_pre, norm_mem_kv, norm_mem_post, w_q_mem, w_kv_mem,
        w_o_mem, norm_ffn_pre, norm_ffn_post, w_gate_up, w_down,
    )
    return second_block(
        x, rel_table_2, ln_g_2, ln_b_2, ffn_w1_2, ffn_w3_2, ffn_w2_2, sgu_w_in_2, sgu_ln_g_2,
        sgu_ln_b_2, sgu_w_s_2, sgu_b_s_2, sgu_w_out_2, kv_w_2, cmp_pe_2, cmp_w1_2, cmp_b1_2,
        cmp_w2_2, nsa_w_qg_2, nsa_w_o_2,
    )


_drawn_inputs = setup_inputs


def setup_inputs(seed=0):
    import zlib

    import numpy as np

    out = dict(_drawn_inputs(seed))
    spreads = {}
    factors = {'norm_mix_post': 3.62,
     'pool_scale': 3.472,
     'norm_mem_pre': 4.209,
     'norm_mem_kv': 2.9,
     'norm_mem_post': 4.056,
     'norm_ffn_pre': 3.812,
     'norm_ffn_post': 16.072,
     'rel_table_2': 4.115,
     'sgu_ln_g_2': 8.0,
     'sgu_ln_b_2': 51.23,
     'sgu_b_s_2': 4.786,
     'cmp_b1_2': 24.293}
    for name, (base, spread) in spreads.items():
        noise = np.random.default_rng([zlib.crc32(name.encode()), seed]).standard_normal(out[name].shape)
        drawn = base * np.exp(spread * noise) if base else spread * noise
        out[name] = jnp.asarray(drawn.astype(out[name].dtype))
    for name, factor in factors.items():
        out[name] = (out[name] * factor).astype(out[name].dtype)
    return out
```

```python
from contextlib import ExitStack

import numpy as np

import concourse.bass as bass
from concourse import mybir

F32 = mybir.dt.float32
F32R = mybir.dt.float32r
I32 = mybir.dt.int32
ALU = mybir.AluOpType
ACT = mybir.ActivationFunctionType
AX_X = mybir.AxisListType.X

P = 128
D = 1024
S = 256
KD = D // P
DFF = 2816
FC = 256
FSTEPS = DFF // FC
HEADS1, HEADS2 = 8, 16
NCMP = 15
BIG_NEG = -1e30
TAKEN = -3e38
TOPK = S // 4
EPS1, EPS2 = 1e-6, 1e-5
ALPHA = 4.0 ** 0.25
UNIT = 2048
RING = 3

C_POOL, C_Q, C_K, C_QI, C_KI, C_GATE = 0, 512, 1536, 1792, 2048, 2116

V_MIX, V_MEMKV, V_MEM, V_FFN, V_PSCALE, V_LNG, V_LNB, V_B1, V_PE, V_BS, V_END = (
    0, 8, 16, 24, 32, 36, 84, 132, 136, 168, 176)
K_ID, K_HOT, K_TRI, K_ICNT, K_BLK, K_CMASK, K_REV, K_END = 0, 128, 640, 896, 960, 964, 996, 1124


def shape_constants():
    c = np.zeros((P, K_END), np.float32)
    c[:, K_ID:K_ID + P] = np.eye(P)
    c[:, K_REV:K_REV + P] = np.eye(P)[::-1]
    dist = np.arange(S)
    nf = np.maximum(dist, 1).astype(np.float32)
    large = 16 + (np.log(nf / np.float32(16)) / np.float32(np.log(8.0)) * np.float32(16)).astype(np.int32)
    bucket = np.where(dist < 16, dist, np.minimum(large, 31))
    for j in range(2 * S):
        c[bucket[S - 1 - j] if j < S else 32, K_HOT + j] = 1.0
    t = np.arange(P)
    c[:, K_TRI + P:K_TRI + 2 * P] = np.where(t[None, :] <= t[:, None], 0.0, BIG_NEG)
    for g in range(4):
        c[:, K_ICNT + 16 * g:K_ICNT + 16 * g + 16] = 1.0 / np.minimum(np.arange(16) + 1, 2 << g)
    for j in range(4):
        c[32 * j:32 * j + 32, K_BLK + j] = 1.0
    for tb in range(2):
        for n in range(NCMP):
            c[:, K_CMASK + 16 * tb + n] = (16 * n + 31 <= t + P * tb)
    return c


def build(nc, A, out):
    ctx = ExitStack()
    with ctx:
        def sb(name, shape, dt=F32):
            return ctx.enter_context(nc.sbuf_tensor(name, shape, dt))

        def sem(name):
            return ctx.enter_context(nc.semaphore(name))

        raw = sb("raw", [P, RING, UNIT])
        whi = sb("whi", [P, RING, UNIT], F32R)
        wlo = sb("wlo", [P, RING, UNIT], F32R)
        st_hi = sb("st_hi", [P, 16, S], F32R)
        st_lo = sb("st_lo", [P, 16, S], F32R)
        hid_hi = sb("hid_hi", [P, 2, S], F32R)
        hid_lo = sb("hid_lo", [P, 2, S], F32R)
        zero_r = sb("zero_r", [P, P], F32R)
        silu = sb("silu", [P, 2, FC])
        hidden = sb("hidden", [P, 2, FC])
        res = sb("res", [P, 2, D])
        tmp = sb("tmp", [P, 2, D])
        gb = sb("gb", [P, 2, D])
        con = sb("con", [P, K_END])
        vec = sb("vec", [P, V_END])
        table = sb("table", [P, P])
        sumsq = sb("sumsq", [P, 14])
        stats = sb("stats", [P, 2, 24])
        mv = sb("mv", [P, 2, 2])
        nrm = sb("nrm", [P, 2, 4])
        top8 = sb("top8", [P, 8])
        rowmax = sb("rowmax", [P, 3, 4])
        negmax = sb("negmax", [P, 3, 4])
        rowsum = sb("rowsum", [P, 3, 4])
        factor = sb("factor", [P, 3, 4])
        cmp_stat = sb("cmp_stat", [P, 3, 32])
        big = sb("big", [P, 16000])
        ps = ctx.enter_context(nc.psum_tensor("ps", [P, 8, 512], F32))
        bias_rows = nc.dram_tensor("bias_rows", [P, 512], F32)

        ident = con[:, K_ID:K_ID + P]
        reverse = con[:, K_REV:K_REV + P]

        def carve(start, *dims):
            n = int(np.prod(dims))
            a = big[:, start:start + n]
            if len(dims) == 2:
                return a.rearrange("p (a b) -> p a b", b=dims[1])
            if len(dims) == 3:
                return a.rearrange("p (a b c) -> p a b c", b=dims[1], c=dims[2])
            if len(dims) == 4:
                return a.rearrange("p (a b c d) -> p a b c d", b=dims[1], c=dims[2], d=dims[3])
            return a

        def view(ap, *dims):
            return bass.AP(ap.tensor, ap.offset, [list(ap.ap[0])] + [list(d) for d in dims])

        bias1 = carve(0, HEADS1, 384)
        gate = carve(3072, 2, 2, D)
        shifted1 = carve(3072, HEADS1, S)
        q1 = carve(7168, HEADS1, S)
        k1 = carve(9216, S)
        v1 = carve(9472, 2, P)
        prob1 = carve(9728, 3, 384)
        probT1 = carve(10880, 2, 384)
        kidx = carve(9728, 2, S)
        qidx = carve(10240, 2, S)
        score = carve(10752, 384)
        relu_w = carve(11136, S)
        upad = carve(11648, 4, 272)
        winA = carve(12736, 4, 272)
        winB = carve(13824, 4, 272)
        widx = carve(14912, 2, 4)
        selmask = carve(14920, 384)
        poolw = carve(15304, 4, P)
        memx = carve(0, 2, D)
        km = carve(3072, 4, S)
        vm = carve(4096, 2, 512)
        qm = carve(5120, 4, S)
        probm = carve(6144, 3, 512)
        probTm = carve(7680, 2, 512)
        zv = carve(0, 2, 2048)
        zu = carve(4096, 2, 2048)
        sgu_gb = carve(8192, 2, 2048)
        ws = carve(12288, 8, P)
        wsT = carve(13312, 8, P)
        bias2 = carve(0, HEADS2, S)
        shifted2 = carve(8192, HEADS2, S)
        q2 = carve(4096, HEADS2, S)
        k2 = carve(8192, 2, 2, S)
        v2 = carve(9216, 2, 2, S)
        kc = carve(10240, 4, 32)
        vc = carve(10368, 4, 4, 64)
        gate2 = carve(11392, 2, 48)
        prob2 = carve(11488, 3, 768)
        probT2 = carve(13792, 2, 768)
        cmp_e = carve(11488, 4, P)
        cmp_f = carve(12000, 16, 60)
        cmp_g = carve(12960, 2, 4, 32)
        cmp_gr = carve(13216, 2, 4, P)
        cmp_w2 = carve(14240, 2, 2, P)
        tmpf = tmp[:, :, :].rearrange("p a b -> p (a b)")
        cmp_p = tmpf[:, 0:1024].rearrange("p (x n) -> p x n", n=32)
        cmp_pT = tmpf[:, 1024:2048].rearrange("p (g t) -> p g t", g=4)

        const_loaded = sem("const_loaded")
        x_loaded = sem("x_loaded")
        table_loaded = sem("table_loaded")
        rows_stored = sem("rows_stored")
        bias1_loaded = sem("bias1_loaded")
        bias2_loaded = sem("bias2_loaded")
        poolw_loaded = sem("poolw_loaded")
        memx_loaded = sem("memx_loaded")
        ws_loaded = sem("ws_loaded")
        sgu_gb_loaded = sem("sgu_gb_loaded")
        cmp_w2_loaded = sem("cmp_w2_loaded")
        gb_loaded = sem("gb_loaded")
        raw_loaded = [sem(f"raw_loaded{s}") for s in range(RING)]
        whi_ready = sem("whi_ready")
        wlo_ready = sem("wlo_ready")
        w_used = sem("w_used")
        bank_full = [sem(f"bank_full{b}") for b in range(8)]
        bank_read = [sem(f"bank_read{b}") for b in range(8)]
        hi_rounded = sem("hi_rounded")
        sumsq_ready = sem("sumsq_ready")
        xn_ready = sem("xn_ready")
        res_ready = sem("res_ready")
        silu_ready = sem("silu_ready")
        zeros_ready = sem("zeros_ready")
        selected = sem("selected")
        bias_masked = sem("bias_masked")
        pooled = sem("pooled")
        max_ready = sem("max_ready")
        exp_ready = sem("exp_ready")
        prob_ready = sem("prob_ready")
        ws_masked = sem("ws_masked")
        zv_normed = sem("zv_normed")
        zv_ready = sem("zv_ready")
        cmp_f_ready = sem("cmp_f_ready")
        cmp_gr_ready = sem("cmp_gr_ready")
        cmp_exp_in = sem("cmp_exp_in")
        cmp_exp_out = sem("cmp_exp_out")
        cmp_p_ready = sem("cmp_p_ready")
        act_step = sem("act_step")
        dve_step = sem("dve_step")
        pool_step = sem("pool_step")
        out_stored = sem("out_stored")

        unit_loads = []
        unit_len = []
        first = {}

        def slot_view(s, kt):
            return raw[:, s, :].rearrange("p (k c) -> p k c", k=kt)

        def rows(w, k0, kt, c0, cols):
            return w[k0 * P:(k0 + kt) * P, c0:c0 + cols].rearrange("(k p) c -> p k c", p=P)

        def unit(w, k0, kt, c0, cols):
            s = len(unit_loads) % RING
            dst = raw[:, s, 0:kt * cols].rearrange("p (k c) -> p k c", k=kt)
            h = kt // 2
            unit_loads.append([(dst[:, 0:h, :], rows(w, k0, h, c0, cols)),
                               (dst[:, h:kt, :], rows(w, k0 + h, h, c0, cols))])
            unit_len.append(kt * cols)

        def columns_256(name, w, c0, n):
            first[name] = len(unit_loads)
            for j in range(n):
                unit(w, 0, KD, c0 + 256 * j, 256)

        def chunks_512(name, w, c0, chunks, kt):
            first[name] = len(unit_loads)
            for c in range(chunks):
                for k0 in range(0, kt, 4):
                    unit(w, k0, 4, c0 + 512 * c, 512)

        def swiglu_units(n):
            first["ffn", n] = len(unit_loads)
            unit_loads.extend([None] * (3 * FSTEPS))
            unit_len.extend([UNIT] * (3 * FSTEPS))

        W_IN = A["w_in"]
        first["kidx"] = len(unit_loads)
        unit(W_IN, 0, KD, C_KI, P)
        columns_256("qidx", W_IN, C_QI, 1)
        columns_256("kv", W_IN, C_K, 1)
        columns_256("q", W_IN, C_Q, 4)
        columns_256("u", W_IN, C_POOL, 2)
        chunks_512("gate", W_IN, C_GATE, 4, KD)
        chunks_512("pp", A["w_proj_pool"], 0, 2, 4)
        chunks_512("pa", A["w_proj_attn"], 0, 2, KD)
        chunks_512("out", A["w_out"], 0, 2, KD)
        columns_256("km", A["w_kv_mem"], 0, 2)
        chunks_512("vm", A["w_kv_mem"], 512, 1, KD)
        columns_256("qm", A["w_q_mem"], 0, 2)
        chunks_512("om", A["w_o_mem"], 0, 2, 4)
        swiglu_units(0)
        swiglu_units(1)
        chunks_512("sgv", A["sgu_w_in_2"][0], 2048, 4, KD)
        chunks_512("sgu", A["sgu_w_in_2"][0], 0, 4, KD)
        chunks_512("sgo", A["sgu_w_out_2"][0], 0, 2, 16)
        swiglu_units(2)
        KV = A["kv_w_2"]
        for slot in range(2):
            columns_256(("cin", slot), KV, 256 * slot, 1)
            first["cw1", slot] = len(unit_loads)
            for k0 in (0, 8):
                unit(A["cmp_w1_2"][slot], k0, 8, 0, 256)
        columns_256("k2", KV, 512, 1)
        columns_256("v2", KV, 768, 1)
        columns_256("k2w", KV, 1024, 1)
        columns_256("v2w", KV, 1280, 1)
        swiglu_units(3)
        columns_256("q2", A["nsa_w_qg_2"][0], 0, 4)
        first["g2"] = len(unit_loads)
        unit(A["nsa_w_qg_2"][0], 0, KD, D, 48)
        chunks_512("o2", A["nsa_w_o_2"][0], 0, 2, KD)
        swiglu_units(4)
        UNITS = len(unit_loads)
        GU = A["w_gate_up"]
        SWIGLU = [(GU[:, 0:DFF], GU[:, DFF:2 * DFF], A["w_down"])]
        for a, b in ((0, 0), (0, 1), (1, 0), (1, 1)):
            SWIGLU.append((A["ffn_w1_2"][a, b], A["ffn_w3_2"][a, b], A["ffn_w2_2"][a, b]))

        def at(base, i=0):
            return base + RING * i, base % RING, base // RING + i

        use = {}
        fills = [0] * 8
        signal = {}
        signals = [0] * 8
        split_no = {}
        splits = [0]

        def plan(key, bank, split=False, times=1, unit=None):
            use[key] = (bank, fills[bank])
            fills[bank] += times
            if unit is None:
                signal[key] = (bank_full[bank], signals[bank] + 1)
                signals[bank] += times
            else:
                signal[key] = (w_used, unit + 1)
            if split:
                plan_split(key, times)

        def plan_split(key, times=1):
            split_no[key] = splits[0]
            splits[0] += times

        def plan_chunks(keys, banks, u0, units):
            for c, b in enumerate(banks):
                plan(keys(c, 0), b)
                plan(keys(c, 1), b + 1, unit=u0 + units * (c + 1) - 1)

        def plan_st(name, tiles=KD):
            for j in range(tiles // 2):
                plan(("st", name, j), 6 + j % 2, split=True)

        def plan_y(n, u0, units):
            for h in range(2):
                plan(("y", n, 0, h), h)
                plan(("y", n, 1, h), 2 + h, unit=u0 + units * (h + 1) - 1)

        def plan_ffn(n):
            plan(("up", n, 0), 4, times=FSTEPS)
            plan(("up", n, 1), 5, times=FSTEPS, unit=first["ffn", n] + 1)
            plan(("hid", n), 6, split=True, times=FSTEPS)
            for tb, h in ((0, 0), (0, 1), (1, 0)):
                plan(("y", ("ffn", n), tb, h), 2 * tb + h)
            plan(("y", ("ffn", n), 1, 1), 3, unit=first["ffn", n] + 3 * FSTEPS - 1)

        plan("rows", 0)
        plan_st("mix")
        plan("kidx", 4)
        plan("widx", 5, unit=first["kidx"])
        plan("qidx", 0, unit=first["qidx"])
        plan("kv", 1, unit=first["kv"])
        for j, b in enumerate((2, 3, 4)):
            plan(("dots", j), b)
        for j, b in enumerate((5, 0, 1, 5)):
            plan(("q", j), b, unit=first["q"] + j)
        for j in range(2):
            plan(("rev1", j), 6 + j)
        for j in range(2):
            plan(("u", j), j, unit=first["u"] + j)
        for j in range(2):
            plan(("rev1", 2 + j), 6 + j)
        plan_chunks(lambda c, tb: ("gate", c, tb), (2, 4, 0, 2), first["gate"], 2)
        for j in range(2):
            plan(("pool", j), 6 + j, split=True)
        plan_chunks(lambda c, tb: ("pp", c, tb), (4, 0), first["pp"], 1)
        for h in range(HEADS1):
            plan(("L1", h), h % 2)
            plan(("T1", h), 2 + h % 2)
            plan(("O1", h), 4 + h % 2, split=True)
        plan_chunks(lambda c, tb: ("pa", c, tb), (0, 2), first["pa"], 2)
        plan_st("merged")
        plan_y("mix", first["out"], 2)
        plan_st("mem")
        for j in range(2):
            plan(("km", j), 4 + j, unit=first["km"] + j)
        plan_chunks(lambda c, tb: ("vm", tb), (4,), first["vm"], 2)
        plan_st("memq")
        for j in range(2):
            plan(("qm", j), 4 + j, unit=first["qm"] + j)
        for h in range(4):
            plan(("Lm", h), h % 2)
            plan(("Tm", h), 2 + h % 2)
            plan(("Om", h), 4 + h % 2, split=True)
        plan_y("mem", first["om"], 1)
        plan_st("ffn0")
        plan_ffn(0)
        plan_st("b2")
        plan_ffn(1)
        plan_st("ln0")
        for j in range(2):
            plan(("wsT", j), 6 + j)
        plan_chunks(lambda c, tb: ("sgv", c, tb), (0, 2, 4, 0), first["sgv"], 2)
        plan_chunks(lambda c, tb: ("sgu", c, tb), (2, 4, 0, 2), first["sgu"], 2)
        for tb in range(2):
            for gp in range(4):
                plan(("mixed", tb, gp), 2 + gp)
        plan_st("um", 16)
        plan_y("sgu", first["sgo"], 4)
        for j in range(8):
            plan(("rev2", j), 4 + j % 4)
        plan_st("ln1")
        plan_ffn(2)
        plan_st("ln2")
        for slot in range(2):
            plan(("cin", slot), 4, unit=first["cin", slot])
            plan_split(("cf", slot))
            plan(("cg", slot, 0), 0)
            plan(("cg", slot, 1), 1, unit=first["cw1", slot] + 1)
        plan("kc", 5)
        plan("vc", 4)
        for j, name in enumerate(("k2", "v2", "k2w", "v2w")):
            plan(name, j, unit=first[name])
        plan_ffn(3)
        plan_st("ln3")
        for j in range(4):
            plan(("q2", j), j, unit=first["q2"] + j)
        plan("g2", 4, unit=first["g2"])
        plan("Lc", 5)
        for h in range(HEADS2):
            plan(("L2", h, 0), 2 * (h % 2))
            plan(("L2", h, 1), 2 * (h % 2) + 1)
            if h == 0:
                plan(("Tc", 0), 6)
                plan(("Tc", 1), 7)
            plan(("T2", h, 0), 6)
            plan(("T2", h, 1), 7)
            if h % 2 == 0:
                plan(("O2", h // 2), 4 + (h // 2) % 2, split=True)
        plan_y("nsa", first["o2"], 2)
        plan_st("ln4")
        plan_ffn(4)

        def bank(key):
            return ps[:, use[key][0], :]

        def full(key, i=0):
            s, n = signal[key]
            return s, n + i

        def read(key, i=0):
            b, n = use[key]
            return bank_read[b], n + 1 + i

        def is_full(key):
            return bank_full[use[key][0]], 1

        def is_read(key):
            return bank_read[use[key][0]], 1

        NORM_ORDER = ["mix", "mem", ("ffn", 0), ("ffn", 1), "sgu", ("ffn", 2), ("ffn", 3), "nsa", ("ffn", 4)]
        XN_ORDER = ["mix", "merged", "mem", "memq", "ffn0", "ln0", "ln1", "ln2", "ln3", "ln4",
                    "end"]
        XN = {name: 2 * i + 2 for i, name in enumerate(XN_ORDER)}
        SQ = {name: 2 * i for i, name in enumerate(["mix", "mem", "ymix", "memq", "ymem", "ffn0", "yffn0"])}
        RES = {name: 2 * i + 2 for i, name in enumerate(NORM_ORDER)}
        GBL = {}
        for i, name in enumerate(NORM_ORDER):
            GBL[name] = 16 * (i + 1) if i < 3 else 48 + 32 * (i - 2)
        ATT0 = {"self": 0, "mem": HEADS1, "nsa": HEADS1 + 4}

        block = ctx.enter_context(nc.Block())

        @block.sync
        def _(sp):
            sp.dma_start(res[:, :, :], A["x"][0].rearrange("(t p) d -> p t d", p=P)).then_inc(x_loaded, 16)
            sp.dma_start(con[:, :], A["shape_consts"]).then_inc(const_loaded, 16)
            sp.dma_start(vec[:, :], A["vectors"]).then_inc(const_loaded, 16)

            def slot_free(u):
                sp.wait_ge(wlo_ready, u - 2)

            def load_up(n, i, half, u, s):
                slot_free(u)
                dst = raw[:, s, :].rearrange("p (k g c) -> p k g c", k=4, g=2)
                for g in range(2):
                    w = SWIGLU[n][g][512 * half:512 * half + 512, bass.ds(FC * i, FC)]
                    sp.dma_start(dst[:, :, g, :], w.rearrange("(k p) c -> p k c", p=P)).then_inc(raw_loaded[s], 16)

            def load_down(n, i, u, s):
                slot_free(u)
                dst = slot_view(s, 2)
                w = SWIGLU[n][2][bass.ds(FC * i, FC), :].rearrange("(k p) c -> p k c", p=P)
                for h in range(2):
                    sp.dma_start(dst[:, h:h + 1, :], w[:, h:h + 1, :]).then_inc(raw_loaded[s], 16)

            def step(n, i, u0):
                for half in range(2):
                    u, s, _ = at(u0 + 2 + half, i - 1)
                    load_up(n, i, half, u, s)
                u, s, _ = at(u0 + 4, i - 1)
                load_down(n, i - 1, u, s)

            u = 0
            ffn = 0
            while u < UNITS:
                if unit_loads[u] is not None:
                    if u >= RING:
                        slot_free(u)
                    for dst, src in unit_loads[u]:
                        sp.dma_start(dst, src).then_inc(raw_loaded[u % RING], 16)
                    u += 1
                    continue
                for half in range(2):
                    load_up(ffn, 0, half, u + half, (u + half) % RING)
                with sp.Fori(1, FSTEPS - 1) as i:
                    step(ffn, i, u)
                step(ffn, FSTEPS - 1, u)
                last = u + 3 * FSTEPS - 1
                load_down(ffn, FSTEPS - 1, last, last % RING)
                u += 3 * FSTEPS
                ffn += 1
            for tb in range(2):
                sp.wait_ge(res_ready, RES["ffn", 4] - 1 + tb)
                sp.dma_start(out[0, tb * P:tb * P + P, :], res[:, tb, :]).then_inc(out_stored, 16)
            sp.wait_ge(out_stored, 32)

        @block.tensor
        def _(pe):
            def room(key):
                b, n = use[key]
                if n:
                    pe.wait_ge(bank_read[b], n)

            def product(o, a, b, start, stop):
                pe.matmul(o, a[0], b[0], start=start, stop=False)
                pe.matmul(o, a[0], b[1], start=False, stop=False)
                return pe.matmul(o, a[1], b[0], start=False, stop=stop)

            def weights(u, kt, cols):
                pe.wait_ge(wlo_ready, u + 1)
                s = u % RING
                n = kt * cols
                return [w[:, s, 0:n].rearrange("p (k c) -> p k c", k=kt) for w in (whi, wlo)]

            def features(u, tiles, k0=0):
                w = weights(u, KD, unit_len[u] // KD)
                for t, (c, o) in enumerate(tiles):
                    for k in range(KD):
                        mm = product(o, [x[:, k, c:c + P] for x in w], [x[:, k0 + k, :] for x in (st_hi, st_lo)],
                                     k == 0, k == KD - 1)
                return mm

            def tokens(w, outs, kts, k0, start, stop):
                done = []
                for tb, o in enumerate(outs):
                    for k in range(kts):
                        mm = product(o, [x[:, k0 + k, tb * P:tb * P + P] for x in (st_hi, st_lo)],
                                     [x[:, k, :] for x in w], start and k == 0, stop and k == kts - 1)
                    done.append(mm)
                return done

            def transpose_st(name, src, tiles, ready=None):
                if ready is not None:
                    pe.wait_ge(*ready)
                for j in range(tiles // 2):
                    key = ("st", name, j)
                    room(key)
                    for kk in range(2):
                        for tb in range(2):
                            k = 2 * j + kk
                            mm = pe.transpose(bank(key)[:, (2 * kk + tb) * P:(2 * kk + tb + 1) * P],
                                              src[:, tb, k * P:k * P + P], ident)
                    mm.then_inc(*is_full(key))

            def wait_st(name, tiles=KD):
                pe.wait_ge(*read(("st", name, tiles // 2 - 2)))
                pe.wait_ge(*read(("st", name, tiles // 2 - 1)))

            def chunked(u0, chunks, kt, keys, k0=0):
                u = u0
                for c in range(chunks):
                    for tb in range(2):
                        room(keys(c, tb))
                    for q in range(kt // 4):
                        w = weights(u, 4, 512)
                        last = q == kt // 4 - 1
                        mms = tokens(w, [bank(keys(c, tb)) for tb in range(2)], 4, k0 + 4 * q, q == 0, last)
                        if last:
                            mms[0].then_inc(*is_full(keys(c, 0)))
                        mms[1].then_inc(w_used, 1)
                        u += 1

            pe.wait_ge(const_loaded, 32)
            pe.wait_ge(table_loaded, 32)
            pe.wait_ge(zeros_ready, 1)
            pe.matmul(bank("rows"), table[:, :], con[:, K_HOT:K_HOT + 512], start=True,
                      stop=True).then_inc(*is_full("rows"))

            transpose_st("mix", tmp, KD, (xn_ready, XN["mix"]))
            wait_st("mix")
            room("kidx")
            u = first["kidx"]
            features(u, [(0, bank("kidx")[:, 0:S])]).then_inc(*is_full("kidx"))
            room("widx")
            w = weights(u, KD, P)
            mms = tokens([x[:, :, 64:68] for x in w], [bank("widx")[:, 4 * tb:4 * tb + 4] for tb in range(2)],
                         KD, 0, True, True)
            mms[1].then_inc(w_used, 1)
            room("qidx")
            u = first["qidx"]
            features(u, [(0, bank("qidx")[:, 0:S]), (P, bank("qidx")[:, S:2 * S])]).then_inc(w_used, 1)
            room("kv")
            u = first["kv"]
            features(u, [(0, bank("kv")[:, 0:S])])
            w = weights(u, KD, 256)
            mms = tokens([x[:, :, P:2 * P] for x in w],
                         [bank("kv")[:, S + tb * P:S + tb * P + P] for tb in range(2)], KD, 0, True, True)
            mms[1].then_inc(w_used, 1)

            pe.wait_ge(*read("kidx"))
            pe.wait_ge(*read("qidx"))
            room(("dots", 0))
            for j in range(2):
                mm = pe.matmul(bank(("dots", 0))[:, S * j:S * j + S].rearrange("p (a b) -> p a b", a=2),
                               qidx[:, j, 0:P], kidx[:, :, 0:P], start=True, stop=True)
            mm.then_inc(*is_full(("dots", 0)))
            for j in range(2):
                room(("dots", 1 + j))
                pe.matmul(bank(("dots", 1 + j)), qidx[:, j, P:2 * P], kidx[:, :, :].rearrange("p a b -> p (a b)"),
                          start=True, stop=True).then_inc(*is_full(("dots", 1 + j)))

            def feature_pairs(name, n, k0=0):
                for j in range(n):
                    key = (name, j)
                    room(key)
                    features(first[name] + j, [(0, bank(key)[:, 0:S]), (P, bank(key)[:, S:2 * S])],
                             k0).then_inc(w_used, 1)

            def reverse_rows(name, shifted, j):
                key = (name, j)
                room(key)
                pe.matmul(bank(key), reverse, shifted[:, 2 * j:2 * j + 2, :].rearrange("p a b -> p (a b)"),
                          start=True, stop=True).then_inc(*is_full(key))

            feature_pairs("q", 4)
            pe.wait_ge(bias1_loaded, 16)
            reverse_rows("rev1", shifted1, 0)
            reverse_rows("rev1", shifted1, 1)
            feature_pairs("u", 2)
            reverse_rows("rev1", shifted1, 2)
            reverse_rows("rev1", shifted1, 3)
            chunked(first["gate"], 4, KD, lambda c, tb: ("gate", c, tb))

            pe.wait_ge(pooled, 1)
            pe.wait_ge(poolw_loaded, 16)
            for j in range(2):
                room(("pool", j))
                for g in (2 * j, 2 * j + 1):
                    src = (winA, winB)[g % 2]
                    mm = pe.matmul(bank(("pool", j))[:, (g % 2) * S:(g % 2 + 1) * S], poolw[:, g, :],
                                   src[:, g, 16:272], start=True, stop=True)
                mm.then_inc(*is_full(("pool", j)))
            pe.wait_ge(*read(("pool", 0)))
            pe.wait_ge(*read(("pool", 1)))
            chunked(first["pp"], 2, 4, lambda c, tb: ("pp", c, tb), k0=8)

            for t in range(HEADS1 + 3):
                h = t
                if h < HEADS1:
                    if h == 0:
                        pe.wait_ge(*read(("q", 3)))
                        pe.wait_ge(*read("kv"))
                    room(("L1", h))
                    L = bank(("L1", h))
                    pe.matmul(L[:, 0:P], q1[:, h, 0:P], k1[:, 0:P], start=True, stop=True)
                    pe.matmul(L[:, P:3 * P], q1[:, h, P:S], k1[:, :], start=True,
                              stop=True).then_inc(*is_full(("L1", h)))
                h = t - 2
                if 0 <= h < HEADS1:
                    room(("T1", h))
                    pe.wait_ge(prob_ready, ATT0["self"] + h + 1)
                    T, pr = bank(("T1", h)), prob1[:, h % 3, :]
                    for c in range(3):
                        mm = pe.transpose(T[:, c * P:c * P + P], pr[:, c * P:c * P + P], ident)
                    mm.then_inc(*is_full(("T1", h)))
                h = t - 3
                if 0 <= h < HEADS1:
                    room(("O1", h))
                    pe.wait_ge(*read(("T1", h)))
                    O, pT = bank(("O1", h)), probT1[:, h % 2, :]
                    pe.matmul(O[:, 0:P], v1[:, 0, :], pT[:, 0:P], start=True, stop=True)
                    pe.matmul(O[:, P:S], v1[:, 0, :], pT[:, P:S], start=True, stop=False)
                    pe.matmul(O[:, P:S], v1[:, 1, :], pT[:, S:S + P], start=False,
                              stop=True).then_inc(*is_full(("O1", h)))
            for h in (HEADS1 - 2, HEADS1 - 1):
                pe.wait_ge(*read(("O1", h)))
            chunked(first["pa"], 2, KD, lambda c, tb: ("pa", c, tb))
            transpose_st("merged", tmp, KD, (xn_ready, XN["merged"]))
            wait_st("merged")
            chunked(first["out"], 2, KD, lambda c, tb: ("y", "mix", tb, c))

            transpose_st("mem", memx, KD, (xn_ready, XN["mem"]))
            wait_st("mem")
            feature_pairs("km", 2, 8)
            chunked(first["vm"], 1, KD, lambda c, tb: ("vm", tb), 8)
            transpose_st("memq", tmp, KD, (xn_ready, XN["memq"]))
            wait_st("memq")
            feature_pairs("qm", 2)
            for t in range(4 + 3):
                h = t
                if h < 4:
                    if h == 0:
                        pe.wait_ge(*read(("qm", 0)))
                        pe.wait_ge(*read(("qm", 1)))
                    room(("Lm", h))
                    for tb in range(2):
                        mm = pe.matmul(bank(("Lm", h))[:, tb * S:tb * S + S], qm[:, h, tb * P:tb * P + P],
                                       km[:, h, :], start=True, stop=True)
                    mm.then_inc(*is_full(("Lm", h)))
                h = t - 2
                if 0 <= h < 4:
                    room(("Tm", h))
                    pe.wait_ge(prob_ready, ATT0["mem"] + h + 1)
                    for kb in range(2):
                        for tb in range(2):
                            c = (2 * kb + tb) * P
                            mm = pe.transpose(bank(("Tm", h))[:, c:c + P],
                                              probm[:, h % 3, tb * S + kb * P:tb * S + kb * P + P], ident)
                    mm.then_inc(*is_full(("Tm", h)))
                h = t - 3
                if 0 <= h < 4:
                    room(("Om", h))
                    pe.wait_ge(*read(("Tm", h)))
                    for kb in range(2):
                        mm = pe.matmul(bank(("Om", h))[:, 0:S], vm[:, kb, h * P:h * P + P],
                                       probTm[:, h % 2, kb * S:kb * S + S], start=kb == 0, stop=kb == 1)
                    mm.then_inc(*is_full(("Om", h)))
            for h in (2, 3):
                pe.wait_ge(*read(("Om", h)))
            chunked(first["om"], 2, 4, lambda c, tb: ("y", "mem", tb, c), k0=8)

            def swiglu(n):
                u0 = first["ffn", n]
                up = [("up", n, tb) for tb in range(2)]
                hid = ("hid", n)
                ykeys = [[("y", ("ffn", n), tb, h) for h in range(2)] for tb in range(2)]

                def gate_up(i, base, j):
                    for half in range(2):
                        u, s, _ = at(base + half, j)
                        pe.wait_ge(wlo_ready, u + 1)
                        w = [x[:, s, :].rearrange("p (k c) -> p k c", k=4) for x in (whi, wlo)]
                        if half == 0:
                            for key in up:
                                b, c = use[key]
                                pe.wait_ge(bank_read[b], c + i)
                        mms = tokens(w, [bank(key) for key in up], 4, 4 * half, half == 0, half == 1)
                        if half == 1:
                            mms[0].then_inc(*is_full(up[0]))
                        mms[1].then_inc(w_used, 1)

                def down(i, base, j, end=False):
                    u, s, _ = at(base, j)
                    pe.wait_ge(wlo_ready, u + 1)
                    pe.wait_ge(*read(hid, i))
                    w = [x[:, s, :].rearrange("p (k c) -> p k c", k=2) for x in (whi, wlo)]
                    for tb in range(2):
                        for h in range(2):
                            for f in range(2):
                                mm = product(bank(ykeys[tb][h]),
                                             [x[:, f, tb * P:tb * P + P] for x in (hid_hi, hid_lo)],
                                             [x[:, f, 512 * h:512 * h + 512] for x in w], False, end and f == 1)
                            if end and (tb, h) != (1, 1):
                                mm.then_inc(*is_full(ykeys[tb][h]))
                    mm.then_inc(w_used, 1)

                def turn(i):
                    for key in up:
                        pe.wait_ge(*read(key, i))
                    b, c = use[hid]
                    pe.wait_ge(bank_read[b], c + i)
                    for f in range(2):
                        for tb in range(2):
                            mm = pe.transpose(bank(hid)[:, (2 * f + tb) * P:(2 * f + tb + 1) * P],
                                              hidden[:, tb, f * P:f * P + P], ident)
                    mm.then_inc(*is_full(hid))

                gate_up(0, u0, 0)
                for key in (k for pair in ykeys for k in pair):
                    room(key)
                    pe.matmul(bank(key), zero_r[:, :], st_hi[:, 0:2, :].rearrange("p a b -> p (a b)"), start=True,
                              stop=False)
                turn(0)
                with pe.Fori(1, FSTEPS - 1) as i:
                    gate_up(i, u0 + 2, i - 1)
                    down(i - 1, u0 + 4, i - 1)
                    turn(i)
                i = FSTEPS - 1
                gate_up(i, u0 + 2, i - 1)
                down(i - 1, u0 + 4, i - 1)
                turn(i)
                down(i, u0 + 3 * FSTEPS - 1, 0, end=True)

            transpose_st("ffn0", tmp, KD, (xn_ready, XN["ffn0"]))
            wait_st("ffn0")
            swiglu(0)

            pe.wait_ge(res_ready, RES["ffn", 0])
            transpose_st("b2", res, KD)
            wait_st("b2")
            swiglu(1)
            transpose_st("ln0", tmp, KD, (xn_ready, XN["ln0"]))
            wait_st("ln0")
            pe.wait_ge(ws_masked, 1)
            for j in range(2):
                room(("wsT", j))
                for q in range(4):
                    mm = pe.transpose(bank(("wsT", j))[:, q * P:q * P + P], ws[:, 4 * j + q, :], ident)
                mm.then_inc(*is_full(("wsT", j)))
            chunked(first["sgv"], 4, KD, lambda c, tb: ("sgv", c, tb))
            chunked(first["sgu"], 4, KD, lambda c, tb: ("sgu", c, tb))
            pe.wait_ge(zv_ready, 2)
            pe.wait_ge(*read(("wsT", 0)))
            pe.wait_ge(*read(("wsT", 1)))
            for tb in range(2):
                for gp in range(4):
                    key = ("mixed", tb, gp)
                    room(key)
                    for g in (2 * gp, 2 * gp + 1):
                        mm = pe.matmul(bank(key)[:, (g % 2) * S:(g % 2 + 1) * S], wsT[:, g, :],
                                       zv[:, tb, g * S:g * S + S], start=True, stop=True)
                    mm.then_inc(*is_full(key))
            for gp in range(4):
                pe.wait_ge(*read(("mixed", 1, gp)))
            transpose_st("um", zu, 16)
            wait_st("um", 16)
            chunked(first["sgo"], 2, 16, lambda c, tb: ("y", "sgu", tb, c))
            pe.wait_ge(bias2_loaded, 16)
            for j in range(8):
                reverse_rows("rev2", shifted2, j)
            transpose_st("ln1", tmp, KD, (xn_ready, XN["ln1"]))
            wait_st("ln1")
            swiglu(2)
            transpose_st("ln2", tmp, KD, (xn_ready, XN["ln2"]))
            wait_st("ln2")

            for slot in range(2):
                key = ("cin", slot)
                room(key)
                features(first["cin", slot], [(0, bank(key)[:, 0:S]), (P, bank(key)[:, S:2 * S])]).then_inc(w_used, 1)
                pe.wait_ge(cmp_f_ready, 2 * slot + 2)
                for f in range(2):
                    room(("cg", slot, f))
                fh, fl = (x[:, 8:12, :].rearrange("p a b -> p (a b)")[:, 0:960].rearrange("p (k c) -> p k c", k=16)
                          for x in (st_hi, st_lo))
                for half in range(2):
                    w = weights(first["cw1", slot] + half, KD, 256)
                    for f in range(2):
                        for k in range(KD):
                            mm = product(bank(("cg", slot, f))[:, 0:60], [x[:, k, f * P:f * P + P] for x in w],
                                         [x[:, 8 * half + k, :] for x in (fh, fl)], half == 0 and k == 0,
                                         half == 1 and k == KD - 1)
                        if half == 1 and f == 0:
                            mm.then_inc(*is_full(("cg", slot, 0)))
                    mm.then_inc(w_used, 1)
                pe.wait_ge(cmp_w2_loaded, 64)
                if slot == 0:
                    for f in range(2):
                        pe.wait_ge(*read(("cg", 0, f)))
                    room("kc")
                    for f in range(2):
                        mm = pe.matmul(bank("kc")[:, 0:P], cmp_w2[:, 0, f, :],
                                       cmp_g[:, f, :, :].rearrange("p a b -> p (a b)"), start=f == 0, stop=f == 1)
                    mm.then_inc(*is_full("kc"))
                else:
                    pe.wait_ge(cmp_gr_ready, 1)
                    room("vc")
                    for g in range(4):
                        for f in range(2):
                            mm = pe.matmul(bank("vc")[:, g * 64:g * 64 + 64], cmp_gr[:, f, g, :],
                                           cmp_w2[:, 1, f, 0:64], start=f == 0, stop=f == 1)
                    mm.then_inc(*is_full("vc"))
            for name in ("k2", "v2", "k2w", "v2w"):
                room(name)
                if name[0] == "k":
                    mm = features(first[name], [(0, bank(name)[:, 0:S]), (P, bank(name)[:, S:2 * S])])
                else:
                    w = weights(first[name], KD, 256)
                    mm = tokens(w, [bank(name)[:, tb * S:tb * S + S] for tb in range(2)], KD, 0, True, True)[1]
                mm.then_inc(w_used, 1)
            swiglu(3)
            transpose_st("ln3", tmp, KD, (xn_ready, XN["ln3"]))
            wait_st("ln3")

            feature_pairs("q2", 4)
            room("g2")
            w = weights(first["g2"], KD, 48)
            tokens(w, [bank("g2")[:, 48 * tb:48 * tb + 48] for tb in range(2)], KD, 0, True,
                   True)[1].then_inc(w_used, 1)
            for j in range(4):
                pe.wait_ge(*read(("q2", j)))
            room("Lc")
            for h in range(HEADS2):
                g, j = h // 4, h % 4
                for tb in range(2):
                    c = ((g * 2 + tb) * 4 + j) * 16
                    mm = pe.matmul(bank("Lc")[:, c:c + 16], q2[:, h, tb * P:tb * P + P], kc[:, g, 0:16],
                                   start=True, stop=True)
            mm.then_inc(*is_full("Lc"))
            pT = cmp_pT

            def scores2(h):
                pair = h // 8
                for tb in range(2):
                    key = ("L2", h, tb)
                    room(key)
                    n = P * (tb + 1)
                    pe.matmul(bank(key)[:, 0:2 * n].rearrange("p (a b) -> p a b", a=2), q2[:, h, tb * P:tb * P + P],
                              k2[:, pair, :, 0:n], start=True, stop=True).then_inc(*is_full(key))

            def turn2(h):
                pe.wait_ge(prob_ready, ATT0["nsa"] + h + 1)
                pr = prob2[:, h % 3, :]
                room(("T2", h, 0))
                T = bank(("T2", h, 0))
                for br in range(2):
                    pe.transpose(T[:, 2 * br * P:2 * br * P + P], pr[:, br * P:br * P + P], ident)
                    mm = pe.transpose(T[:, (2 * br + 1) * P:(2 * br + 2) * P], pr[:, S + br * S:S + br * S + P], ident)
                mm.then_inc(*is_full(("T2", h, 0)))
                room(("T2", h, 1))
                T = bank(("T2", h, 1))
                for br in range(2):
                    mm = pe.transpose(T[:, br * P:br * P + P], pr[:, S + br * S + P:S + br * S + S], ident)
                mm.then_inc(*is_full(("T2", h, 1)))

            def values2(h):
                key = ("O2", h // 2)
                if h % 2 == 0:
                    room(key)
                pe.wait_ge(*read(("T2", h, 0)))
                pe.wait_ge(*read(("T2", h, 1)))
                r = 64 * (h % 2)
                O, g, p = bank(key)[r:r + 64, :], h // 4, probT2[:, h % 2, :]
                pe.matmul(O[:, 0:S], vc[:, g, h % 4, :], pT[:, g, :], start=True, stop=False)
                for br in range(2):
                    pe.matmul(O[:, P:S], v2[:, 1, br, g * 64:g * 64 + 64],
                              p[:, 512 + br * P:512 + br * P + P], start=False, stop=False)
                for br in range(2):
                    mm = pe.matmul(O[:, 0:S], v2[:, 0, br, g * 64:g * 64 + 64], p[:, br * S:br * S + S], start=False,
                                   stop=br == 1)
                if h % 2:
                    mm.then_inc(*is_full(key))

            scores2(0)
            scores2(1)
            pe.wait_ge(cmp_p_ready, 1)
            for q in range(2):
                room(("Tc", q))
                for g in (2 * q, 2 * q + 1):
                    for tb in range(2):
                        c = ((g % 2) * 2 + tb) * P
                        x = (g * 2 + tb) * 4
                        mm = pe.transpose(bank(("Tc", q))[:, c:c + P],
                                          cmp_p[:, x:x + 4, :].rearrange("p a b -> p (a b)"), ident)
                mm.then_inc(*is_full(("Tc", q)))
            pe.wait_ge(*read(("Tc", 0)))
            pe.wait_ge(*read(("Tc", 1)))
            for t in range(2, HEADS2 + 3):
                if t < HEADS2:
                    scores2(t)
                if t - 2 < HEADS2:
                    turn2(t - 2)
                if 0 <= t - 3:
                    values2(t - 3)
            for j in (6, 7):
                pe.wait_ge(*read(("O2", j)))
            chunked(first["o2"], 2, KD, lambda c, tb: ("y", "nsa", tb, c))
            transpose_st("ln4", tmp, KD, (xn_ready, XN["ln4"]))
            wait_st("ln4")
            swiglu(4)

        @block.scalar
        def _(act):
            nxt = [0]
            chain = [0]

            def link(ins):
                chain[0] += 1
                ins.then_inc(act_step, 1)
                act.wait_ge(act_step, chain[0])

            def split(u, s, q, n=UNIT):
                act.wait_ge(raw_loaded[s], 32 * (q + 1))
                if not isinstance(u, int) or u >= RING:
                    act.wait_ge(w_used, u - 2)
                act.copy(whi[:, s, 0:n], raw[:, s, 0:n]).then_inc(whi_ready, 1)

            def beside(u):
                while nxt[0] <= min(u + 2, UNITS - 1):
                    n = nxt[0]
                    split(*at(n), unit_len[n])
                    nxt[0] += 1

            def st_out(key, dst, scale=None, bias=None):
                act.wait_ge(*full(key))
                src = bank(key)
                if scale is None:
                    mm = act.copy(dst.rearrange("p a b -> p (a b)"), src)
                else:
                    for kk in range(2):
                        if bias is None:
                            mm = act.mul(dst[:, kk, :], src[:, kk * S:kk * S + S], scale[:, kk:kk + 1])
                        else:
                            mm = act.activation(dst[:, kk, :], src[:, kk * S:kk * S + S], ACT.Identity,
                                                scale=scale[:, kk:kk + 1], bias=bias[:, kk:kk + 1])
                mm.then_inc(hi_rounded, 1)

            def st_all(name, tiles=KD, k0=0, v=None, vb=None):
                for j in range(tiles // 2):
                    k = 2 * j
                    st_out(("st", name, j), st_hi[:, k0 + k:k0 + k + 2, :],
                           None if v is None else vec[:, v + k:v + k + 2],
                           None if vb is None else vec[:, vb + k:vb + k + 2])

            def square(name, src, tb, junk):
                c = SQ[name] + tb
                act.activation(junk, src, ACT.Square, accum_out=sumsq[:, c:c + 1]).then_inc(sumsq_ready, 1)

            act.wait_ge(x_loaded, 16)
            for tb in range(2):
                square("mix", res[:, tb, :], tb, tmp[:, tb, :])
            beside(0)
            act.wait_ge(*full("rows"))
            act.copy(gb[:, 0, 0:512], bank("rows")).then_inc(*is_read("rows"))
            act.wait_ge(*read("rows"))
            act.dma_start(bias_rows[:, :], gb[:, 0, 0:512]).then_inc(rows_stored, 16)

            act.wait_ge(const_loaded, 32)
            st_all("mix", v=V_MIX)
            u = first["kidx"]
            beside(u)
            act.wait_ge(*full("kidx"))
            act.wait_ge(zeros_ready, 1)
            link(act.copy(kidx[0:64, 0, :], bank("kidx")[0:64, 0:S]))
            act.copy(kidx[64:128, 1, :], bank("kidx")[0:64, 0:S]).then_inc(*is_read("kidx"))
            act.wait_ge(*full("widx"))
            act.mul(widx[:, :, :], bank("widx")[:, 0:8].rearrange("p (a b) -> p a b", a=2),
                    1.0 / 16).then_inc(*is_read("widx"))
            beside(first["qidx"])
            beside(first["kv"])
            act.wait_ge(*full("kv"))
            link(act.copy(k1[:, :], bank("kv")[:, 0:S]))
            act.copy(v1[:, :, :].rearrange("p a b -> p (a b)"), bank("kv")[:, S:2 * S]).then_inc(*is_read("kv"))
            for j in range(4):
                beside(first["q"] + j)
                act.wait_ge(*full(("q", j)))
                act.mul(q1[:, 2 * j:2 * j + 2, :].rearrange("p a b -> p (a b)"), bank(("q", j)),
                        float(P) ** -0.5).then_inc(*is_read(("q", j)))
            def bias_out(key, dst):
                act.wait_ge(*full(key))
                act.copy(dst, bank(key).rearrange("p (a b) -> p a b", a=2)).then_inc(*is_read(key))

            for j in range(2):
                bias_out(("rev1", j), bias1[:, 2 * j:2 * j + 2, P:384])
            for j in range(2):
                beside(first["u"] + j)
                act.wait_ge(*full(("u", j)))
                act.copy(upad[:, 2 * j:2 * j + 2, 16:272],
                         bank(("u", j)).rearrange("p (a b) -> p a b", a=2)).then_inc(*is_read(("u", j)))
            for j in range(2, 4):
                bias_out(("rev1", j), bias1[:, 2 * j:2 * j + 2, P:384])
            for c in range(4):
                beside(first["gate"] + 2 * c)
                beside(first["gate"] + 2 * c + 1)
                for tb in range(2):
                    act.wait_ge(*full(("gate", c, tb)))
                    act.activation(gate[:, c // 2, tb, 512 * (c % 2):512 * (c % 2) + 512], bank(("gate", c, tb)),
                                   ACT.Sigmoid).then_inc(*is_read(("gate", c, tb)))
            for j in range(2):
                st_out(("pool", j), st_hi[:, 8 + 2 * j:10 + 2 * j, :], vec[:, V_PSCALE + 2 * j:V_PSCALE + 2 * j + 2])
            beside(first["pp"])
            beside(first["pp"] + 1)

            for t in range(HEADS1 + 3):
                if t < HEADS1:
                    b = t % 3
                    act.wait_ge(max_ready, ATT0["self"] + t + 1)
                    act.activation(prob1[:, b, 0:P], prob1[:, b, 0:P], ACT.Exp, bias=negmax[:, b, 0:1],
                                   accum_out=rowsum[:, b, 0:1])
                    act.activation(prob1[:, b, P:384], prob1[:, b, P:384], ACT.Exp, bias=negmax[:, b, 1:2],
                                   accum_out=rowsum[:, b, 1:2]).then_inc(exp_ready, 1)
                h = t - 2
                if 0 <= h < HEADS1:
                    act.wait_ge(*full(("T1", h)))
                    act.copy(probT1[:, h % 2, :], bank(("T1", h))[:, 0:384]).then_inc(*is_read(("T1", h)))
                h = t - 3
                if 0 <= h < HEADS1:
                    act.wait_ge(*full(("O1", h)))
                    act.copy(st_hi[:, h, :], bank(("O1", h))[:, 0:S]).then_inc(hi_rounded, 1)
            for k in range(4):
                beside(first["pa"] + k)
            st_all("merged")
            for k in range(4):
                beside(first["out"] + k)
            act.wait_ge(memx_loaded, 16)
            for tb in range(2):
                square("mem", memx[:, tb, :], tb, carve(11648, D) if tb == 0 else carve(12672, D))
            st_all("mem", k0=8, v=V_MEMKV)

            def square_y(n, name):
                for tb in range(2):
                    for h in range(2):
                        act.wait_ge(*full(("y", n, tb, h)))
                    square(name, ps[:, 2 * tb:2 * tb + 2, :], tb, tmp[:, tb, :].rearrange("p (a b) -> p a b", a=2))

            def square_res(n, name):
                for tb in range(2):
                    act.wait_ge(res_ready, RES[n] - 1 + tb)
                    square(name, res[:, tb, :], tb, tmp[:, tb, :])

            square_y("mix", "ymix")
            beside(first["km"])
            act.wait_ge(*full(("km", 0)))
            act.copy(km[:, 0:2, :].rearrange("p a b -> p (a b)"), bank(("km", 0))).then_inc(*is_read(("km", 0)))
            square_res("mix", "memq")
            beside(first["km"] + 1)
            act.wait_ge(*full(("km", 1)))
            act.copy(km[:, 2:4, :].rearrange("p a b -> p (a b)"), bank(("km", 1))).then_inc(*is_read(("km", 1)))
            beside(first["vm"])
            beside(first["vm"] + 1)
            for tb in range(2):
                act.wait_ge(*full(("vm", tb)))
                act.copy(vm[:, tb, :], bank(("vm", tb))).then_inc(*is_read(("vm", tb)))
            st_all("memq", v=V_MEM)
            for j in range(2):
                beside(first["qm"] + j)
                act.wait_ge(*full(("qm", j)))
                act.mul(qm[:, 2 * j:2 * j + 2, :].rearrange("p a b -> p (a b)"), bank(("qm", j)),
                        float(P) ** -0.5).then_inc(*is_read(("qm", j)))
            for t in range(4 + 3):
                if t < 4:
                    b = t % 3
                    act.wait_ge(max_ready, ATT0["mem"] + t + 1)
                    for tb in range(2):
                        mm = act.activation(probm[:, b, tb * S:tb * S + S], bank(("Lm", t))[:, tb * S:tb * S + S],
                                            ACT.Exp, bias=negmax[:, b, tb:tb + 1], accum_out=rowsum[:, b, tb:tb + 1])
                    mm.then_inc(*is_read(("Lm", t)))
                h = t - 2
                if 0 <= h < 4:
                    act.wait_ge(*full(("Tm", h)))
                    act.copy(probTm[:, h % 2, :], bank(("Tm", h))).then_inc(*is_read(("Tm", h)))
                h = t - 3
                if 0 <= h < 4:
                    act.wait_ge(*full(("Om", h)))
                    act.copy(st_hi[:, 8 + h, :], bank(("Om", h))[:, 0:S]).then_inc(hi_rounded, 1)
            beside(first["om"])
            beside(first["om"] + 1)
            square_y("mem", "ymem")
            square_res("mem", "ffn0")
            st_all("ffn0", v=V_FFN)

            def swiglu(n):
                u0 = first["ffn", n]

                def gate_out(i):
                    for tb in range(2):
                        if tb == 0:
                            act.wait_ge(*full(("up", n, 0), i))
                        elif isinstance(i, int) and i == 0:
                            act.wait_ge(*full(("up", n, 1)))
                        else:
                            act.wait_ge(w_used, u0 + 1 + 3 * i)
                        act.activation(silu[:, tb, :], bank(("up", n, tb))[:, 0:FC], ACT.Silu).then_inc(silu_ready, 1)

                def hidden_out(i):
                    act.wait_ge(*full(("hid", n), i))
                    act.copy(hid_hi[:, :, :].rearrange("p a b -> p (a b)"), bank(("hid", n))).then_inc(hi_rounded, 1)

                beside(u0)
                beside(u0 + 1)
                gate_out(0)
                hidden_out(0)
                with act.Fori(1, FSTEPS - 1) as i:
                    split(*at(u0 + 4, i - 1))
                    split(*at(u0 + 5, i - 1))
                    gate_out(i)
                    split(*at(u0 + 6, i - 1))
                    hidden_out(i)
                nxt[0] = u0 + 3 * FSTEPS - 2
                i = FSTEPS - 1
                beside(u0 + 3 * i - 1)
                beside(u0 + 3 * i)
                gate_out(i)
                beside(u0 + 3 * i + 1)
                hidden_out(i)
                beside(u0 + 3 * i + 2)

            swiglu(0)
            square_y(("ffn", 0), "yffn0")
            st_all("b2")
            swiglu(1)
            st_all("ln0", v=V_LNG, vb=V_LNB)
            for j in range(2):
                act.wait_ge(*full(("wsT", j)))
                act.copy(wsT[:, 4 * j:4 * j + 4, :].rearrange("p a b -> p (a b)"),
                         bank(("wsT", j))).then_inc(*is_read(("wsT", j)))
            for part, z in (("sgv", zv), ("sgu", zu)):
                for c in range(4):
                    beside(first[part] + 2 * c)
                    beside(first[part] + 2 * c + 1)
                    for tb in range(2):
                        act.wait_ge(*full((part, c, tb)))
                        act.activation(z[:, tb, 512 * c:512 * c + 512], bank((part, c, tb)),
                                       ACT.Gelu).then_inc(*is_read((part, c, tb)))
            st_all("um", 16)
            for k in range(8):
                beside(first["sgo"] + k)
            for j in range(8):
                bias_out(("rev2", j), bias2[:, 2 * j:2 * j + 2, :])
            st_all("ln1", v=V_LNG + 8, vb=V_LNB + 8)
            swiglu(2)
            st_all("ln2", v=V_LNG + 16, vb=V_LNB + 16)

            act.wait_ge(zeros_ready, 2)
            for slot in range(2):
                u = first["cin", slot]
                beside(u)
                key = ("cin", slot)
                act.wait_ge(*full(key))
                src = bank(key).rearrange("p (a m r) -> p a m r", a=2, r=2)
                for half in range(2):
                    for par in range(2):
                        mm = act.copy(cmp_e[64 * par:64 * par + 64, half::2, :], src[64 * half:64 * half + 64, :, :, par])
                        if (half, par) != (1, 1):
                            link(mm)
                mm.then_inc(*is_read(key))
                act.wait_ge(cmp_f_ready, 2 * slot + 1)
                fh = st_hi[:, 8:12, :].rearrange("p a b -> p (a b)")[:, 0:960]
                act.copy(fh, cmp_f[:, :, :].rearrange("p a b -> p (a b)")).then_inc(hi_rounded, 1)
                beside(u + 1)
                beside(u + 2)
                for f in range(2):
                    act.wait_ge(*full(("cg", slot, f)))
                    act.activation(cmp_g[:, f, :, 0:NCMP], bank(("cg", slot, f))[:, 0:60].rearrange("p (g n) -> p g n", g=4),
                                   ACT.Gelu, bias=vec[:, V_B1 + 2 * slot + f:V_B1 + 2 * slot + f + 1])\
                       .then_inc(*is_read(("cg", slot, f)))
                if slot == 0:
                    act.wait_ge(*full("kc"))
                    act.copy(kc[:, :, :].rearrange("p a b -> p (a b)"), bank("kc")[:, 0:P]).then_inc(*is_read("kc"))
            for name in ("k2", "v2", "k2w", "v2w"):
                beside(first[name])
                br = int(name[-1] == "w")
                act.wait_ge(*full(name))
                dst = (k2 if name[0] == "k" else v2)[:, :, br, :]
                act.copy(dst, bank(name).rearrange("p (a b) -> p a b", a=2)).then_inc(*is_read(name))
            swiglu(3)
            st_all("ln3", v=V_LNG + 24, vb=V_LNB + 24)

            act.wait_ge(zeros_ready, 3)
            for j in range(4):
                beside(first["q2"] + j)
                act.wait_ge(*full(("q2", j)))
                src = bank(("q2", j))
                r = 64 * (j % 2)
                for k in range(4):
                    mm = act.mul(q2[r:r + 64, 4 * j + k, :],
                                 src[64 * (k % 2):64 * (k % 2) + 64, (k // 2) * S:(k // 2 + 1) * S], 0.125)
                    if k < 3:
                        link(mm)
                mm.then_inc(*is_read(("q2", j)))
            beside(first["g2"])
            act.wait_ge(*full("g2"))
            act.activation(gate2[:, :, :].rearrange("p a b -> p (a b)"), bank("g2")[:, 0:96],
                           ACT.Sigmoid).then_inc(*is_read("g2"))
            act.wait_ge(cmp_exp_in, 1)
            act.activation(cmp_p[:, :, 0:16], cmp_p[:, :, 0:16], ACT.Exp).then_inc(cmp_exp_out, 1)

            def exp2(h):
                b = h % 3
                act.wait_ge(max_ready, ATT0["nsa"] + h + 1)
                for x in range(4):
                    lo = (0, P, S, 2 * S)[x]
                    n = (P, P, S, S)[x]
                    mm = act.activation(prob2[:, b, lo:lo + n], prob2[:, b, lo:lo + n], ACT.Exp,
                                        bias=negmax[:, b, x:x + 1], accum_out=rowsum[:, b, x:x + 1])
                mm.then_inc(exp_ready, 1)

            exp2(0)
            exp2(1)
            for q in range(2):
                act.wait_ge(*full(("Tc", q)))
                act.copy(cmp_pT[:, 2 * q:2 * q + 2, :].rearrange("p a b -> p (a b)"),
                         bank(("Tc", q))).then_inc(*is_read(("Tc", q)))
            for t in range(2, HEADS2 + 4):
                if t < HEADS2:
                    exp2(t)
                h = t - 2
                if h < HEADS2:
                    act.wait_ge(*full(("T2", h, 0)))
                    act.copy(probT2[:, h % 2, 0:512], bank(("T2", h, 0))).then_inc(*is_read(("T2", h, 0)))
                h = t - 4
                if h >= 0 and h % 2:
                    act.wait_ge(*full(("O2", h // 2)))
                    act.copy(st_hi[:, h // 2, :], bank(("O2", h // 2))[:, 0:S]).then_inc(hi_rounded, 1)
            for k in range(4):
                beside(first["o2"] + k)
            st_all("ln4", v=V_LNG + 32, vb=V_LNB + 32)
            swiglu(4)

        @block.vector
        def _(dve):
            nxt = [0]
            chain = [0]

            def link(ins):
                chain[0] += 1
                ins.then_inc(dve_step, 1)
                dve.wait_ge(dve_step, chain[0])

            def split(u, s, q, n=UNIT):
                dve.wait_ge(whi_ready, u + 1)
                dve.tensor_tensor(wlo[:, s, 0:n], raw[:, s, 0:n], whi[:, s, 0:n].bitcast(F32),
                                  ALU.subtract).then_inc(wlo_ready, 1)

            def beside(u):
                while nxt[0] <= min(u + 2, UNITS - 1):
                    n = nxt[0]
                    split(*at(n), unit_len[n])
                    nxt[0] += 1

            def st_out(key, hi, lo, scale=None, bias=None):
                dve.wait_ge(hi_rounded, split_no[key] + 1)
                src = bank(key)
                if scale is None:
                    mm = dve.tensor_tensor(lo.rearrange("p a b -> p (a b)"), src,
                                           hi.rearrange("p a b -> p (a b)").bitcast(F32), ALU.subtract)
                elif bias is None:
                    for kk in range(2):
                        mm = dve.scalar_tensor_tensor(lo[:, kk, :], src[:, kk * S:kk * S + S], scale[:, kk:kk + 1],
                                                      hi[:, kk, :].bitcast(F32), ALU.mult, ALU.subtract)
                else:
                    for kk in range(2):
                        link(dve.tensor_scalar(full_st[:, kk, :], src[:, kk * S:kk * S + S], scale[:, kk:kk + 1],
                                               bias[:, kk:kk + 1], ALU.mult, ALU.add))
                        mm = dve.tensor_tensor(lo[:, kk, :], full_st[:, kk, :], hi[:, kk, :].bitcast(F32), ALU.subtract)
                mm.then_inc(*is_read(key))

            full_st = hidden

            def st_all(name, tiles=KD, k0=0, v=None, vb=None):
                for j in range(tiles // 2):
                    k = 2 * j
                    st_out(("st", name, j), st_hi[:, k0 + k:k0 + k + 2, :], st_lo[:, k0 + k:k0 + k + 2, :],
                           None if v is None else vec[:, v + k:v + k + 2],
                           None if vb is None else vec[:, vb + k:vb + k + 2])

            def rsqrt(tb):
                v, y, a, b = (nrm[:, tb, i:i + 1] for i in range(4))
                link(dve.tensor_scalar(b.bitcast(I32), v.bitcast(I32), 1, None, ALU.logical_shift_right))
                link(dve.tensor_scalar(y.bitcast(I32), b.bitcast(I32), -1.0, float(0x5F3759DF), ALU.mult, ALU.add))
                for _ in range(3):
                    link(dve.scalar_tensor_tensor(a, y, y, v, ALU.mult, ALU.mult))
                    link(dve.tensor_scalar(b, a, -0.5, 1.5, ALU.mult, ALU.add))
                    link(dve.tensor_tensor(y, y, b, ALU.mult))
                return y

            def rms(name, tb):
                dve.wait_ge(sumsq_ready, SQ[name] + tb + 1)
                link(dve.tensor_scalar(nrm[:, tb, 0:1], sumsq[:, SQ[name] + tb:SQ[name] + tb + 1], 1.0 / D, EPS1, ALU.mult, ALU.add))
                return rsqrt(tb)

            def pre_norm(name, src, dst):
                for tb in range(2):
                    y = rms(name, tb)
                    dve.tensor_scalar(dst[:, tb, :], src[:, tb, :], y, None, ALU.mult).then_inc(xn_ready, 1)

            def post_norm_rms(n, name):
                dve.wait_ge(gb_loaded, GBL[n])
                for tb in range(2):
                    y = rms(name, tb)
                    for h in range(2):
                        key = ("y", n, tb, h)
                        dve.scalar_tensor_tensor(tmp[:, tb, 512 * h:512 * h + 512], bank(key), y,
                                                 gb[:, 0, 512 * h:512 * h + 512], ALU.mult,
                                                 ALU.mult).then_inc(*is_read(key))
                    for h in range(2):
                        dve.wait_ge(*read(("y", n, tb, h)))
                    dve.tensor_tensor(res[:, tb, :], res[:, tb, :], tmp[:, tb, :], ALU.add).then_inc(res_ready, 1)

            def layer_norm_stats(tb, parts, eps):
                link(dve.bn_aggr(mv[:, tb, :], stats[:, tb, 0:6 * parts]))
                link(dve.tensor_scalar(nrm[:, tb, 0:1], mv[:, tb, 1:2], eps, None, ALU.add))
                return rsqrt(tb)

            def post_norm_ln(n, halved, last=False):
                f = 2.0 if halved else 1.0
                if n != ("ffn", 1):
                    dve.wait_ge(res_ready, RES[n] - 2)
                for tb in range(2):
                    for h in range(2):
                        key = ("y", n, tb, h)
                        dve.wait_ge(*full(key))
                        part = tmp[:, tb, 512 * h:512 * h + 512]
                        dve.scalar_tensor_tensor(part, res[:, tb, 512 * h:512 * h + 512], f * ALPHA, bank(key),
                                                 ALU.mult, ALU.add).then_inc(*is_read(key))
                        dve.wait_ge(*read(key))
                        link(dve.bn_stats(stats[:, tb, 6 * h:6 * h + 6], part))
                    y = layer_norm_stats(tb, 2, EPS2 * f * f)
                    dve.tensor_scalar(tmp[:, tb, :], tmp[:, tb, :], mv[:, tb, 0:1], y, ALU.subtract,
                                      ALU.mult).then_inc(xn_ready, 1)

            dve.wait_ge(x_loaded, 16)
            pre_norm("mix", res, tmp)
            beside(0)
            dve.wait_ge(const_loaded, 32)
            st_all("mix", v=V_MIX)
            dve.wait_ge(zeros_ready, 1)
            beside(first["kidx"])
            beside(first["qidx"])
            dve.wait_ge(*full("qidx"))
            dve.tensor_copy(qidx[:, :, :].rearrange("p a b -> p (a b)"), bank("qidx")).then_inc(*is_read("qidx"))
            beside(first["kv"])
            dve.wait_ge(*read("widx"))
            for tb in range(2):
                n = P * (tb + 1)
                acc = score[:, 0:P] if tb == 0 else score[:, P:384]
                for h in range(4):
                    key = ("dots", 0 if tb == 0 else 1 + h // 2)
                    c = S * (h // 2) + P * (h % 2) if tb == 0 else S * (h % 2)
                    if h == 0 or (tb and h == 2):
                        dve.wait_ge(*full(key))
                    mm = dve.tensor_scalar(relu_w[:, 0:n], bank(key)[:, c:c + n], 0.0, widx[:, tb, h:h + 1],
                                           ALU.max, ALU.mult)
                    if h == 3 or (tb and h == 1):
                        mm.then_inc(*is_read(key))
                        dve.wait_ge(*read(key))
                    else:
                        link(mm)
                    other = con[:, K_TRI + P:K_TRI + 2 * P] if tb == 0 else con[:, K_TRI:K_TRI + 2 * P]
                    link(dve.tensor_tensor(acc, relu_w[:, 0:n], other if h == 0 else acc, ALU.add))

            def top_round(r):
                if r < TOPK // 4:
                    acc = score[:, 0:P] if r < TOPK // 8 else score[:, P:384]
                    link(dve.max(top8[:, :], acc))
                    link(dve.match_replace(acc, top8[:, :], acc, TAKEN))
                if r == TOPK // 4:
                    dve.tensor_scalar(selmask[:, :], score[:, :], TAKEN / 1.5, BIG_NEG, ALU.is_gt,
                                      ALU.mult).then_inc(selected, 1)

            r = 0
            for name, n in (("q", 4), ("u", 2), ("gate", 8)):
                for j in range(n):
                    beside(first[name] + j)
                    for _ in range(2):
                        top_round(r)
                        r += 1
            for j in range(2):
                k = 8 + 2 * j
                st_out(("pool", j), st_hi[:, k:k + 2, :], st_lo[:, k:k + 2, :],
                       vec[:, V_PSCALE + 2 * j:V_PSCALE + 2 * j + 2])
            for c in range(2):
                beside(first["pp"] + c)
                for tb in range(2):
                    dve.wait_ge(*full(("pp", c, tb)))
                    g = gate[:, 0, tb, 512 * c:512 * c + 512]
                    dve.wait_ge(*read(("gate", c, tb)))
                    dve.tensor_tensor(g, bank(("pp", c, tb)), g, ALU.mult).then_inc(*is_read(("pp", c, tb)))

            def normalize(b, segments):
                link(dve.reciprocal(factor[:, b, 0:len(segments)], rowsum[:, b, 0:len(segments)]))
                for x, seg in enumerate(segments):
                    mm = dve.tensor_scalar(seg, seg, factor[:, b, x:x + 1], None, ALU.mult)
                    if x < len(segments) - 1:
                        link(mm)
                mm.then_inc(prob_ready, 1)

            dve.wait_ge(bias_masked, 1)
            for t in range(HEADS1 + 3):
                if t < HEADS1:
                    b = t % 3
                    dve.wait_ge(*full(("L1", t)))
                    L = bank(("L1", t))
                    if t >= 3:
                        dve.wait_ge(*full(("T1", t - 3)))
                    link(dve.tensor_tensor_reduce(prob1[:, b, 0:P], L[:, 0:P], bias1[:, t, 0:P], 1.0, -3e38,
                                                  ALU.add, ALU.max, rowmax[:, b, 0:1]))
                    dve.tensor_tensor_reduce(prob1[:, b, P:384], L[:, P:384], bias1[:, t, P:384], 1.0, -3e38,
                                             ALU.add, ALU.max, rowmax[:, b, 1:2]).then_inc(*is_read(("L1", t)))
                    dve.wait_ge(*read(("L1", t)))
                    dve.tensor_scalar(negmax[:, b, 0:2], rowmax[:, b, 0:2], -1.0, None,
                                      ALU.mult).then_inc(max_ready, 1)
                h = t - 1
                if 0 <= h < HEADS1:
                    b = h % 3
                    dve.wait_ge(exp_ready, h + 1)
                    normalize(b, [prob1[:, b, 0:P], prob1[:, b, P:384]])
                h = t - 3
                if 0 <= h < HEADS1:
                    dve.wait_ge(hi_rounded, split_no["O1", h] + 1)
                    dve.tensor_tensor(st_lo[:, h, :], bank(("O1", h))[:, 0:S], st_hi[:, h, :].bitcast(F32),
                                      ALU.subtract).then_inc(*is_read(("O1", h)))
            for c in range(2):
                beside(first["pa"] + 2 * c)
                beside(first["pa"] + 2 * c + 1)
                for tb in range(2):
                    dve.wait_ge(*full(("pa", c, tb)))
                    dve.wait_ge(*read(("gate", 2 + c, tb)))
                    g = gate[:, 1, tb, 512 * c:512 * c + 512]
                    dve.tensor_tensor(g, bank(("pa", c, tb)), g, ALU.mult).then_inc(*is_read(("pa", c, tb)))
                    dve.wait_ge(*read(("pa", c, tb)))
                    dve.wait_ge(*read(("pp", c, tb)))
                    mm = dve.tensor_tensor(tmp[:, tb, 512 * c:512 * c + 512], gate[:, 0, tb, 512 * c:512 * c + 512],
                                           g, ALU.add)
                    if c:
                        mm.then_inc(xn_ready, 1)
                    else:
                        link(mm)
            st_all("merged")
            for k in range(4):
                beside(first["out"] + k)
            dve.wait_ge(memx_loaded, 16)
            pre_norm("mem", memx, memx)
            st_all("mem", k0=8, v=V_MEMKV)
            post_norm_rms("mix", "ymix")
            beside(first["km"])
            pre_norm("memq", res, tmp)
            beside(first["km"] + 1)
            beside(first["vm"])
            beside(first["vm"] + 1)
            st_all("memq", v=V_MEM)
            beside(first["qm"])
            beside(first["qm"] + 1)
            for t in range(4 + 3):
                if t < 4:
                    b = t % 3
                    dve.wait_ge(*full(("Lm", t)))
                    link(dve.tensor_reduce(rowmax[:, b, 0:2], bank(("Lm", t)).rearrange("p (a b) -> p a b", a=2),
                                           AX_X, ALU.max))
                    dve.tensor_scalar(negmax[:, b, 0:2], rowmax[:, b, 0:2], -1.0, None,
                                      ALU.mult).then_inc(max_ready, 1)
                h = t - 1
                if 0 <= h < 4:
                    b = h % 3
                    dve.wait_ge(*read(("Lm", h)))
                    link(dve.reciprocal(factor[:, b, 0:2], rowsum[:, b, 0:2]))
                    link(dve.tensor_scalar(probm[:, b, 0:S], probm[:, b, 0:S], factor[:, b, 0:1], None, ALU.mult))
                    dve.tensor_scalar(probm[:, b, S:512], probm[:, b, S:512], factor[:, b, 1:2], None,
                                      ALU.mult).then_inc(prob_ready, 1)
                h = t - 3
                if 0 <= h < 4:
                    dve.wait_ge(hi_rounded, split_no["Om", h] + 1)
                    dve.tensor_tensor(st_lo[:, 8 + h, :], bank(("Om", h))[:, 0:S], st_hi[:, 8 + h, :].bitcast(F32),
                                      ALU.subtract).then_inc(*is_read(("Om", h)))
            beside(first["om"])
            beside(first["om"] + 1)
            post_norm_rms("mem", "ymem")
            pre_norm("ffn0", res, tmp)
            st_all("ffn0", v=V_FFN)

            def swiglu(n):
                u0 = first["ffn", n]

                def hidden_in(i):
                    for tb in range(2):
                        dve.wait_ge(silu_ready, 2 * FSTEPS * n + tb + 1 + 2 * i)
                        dve.tensor_tensor(hidden[:, tb, :], bank(("up", n, tb))[:, FC:2 * FC], silu[:, tb, :],
                                          ALU.mult).then_inc(*is_read(("up", n, tb)))

                def hidden_out(i):
                    dve.wait_ge(hi_rounded, split_no["hid", n] + 1 + i)
                    dve.tensor_tensor(hid_lo[:, :, :].rearrange("p a b -> p (a b)"), bank(("hid", n)),
                                      hid_hi[:, :, :].rearrange("p a b -> p (a b)").bitcast(F32),
                                      ALU.subtract).then_inc(*is_read(("hid", n)))

                beside(u0)
                beside(u0 + 1)
                hidden_in(0)
                hidden_out(0)
                with dve.Fori(1, FSTEPS - 1) as i:
                    split(*at(u0 + 4, i - 1))
                    split(*at(u0 + 5, i - 1))
                    hidden_in(i)
                    split(*at(u0 + 6, i - 1))
                    hidden_out(i)
                nxt[0] = u0 + 3 * FSTEPS - 2
                i = FSTEPS - 1
                beside(u0 + 3 * i - 1)
                beside(u0 + 3 * i)
                hidden_in(i)
                beside(u0 + 3 * i + 1)
                hidden_out(i)
                beside(u0 + 3 * i + 2)

            swiglu(0)
            post_norm_rms(("ffn", 0), "yffn0")
            st_all("b2")
            swiglu(1)
            post_norm_ln(("ffn", 1), True)
            st_all("ln0", v=V_LNG, vb=V_LNB)
            for c in range(4):
                beside(first["sgv"] + 2 * c)
                beside(first["sgv"] + 2 * c + 1)
                for tb in range(2):
                    dve.wait_ge(*read(("sgv", c, tb)))
                    link(dve.bn_stats(stats[:, tb, 6 * c:6 * c + 6], zv[:, tb, 512 * c:512 * c + 512]))
            for tb in range(2):
                y = layer_norm_stats(tb, 4, EPS2)
                dve.tensor_scalar(zv[:, tb, :], zv[:, tb, :], mv[:, tb, 0:1], y, ALU.subtract,
                                  ALU.mult).then_inc(zv_normed, 1)
            for k in range(8):
                beside(first["sgu"] + k)
            for tb in range(2):
                for gp in range(4):
                    key = ("mixed", tb, gp)
                    dve.wait_ge(*full(key))
                    if gp == 0:
                        dve.wait_ge(*read(("sgu", 3, tb)))
                    for g in (2 * gp, 2 * gp + 1):
                        z = zu[:, tb, g * S:g * S + S]
                        mm = dve.scalar_tensor_tensor(z, bank(key)[:, (g % 2) * S:(g % 2 + 1) * S],
                                                      vec[:, V_BS + g:V_BS + g + 1], z, ALU.add, ALU.mult)
                        if g % 2 == 0:
                            link(mm)
                    mm.then_inc(*is_read(key))
            st_all("um", 16)
            for k in range(8):
                beside(first["sgo"] + k)
            post_norm_ln("sgu", False)
            st_all("ln1", v=V_LNG + 8, vb=V_LNB + 8)
            swiglu(2)
            post_norm_ln(("ffn", 2), True)
            st_all("ln2", v=V_LNG + 16, vb=V_LNB + 16)

            for slot in range(2):
                u = first["cin", slot]
                beside(u)
                dve.wait_ge(*read(("cin", slot)))
                e = cmp_e[:, :, :]
                pe_vec = vec[:, V_PE + 16 * slot:V_PE + 16 * slot + 16]
                dve.tensor_tensor(view(cmp_f[:, 0, 0:1], (60, 16), (15, 4), (1, 15)),
                                  view(e[:, 0, 0:1], (1, 16), (P, 4), (8, 15)),
                                  view(pe_vec, (1, 16), (0, 4), (0, 15)), ALU.add).then_inc(cmp_f_ready, 1)
                fh, fl = (x[:, 8:12, :].rearrange("p a b -> p (a b)")[:, 0:960] for x in (st_hi, st_lo))
                dve.wait_ge(hi_rounded, split_no["cf", slot] + 1)
                dve.tensor_tensor(fl, cmp_f[:, :, :].rearrange("p a b -> p (a b)"), fh.bitcast(F32),
                                  ALU.subtract).then_inc(cmp_f_ready, 1)
                beside(u + 1)
                beside(u + 2)
            for f in range(2):
                dve.wait_ge(*read(("cg", 1, f)))
                mm = dve.tensor_copy(cmp_gr[:, f, :, :].rearrange("p g (j n) -> p g j n", j=4),
                                     view(cmp_g[:, f, 0, 0:1], (32, 4), (0, 4), (1, 32)))
            mm.then_inc(cmp_gr_ready, 1)
            dve.wait_ge(*full("vc"))
            for j in range(4):
                mm = dve.tensor_scalar(vc[:, :, j, :], bank("vc")[:, 0:256].rearrange("p (g d) -> p g d", g=4),
                                       con[:, K_BLK + j:K_BLK + j + 1], None, ALU.mult)
            mm.then_inc(*is_read("vc"))
            for name in ("k2", "v2", "k2w", "v2w"):
                beside(first[name])
            swiglu(3)
            post_norm_ln(("ffn", 3), True)
            st_all("ln3", v=V_LNG + 24, vb=V_LNB + 24)

            for j in range(4):
                beside(first["q2"] + j)
            beside(first["g2"])
            dve.wait_ge(res_ready, RES["ffn", 3])
            for j in range(4, 8):
                dve.wait_ge(*read(("rev2", j)))
            flat = cmp_p[:, :, :]
            link(dve.memset(flat[:, :, 0:16], BIG_NEG))
            link(dve.memset(flat[:, :, 16:32], 0.0))
            dve.wait_ge(*full("Lc"))
            for tb in range(2):
                n, c0 = ((7, P + 31), (NCMP, 31))[tb]
                mm = dve.tensor_tensor(view(flat[:, 4 * tb, 0:1], (256, 4), (32, 4), (1, n)),
                                       view(bank("Lc")[:, 64 * tb:64 * tb + 1], (128, 4), (16, 4), (1, n)),
                                       view(bias2[:, 0, c0:c0 + 1], (4 * S, 4), (S, 4), (16, n)), ALU.add)
                if tb == 0:
                    link(mm)
            mm.then_inc(*is_read("Lc"))
            dve.wait_ge(*read("Lc"))
            link(dve.tensor_reduce(cmp_stat[:, 0, :], flat[:, :, 0:16], AX_X, ALU.max))
            dve.tensor_tensor(flat[:, :, 0:16], flat[:, :, 0:16], view(cmp_stat[:, 0, 0:1], (1, 32), (0, 16)),
                              ALU.subtract).then_inc(cmp_exp_in, 1)

            def max2(h):
                b = h % 3
                if h >= 3:
                    dve.wait_ge(*full(("T2", h - 3, 1)))
                for tb in range(2):
                    dve.wait_ge(*full(("L2", h, tb)))
                    L = bank(("L2", h, tb))
                    n = P * (tb + 1)
                    for br in range(2):
                        lo = S * tb + n * br
                        mm = dve.tensor_tensor_reduce(prob2[:, b, lo:lo + n], L[:, n * br:n * br + n],
                                                      bias2[:, h, S - n:S], 1.0, -3e38, ALU.add, ALU.max,
                                                      rowmax[:, b, 2 * tb + br:2 * tb + br + 1])
                    mm.then_inc(*is_read(("L2", h, tb)))
                dve.wait_ge(*read(("L2", h, 1)))
                dve.tensor_scalar(negmax[:, b, :], rowmax[:, b, :], -1.0, None, ALU.mult).then_inc(max_ready, 1)

            def normalize2(h):
                b = h % 3
                dve.wait_ge(exp_ready, HEADS1 + h + 1)
                link(dve.reciprocal(factor[:, b, :], rowsum[:, b, :]))
                link(dve.tensor_tensor(factor[:, b, :].rearrange("p (a c) -> p a c", a=2),
                                       factor[:, b, :].rearrange("p (a c) -> p a c", a=2),
                                       gate2[:, :, 3 * h + 1:3 * h + 3], ALU.mult))
                for x in range(4):
                    seg = prob2[:, b, (0, P, S, 2 * S)[x]:(P, S, 2 * S, 3 * S)[x]]
                    mm = dve.tensor_scalar(seg, seg, factor[:, b, x:x + 1], None, ALU.mult)
                mm.then_inc(prob_ready, 1)

            dve.wait_ge(*read("g2"))
            max2(0)
            max2(1)
            dve.wait_ge(cmp_exp_out, 1)
            link(dve.tensor_reduce(cmp_stat[:, 1, :], flat[:, :, 0:16], AX_X, ALU.add))
            link(dve.reciprocal(cmp_stat[:, 2, :], cmp_stat[:, 1, :]))
            fac = view(cmp_stat[:, 2, 0:1], (8, 4), (4, 2), (1, 4))
            link(dve.tensor_tensor(fac, fac, view(gate2[:, 0, 0:1], (12, 4), (48, 2), (3, 4)), ALU.mult))
            link(dve.tensor_tensor(flat[:, :, 0:16], flat[:, :, 0:16], view(cmp_stat[:, 2, 0:1], (1, 32), (0, 16)),
                                   ALU.mult))
            for tb in range(2):
                part = view(flat[:, 4 * tb, 0:1], (256, 4), (32, 4), (1, 16))
                mm = dve.tensor_tensor(part, part, view(con[:, K_CMASK + 16 * tb:K_CMASK + 16 * tb + 1], (0, 4), (0, 4),
                                                        (1, 16)), ALU.mult)
            mm.then_inc(cmp_p_ready, 1)
            normalize2(0)
            for t in range(2, HEADS2 + 4):
                if t < HEADS2:
                    max2(t)
                if t - 1 < HEADS2:
                    normalize2(t - 1)
                h = t - 2
                if h < HEADS2:
                    dve.wait_ge(*full(("T2", h, 1)))
                    dve.tensor_copy(probT2[:, h % 2, 512:768],
                                    bank(("T2", h, 1))[:, 0:S]).then_inc(*is_read(("T2", h, 1)))
                h = t - 4
                if h >= 0 and h % 2:
                    key = ("O2", h // 2)
                    dve.wait_ge(hi_rounded, split_no[key] + 1)
                    dve.tensor_tensor(st_lo[:, h // 2, :], bank(key)[:, 0:S], st_hi[:, h // 2, :].bitcast(F32),
                                      ALU.subtract).then_inc(*is_read(key))
            for k in range(4):
                beside(first["o2"] + k)
            post_norm_ln("nsa", False)
            st_all("ln4", v=V_LNG + 32, vb=V_LNB + 32)
            swiglu(4)
            post_norm_ln(("ffn", 4), True)

        @block.gpsimd
        def _(pool):
            chain = [0]

            def link(ins):
                chain[0] += 1
                ins.then_inc(pool_step, 1)
                pool.wait_ge(pool_step, chain[0])

            def load_row(dst, row, signal):
                pool.dma_start(dst, bass.AP(row.tensor, row.offset, [[0, P], [1, row.shape[-1]]])).then_inc(signal, 16)

            link(pool.memset(table[:, :], 0.0))
            link(pool.memset(table[32:33, :], BIG_NEG))
            pool.dma_start(table[0:32, 0:HEADS1], A["rel_bias_table"]).then_inc(table_loaded, 16)
            pool.dma_start(table[0:32, HEADS1:HEADS1 + HEADS2], A["rel_table_2"]).then_inc(table_loaded, 16)
            pool.dma_start(poolw[:, :, :], A["pool_w"].rearrange("g c d -> c g d")).then_inc(poolw_loaded, 16)
            pool.memset(zero_r[:, :].bitcast(F32), 0.0)
            pool.memset(kidx[:, :, :], 0.0)
            pool.memset(upad[:, :, 0:16], 0.0).then_inc(zeros_ready, 1)
            pool.wait_ge(rows_stored, 16)
            pool.dma_start(shifted1[:, :, :], bass.AP(bias_rows, 0, [[1, P], [512, HEADS1], [1, S]]))\
                .then_inc(bias1_loaded, 16)
            load_row(gb[:, 0, :], A["norm_mix_post"], gb_loaded)

            pool.wait_ge(const_loaded, 32)
            for j in range(2):
                pool.wait_ge(*read(("u", j)))
            link(pool.tensor_tensor(winA[:, :, 1:272], upad[:, :, 1:272], upad[:, :, 0:271], ALU.add))
            link(pool.tensor_tensor(winB[:, 1:4, 3:272], winA[:, 1:4, 3:272], winA[:, 1:4, 1:270], ALU.add))
            link(pool.tensor_tensor(winA[:, 2:4, 7:272], winB[:, 2:4, 7:272], winB[:, 2:4, 3:268], ALU.add))
            link(pool.tensor_tensor(winB[:, 3, 15:272], winA[:, 3, 15:272], winA[:, 3, 7:264], ALU.add))
            for g in range(4):
                win = (winA, winB)[g % 2]
                link(pool.tensor_tensor(win[:, g, 16:32], win[:, g, 16:32],
                                        con[:, K_ICNT + 16 * g:K_ICNT + 16 * g + 16], ALU.mult))
                link(pool.tensor_scalar(win[:, g, 32:272], win[:, g, 32:272], 1.0 / (2 << g), None, ALU.mult))
                mm = pool.tensor_tensor(win[:, g, 16:272], win[:, g, 16:272], upad[:, g, 16:272], ALU.subtract)
                if g < 3:
                    link(mm)
            mm.then_inc(pooled, 1)
            pool.wait_ge(selected, 1)
            for j in range(4):
                pool.wait_ge(*read(("rev1", j)))
            for lo, src, n in ((0, S, P), (P, P, S)):
                mm = pool.tensor_tensor(bias1[:, :, lo:lo + n], bias1[:, :, src:src + n],
                                        view(selmask[:, lo:lo + 1], (0, HEADS1), (1, n)), ALU.add)
                if lo == 0:
                    link(mm)
            mm.then_inc(bias_masked, 1)
            pool.wait_ge(*read(("O1", HEADS1 - 1)))
            pool.dma_start(memx[:, :, :], A["mem"][0].rearrange("(t p) d -> p t d", p=P)).then_inc(memx_loaded, 16)
            pool.wait_ge(res_ready, RES["mix"])
            load_row(gb[:, 0, :], A["norm_mem_post"], gb_loaded)
            pool.wait_ge(res_ready, RES["mem"])
            load_row(gb[:, 0, :], A["norm_ffn_post"], gb_loaded)
            load_row(sgu_gb[:, 0, :], A["sgu_ln_g_2"][0], sgu_gb_loaded)
            load_row(sgu_gb[:, 1, :], A["sgu_ln_b_2"][0], sgu_gb_loaded)
            pool.dma_start(ws[:, :, :], A["sgu_w_s_2"][0].rearrange("g t s -> t g s")).then_inc(ws_loaded, 16)
            pool.wait_ge(ws_loaded, 16)
            pool.affine_select(out=ws[:, :, :], in_=ws[:, :, :], compare_op=ALU.is_ge, fill=0.0, base=0,
                               pattern=[[0, 8], [-1, P]], channel_multiplier=1).then_inc(ws_masked, 1)

            def load_norm(i):
                load_row(gb[:, 0, :], A["ln_g_2"][i // 3, i % 3], gb_loaded)
                load_row(gb[:, 1, :], A["ln_b_2"][i // 3, i % 3], gb_loaded)

            def residual(n, name):
                pool.wait_ge(gb_loaded, GBL[n])
                for tb in range(2):
                    pool.wait_ge(xn_ready, XN[name] - 1 + tb)
                    link(pool.tensor_tensor(res[:, tb, :], tmp[:, tb, :], gb[:, 0, :], ALU.mult))
                    pool.tensor_tensor(res[:, tb, :], res[:, tb, :], gb[:, 1, :], ALU.add).then_inc(res_ready, 1)
                pool.wait_ge(res_ready, RES[n])

            pool.wait_ge(res_ready, RES["ffn", 0])
            load_norm(0)
            residual(("ffn", 1), "ln0")
            load_norm(1)
            pool.wait_ge(sgu_gb_loaded, 32)
            for tb in range(2):
                pool.wait_ge(zv_normed, tb + 1)
                link(pool.tensor_tensor(zv[:, tb, :], zv[:, tb, :], sgu_gb[:, 0, :], ALU.mult))
                pool.tensor_tensor(zv[:, tb, :], zv[:, tb, :], sgu_gb[:, 1, :], ALU.add).then_inc(zv_ready, 1)
            pool.wait_ge(zv_ready, 2)
            pool.dma_start(shifted2[:, :, :], bass.AP(bias_rows, HEADS1 * 512,
                                                      [[1, P], [512, HEADS2], [1, S]])).then_inc(bias2_loaded, 16)
            residual("sgu", "ln1")
            load_norm(2)
            for slot in range(2):
                for dup in range(2):
                    pool.dma_start(cmp_w2[:, slot, :, 64 * dup:64 * dup + 64],
                                   A["cmp_w2_2"][slot].rearrange("(f p) d -> p f d", p=P)).then_inc(cmp_w2_loaded, 16)
            pool.memset(cmp_g[:, :, :, :], 0.0).then_inc(zeros_ready, 1)
            pool.memset(q2[:, :, :], 0.0).then_inc(zeros_ready, 1)
            residual(("ffn", 2), "ln2")
            load_norm(3)
            residual(("ffn", 3), "ln3")
            load_norm(4)
            residual("nsa", "ln4")
            load_norm(5)
            residual(("ffn", 4), "end")


_MATRICES = ["x", "mem", "norm_mix_post", "w_in", "pool_w", "w_proj_pool", "w_proj_attn", "rel_bias_table",
             "w_out", "norm_mem_post", "w_q_mem", "w_kv_mem", "w_o_mem", "norm_ffn_post", "w_gate_up", "w_down",
             "rel_table_2", "ln_g_2", "ln_b_2", "ffn_w1_2", "ffn_w3_2", "ffn_w2_2", "sgu_w_in_2", "sgu_ln_g_2",
             "sgu_ln_b_2", "sgu_w_s_2", "sgu_w_out_2", "kv_w_2", "cmp_w1_2", "cmp_w2_2", "nsa_w_qg_2", "nsa_w_o_2"]


def _columns(v):
    return np.ascontiguousarray(np.asarray(v).reshape(-1, P).T)


def kernel(**inputs):
    import concourse.bacc as _bacc
    from concourse.bass_utils import run_bass_kernel_spmd as _run

    nc = _bacc.Bacc("TRN2", target_bir_lowering=False, num_devices=1)
    arrays = {name: np.ascontiguousarray(inputs[name]) for name in _MATRICES}
    parts = [_columns(inputs[n]) for n in ("norm_mix_pre", "norm_mem_kv", "norm_mem_pre", "norm_ffn_pre",
                                           "pool_scale")]
    for name in ("ln_g_2", "ln_b_2"):
        parts += [_columns(row) for row in np.asarray(inputs[name]).reshape(6, D)]
    parts += [_columns(row) for row in np.asarray(inputs["cmp_b1_2"])]
    parts += [_columns(row) for row in np.asarray(inputs["cmp_pe_2"]).reshape(2, 32 * 64)]
    parts += [np.asarray(inputs["sgu_b_s_2"])[0].T]
    arrays["vectors"] = np.ascontiguousarray(np.concatenate(parts, axis=1))
    arrays["shape_consts"] = shape_constants()
    A = {name: nc.dram_tensor(f"in_{name}", a.shape, mybir.dt.from_np(a.dtype), kind="ExternalInput").ap()
         for name, a in arrays.items()}
    out = nc.dram_tensor("out_0", (1, S, D), F32, kind="ExternalOutput").ap()
    build(nc, A, out)
    r = _run(nc, [{f"in_{name}": a for name, a in arrays.items()}], core_ids=[0])
    return r.results[0]["out_0"]
```

```python
from contextlib import ExitStack

import numpy as np

import concourse.bass as bass
from concourse import mybir

F32 = mybir.dt.float32
F32R = mybir.dt.float32r
I32 = mybir.dt.int32
ALU = mybir.AluOpType
ACT = mybir.ActivationFunctionType
AX_X = mybir.AxisListType.X

P = 128
D = 1024
S = 256
KD = D // P
DFF = 2816
FC = 256
FSTEPS = DFF // FC
HEADS1, HEADS2 = 8, 16
NCMP = 15
BIG_NEG = -1e30
TAKEN = -3e38
TOPK = S // 4
EPS1, EPS2 = 1e-6, 1e-5
ALPHA = 4.0 ** 0.25
UNIT = 2048
RING = 3

C_POOL, C_Q, C_K, C_QI, C_KI, C_GATE = 0, 512, 1536, 1792, 2048, 2116

V_PSCALE, V_B1, V_PE, V_BS, V_END = 0, 4, 8, 40, 48
K_ID, K_HOT, K_TRI, K_ICNT, K_BLK, K_CMASK, K_REV, K_END = 0, 128, 640, 896, 960, 964, 996, 1124


def shape_constants():
    c = np.zeros((P, K_END), np.float32)
    c[:, K_ID:K_ID + P] = np.eye(P)
    c[:, K_REV:K_REV + P] = np.eye(P)[::-1]
    dist = np.arange(S)
    nf = np.maximum(dist, 1).astype(np.float32)
    large = 16 + (np.log(nf / np.float32(16)) / np.float32(np.log(8.0)) * np.float32(16)).astype(np.int32)
    bucket = np.where(dist < 16, dist, np.minimum(large, 31))
    for j in range(2 * S):
        c[bucket[S - 1 - j] if j < S else 32, K_HOT + j] = 1.0
    t = np.arange(P)
    c[:, K_TRI + P:K_TRI + 2 * P] = np.where(t[None, :] <= t[:, None], 0.0, BIG_NEG)
    for g in range(4):
        c[:, K_ICNT + 16 * g:K_ICNT + 16 * g + 16] = 1.0 / np.minimum(np.arange(16) + 1, 2 << g)
    for j in range(4):
        c[32 * j:32 * j + 32, K_BLK + j] = 1.0
    for tb in range(2):
        for n in range(NCMP):
            c[:, K_CMASK + 16 * tb + n] = (16 * n + 31 <= t + P * tb)
    return c


def build(nc, A, out):
    ctx = ExitStack()
    with ctx:
        def sb(name, shape, dt=F32):
            return ctx.enter_context(nc.sbuf_tensor(name, shape, dt))

        def sem(name):
            return ctx.enter_context(nc.semaphore(name))

        raw = sb("raw", [P, RING, UNIT])
        minus_half = sb("minus_half", [P, 1])
        warm = sb("warm", [P, 16])
        whi = sb("whi", [P, RING, UNIT], F32R)
        wlo = sb("wlo", [P, RING, UNIT], F32R)
        st_hi = sb("st_hi", [P, 16, S], F32R)
        st_lo = sb("st_lo", [P, 16, S], F32R)
        hid_hi = sb("hid_hi", [P, 2, S], F32R)
        hid_lo = sb("hid_lo", [P, 2, S], F32R)
        silu = sb("silu", [P, 2, FC])
        hidden = sb("hidden", [P, 2, FC])
        res = sb("res", [P, 2, D])
        tmp = sb("tmp", [P, 2, D])
        gb = sb("gb", [P, 2, D])
        con = sb("con", [P, K_END])
        vec = sb("vec", [P, V_END])
        table = sb("table", [P, P])
        sumsq = sb("sumsq", [P, 14])
        stats = sb("stats", [P, 2, 24])
        mv = sb("mv", [P, 2, 2])
        meansq = sb("meansq", [P, 48])
        rstd = sb("rstd", [P, 48])
        top8 = sb("top8", [P, 8])
        rowmax = sb("rowmax", [P, 3, 4])
        negmax = sb("negmax", [P, 3, 4])
        rowsum = sb("rowsum", [P, 3, 4])
        factor = sb("factor", [P, 3, 4])
        cmp_stat = sb("cmp_stat", [P, 3, 32])
        big = sb("big", [P, 16000])
        ps = ctx.enter_context(nc.psum_tensor("ps", [P, 8, 512], F32))
        bias_rows = nc.dram_tensor("bias_rows", [P, 512], F32)

        ident = con[:, K_ID:K_ID + P]
        reverse = con[:, K_REV:K_REV + P]

        def carve(start, *dims):
            n = int(np.prod(dims))
            a = big[:, start:start + n]
            if len(dims) == 2:
                return a.rearrange("p (a b) -> p a b", b=dims[1])
            if len(dims) == 3:
                return a.rearrange("p (a b c) -> p a b c", b=dims[1], c=dims[2])
            if len(dims) == 4:
                return a.rearrange("p (a b c d) -> p a b c d", b=dims[1], c=dims[2], d=dims[3])
            return a

        def view(ap, *dims):
            return bass.AP(ap.tensor, ap.offset, [list(ap.ap[0])] + [list(d) for d in dims])

        bias1 = carve(0, HEADS1, 384)
        gate = carve(3072, 2, 2, D)
        shifted1 = carve(5120, HEADS1, S)
        q1 = carve(7168, HEADS1, S)
        k1 = carve(9216, S)
        v1 = carve(9472, 2, P)
        prob1 = carve(9728, 3, 384)
        probT1 = carve(10880, 2, 384)
        kidx = carve(9728, 2, S)
        qidx = carve(10240, 2, S)
        score = carve(10752, 384)
        relu_w = carve(11136, S)
        upad = carve(11648, 4, 272)
        winA = carve(12736, 4, 272)
        winB = carve(13824, 4, 272)
        widx = carve(14912, 2, 4)
        selmask = carve(14920, 384)
        poolw = carve(15304, 4, P)
        memx = carve(0, 2, D)
        km = carve(3072, 4, S)
        vm = carve(4096, 2, 512)
        qm = carve(5120, 4, S)
        probm = carve(6144, 3, 512)
        probTm = carve(7680, 2, 512)
        zv = carve(0, 2, 2048)
        zu = carve(4096, 2, 2048)
        sgu_gb = carve(8192, 2, 2048)
        ws = carve(12288, 8, P)
        wsT = carve(13312, 8, P)
        bias2 = carve(0, HEADS2, S)
        shifted2 = carve(4096, HEADS2, S)
        q2 = carve(4096, HEADS2, S)
        k2 = carve(8192, 2, 2, S)
        v2 = carve(9216, 2, 2, S)
        kc = carve(10240, 4, 32)
        vc = carve(10368, 4, 4, 64)
        gate2 = carve(11392, 2, 48)
        prob2 = carve(11488, 3, 768)
        probT2 = carve(13792, 2, 768)
        cmp_e = carve(11488, 4, P)
        cmp_f = carve(12000, 16, 60)
        cmp_g = carve(12960, 2, 4, 32)
        cmp_gr = carve(13216, 2, 4, P)
        cmp_w2 = carve(14240, 2, 2, P)
        cmp_x = carve(14752, 2, 256)
        tmpf = tmp[:, :, :].rearrange("p a b -> p (a b)")
        cmp_p = tmpf[:, 0:1024].rearrange("p (x n) -> p x n", n=32)
        cmp_pT = tmpf[:, 1024:2048].rearrange("p (g t) -> p g t", g=4)

        ident_loaded = sem("ident_loaded")
        const_loaded = sem("const_loaded")
        x_loaded = [sem(f"x{tb}_loaded") for tb in range(2)]
        table_loaded = sem("table_loaded")
        rows_stored = sem("rows_stored")
        bias1_loaded = sem("bias1_loaded")
        bias2_loaded = sem("bias2_loaded")
        poolw_loaded = sem("poolw_loaded")
        memx_loaded = sem("memx_loaded")
        ws_loaded = sem("ws_loaded")
        sgu_gb_loaded = sem("sgu_gb_loaded")
        cmp_w2_loaded = sem("cmp_w2_loaded")
        gb_loaded = [sem(f"gb{r}_loaded") for r in range(2)]
        raw_loaded = [sem(f"raw_loaded{s}") for s in range(RING)]
        whi_ready = sem("whi_ready")
        wlo_ready = sem("wlo_ready")
        w_used = sem("w_used")
        bank_full = [sem(f"bank_full{b}") for b in range(8)]
        bank_read = [sem(f"bank_read{b}") for b in range(8)]
        hi_rounded = sem("hi_rounded")
        sumsq_ready = sem("sumsq_ready")
        var_ready = sem("var_ready")
        rstd_ready = sem("rstd_ready")
        xn_ready = sem("xn_ready")
        res_ready = sem("res_ready")
        silu_ready = sem("silu_ready")
        zeros_ready = sem("zeros_ready")
        selected = sem("selected")
        bias_masked = sem("bias_masked")
        pooled = sem("pooled")
        max_ready = sem("max_ready")
        exp_ready = sem("exp_ready")
        prob_ready = sem("prob_ready")
        ws_masked = sem("ws_masked")
        zv_normed = sem("zv_normed")
        zv_ready = sem("zv_ready")
        cmp_f_ready = sem("cmp_f_ready")
        cmp_gr_ready = sem("cmp_gr_ready")
        cmp_exp_in = sem("cmp_exp_in")
        cmp_exp_out = sem("cmp_exp_out")
        cmp_p_ready = sem("cmp_p_ready")
        act_step = sem("act_step")
        dve_step = sem("dve_step")
        pool_step = sem("pool_step")
        out_stored = sem("out_stored")

        unit_loads = []
        unit_len = []
        first = {}

        def slot_view(s, kt):
            return raw[:, s, :].rearrange("p (k c) -> p k c", k=kt)

        def rows(w, k0, kt, c0, cols):
            return w[k0 * P:(k0 + kt) * P, c0:c0 + cols].rearrange("(k p) c -> p k c", p=P)

        def unit(w, k0, kt, c0, cols):
            s = len(unit_loads) % RING
            dst = raw[:, s, 0:kt * cols].rearrange("p (k c) -> p k c", k=kt)
            h = kt // 2
            unit_loads.append([(dst[:, 0:h, :], rows(w, k0, h, c0, cols)),
                               (dst[:, h:kt, :], rows(w, k0 + h, h, c0, cols))])
            unit_len.append(kt * cols)

        def columns_256(name, w, c0, n):
            first[name] = len(unit_loads)
            for j in range(n):
                unit(w, 0, KD, c0 + 256 * j, 256)

        def chunks_512(name, w, c0, chunks, kt):
            first[name] = len(unit_loads)
            for c in range(chunks):
                for k0 in range(0, kt, 4):
                    unit(w, k0, 4, c0 + 512 * c, 512)

        def swiglu_units(n):
            first["ffn", n] = len(unit_loads)
            unit_loads.extend([None] * (3 * FSTEPS))
            unit_len.extend([UNIT] * (3 * FSTEPS))

        W_IN = A["w_in"]
        chunks_512("gate0", W_IN, C_GATE, 1, KD)
        first["kidx"] = len(unit_loads)
        unit(W_IN, 0, KD, C_KI, P)
        columns_256("qidx", W_IN, C_QI, 1)
        columns_256("kv", W_IN, C_K, 1)
        columns_256("q", W_IN, C_Q, 4)
        columns_256("u", W_IN, C_POOL, 2)
        chunks_512("gate", W_IN, C_GATE + 512, 3, KD)
        chunks_512("pp", A["w_proj_pool"], 0, 2, 4)
        chunks_512("pa", A["w_proj_attn"], 0, 2, KD)
        chunks_512("out", A["w_out"], 0, 2, KD)
        columns_256("km", A["w_kv_mem"], 0, 2)
        chunks_512("vm", A["w_kv_mem"], 512, 1, KD)
        columns_256("qm", A["w_q_mem"], 0, 2)
        chunks_512("om", A["w_o_mem"], 0, 2, 4)
        swiglu_units(0)
        swiglu_units(1)
        chunks_512("sgv", A["sgu_w_in_2"][0], 2048, 4, KD)
        chunks_512("sgu", A["sgu_w_in_2"][0], 0, 4, KD)
        chunks_512("sgo", A["sgu_w_out_2"][0], 0, 2, 16)
        swiglu_units(2)
        KV = A["kv_w_2"]
        columns_256("v2", KV, 768, 1)
        columns_256("v2w", KV, 1280, 1)
        for slot in range(2):
            columns_256(("cin", slot), KV, 256 * slot, 1)
            first["cw1", slot] = len(unit_loads)
            for k0 in (0, 8):
                unit(A["cmp_w1_2"][slot], k0, 8, 0, 256)
        swiglu_units(3)
        columns_256("k2", KV, 512, 1)
        columns_256("k2w", KV, 1024, 1)
        columns_256("q2", A["nsa_w_qg_2"][0], 0, 4)
        first["g2"] = len(unit_loads)
        unit(A["nsa_w_qg_2"][0], 0, KD, D, 48)
        chunks_512("o2", A["nsa_w_o_2"][0], 0, 2, KD)
        swiglu_units(4)
        UNITS = len(unit_loads)
        GU = A["w_gate_up"]
        SWIGLU = [(GU[:, 0:DFF], GU[:, DFF:2 * DFF], A["w_down"])]
        for a, b in ((0, 0), (0, 1), (1, 0), (1, 1)):
            SWIGLU.append((A["ffn_w1_2"][a, b], A["ffn_w3_2"][a, b], A["ffn_w2_2"][a, b]))

        def at(base, i=0):
            return base + RING * i, base % RING, base // RING + i

        use = {}
        fills = [0] * 8
        signal = {}
        signals = [0] * 8
        split_no = {}
        splits = [0]

        def plan(key, bank, split=False, times=1, unit=None):
            use[key] = (bank, fills[bank])
            fills[bank] += times
            if unit is None:
                signal[key] = (bank_full[bank], signals[bank] + 1)
                signals[bank] += times
            else:
                signal[key] = (w_used, unit + 1)
            if split:
                plan_split(key, times)

        def plan_split(key, times=1):
            split_no[key] = splits[0]
            splits[0] += times

        def plan_chunks(keys, banks, u0, units):
            for c, b in enumerate(banks):
                plan(keys(c, 0), b)
                plan(keys(c, 1), b + 1, unit=u0 + units * (c + 1) - 1)

        def plan_st(name, tiles=KD):
            for tb in range(2):
                for q in range(tiles // 4):
                    plan(("st", name, tb, q), 6 + q % 2, split=True)

        def plan_y(n, u0, units):
            for h in range(2):
                plan(("y", n, 0, h), h)
                plan(("y", n, 1, h), 2 + h, unit=u0 + units * (h + 1) - 1)

        def plan_ffn(n):
            plan(("up", n, 0), 4, times=FSTEPS)
            plan(("up", n, 1), 5, times=FSTEPS, unit=first["ffn", n] + 1)
            plan(("hid", n), 6, split=True, times=FSTEPS - 1)
            for tb in range(2):
                plan(("hid_last", n, tb), 6 + tb, split=True)
            for tb, h in ((0, 0), (0, 1), (1, 0)):
                plan(("y", ("ffn", n), tb, h), 2 * tb + h)
            plan(("y", ("ffn", n), 1, 1), 3, unit=first["ffn", n] + 3 * FSTEPS - 1)

        plan_st("mix")
        plan_chunks(lambda c, tb: ("gate", 0, tb), (2,), first["gate0"], 2)
        plan("rows", 0)
        plan("kidx", 4)
        plan("widx", 5, unit=first["kidx"])
        plan("qidx", 0, unit=first["qidx"])
        plan("kv", 1, unit=first["kv"])
        for j, b in enumerate((2, 3, 4)):
            plan(("dots", j), b)
        for j, b in enumerate((5, 0, 1, 5)):
            plan(("q", j), b, unit=first["q"] + j)
        for j in range(2):
            plan(("rev1", j), 6 + j)
        for j in range(2):
            plan(("u", j), j, unit=first["u"] + j)
        for j in range(2):
            plan(("rev1", 2 + j), 6 + j)
        for j in range(2):
            plan(("pool", j), 6 + j, split=True)
        plan_chunks(lambda c, tb: ("gate", 1 + c, tb), (4, 0, 2), first["gate"], 2)
        plan_chunks(lambda c, tb: ("pp", c, tb), (4, 0), first["pp"], 1)
        for h in range(HEADS1):
            plan(("L1", h), h % 2)
            plan(("T1", h), 2 + h % 2)
            plan(("O1", h), 4 + h % 2, split=True)
        plan_chunks(lambda c, tb: ("pa", c, tb), (0, 2), first["pa"], 2)
        plan_st("merged")
        plan_st("mem")
        plan_y("mix", first["out"], 2)
        for j in range(2):
            plan(("km", j), 4 + j, unit=first["km"] + j)
        plan_chunks(lambda c, tb: ("vm", tb), (4,), first["vm"], 2)
        plan_st("memq")
        for j in range(2):
            plan(("qm", j), 4 + j, unit=first["qm"] + j)
        for h in range(4):
            plan(("Lm", h), h % 2)
            plan(("Tm", h), 2 + h % 2)
            plan(("Om", h), 4 + h % 2, split=True)
        plan_y("mem", first["om"], 1)
        plan_st("ffn0")
        plan_ffn(0)
        plan_st("b2")
        plan_ffn(1)
        plan_st("ln0")
        for j in range(2):
            plan(("wsT", j), 6 + j)
        plan_chunks(lambda c, tb: ("sgv", c, tb), (0, 2, 4, 0), first["sgv"], 2)
        plan_chunks(lambda c, tb: ("sgu", c, tb), (2, 4, 0, 2), first["sgu"], 2)
        for tb in range(2):
            for gp in range(4):
                plan(("mixed", tb, gp), 2 + gp)
        plan_st("um", 16)
        plan_y("sgu", first["sgo"], 4)
        plan_st("ln1")
        plan_ffn(2)
        plan_st("ln2")
        for j, name in enumerate(("v2", "v2w")):
            plan(name, 2 + j, unit=first[name])
        plan(("cin", 0), 4, unit=first["cin", 0])
        for j in range(4):
            plan(("rev2", j), (6, 7, 2, 3)[j])
        plan_split(("cf", 0))
        plan(("cg", 0), 0, unit=first["cw1", 0] + 1)
        plan(("cin", 1), 4, unit=first["cin", 1])
        plan(("cgT", 0), 1)
        for j in range(4, 8):
            plan(("rev2", j), (6, 7, 2, 3)[j - 4])
        plan_split(("cf", 1))
        plan("kc", 5)
        plan(("cg", 1), 0, unit=first["cw1", 1] + 1)
        plan_ffn(3)
        plan("k2", 4, unit=first["k2"])
        plan(("cgT", 1), 6)
        plan("k2w", 5, unit=first["k2w"])
        plan_st("ln3")
        for j in range(4):
            plan(("q2", j), j, unit=first["q2"] + j)
        plan("g2", 4, unit=first["g2"])
        plan("vc", 6)
        plan("Lc", 5)
        for h in range(HEADS2):
            plan(("L2", h, 0), 2 * (h % 2))
            plan(("L2", h, 1), 2 * (h % 2) + 1)
            plan(("T2", h, 0), 6)
            plan(("T2", h, 1), 7)
            if h == 1:
                plan(("Tc", 0), 6)
                plan(("Tc", 1), 7)
            if h % 2 == 0:
                plan(("O2", h // 2), 4 + (h // 2) % 2, split=True)
        plan_y("nsa", first["o2"], 2)
        plan_st("ln4")
        plan_ffn(4)

        def bank(key):
            return ps[:, use[key][0], :]

        def full(key, i=0):
            s, n = signal[key]
            return s, n + i

        def read(key, i=0):
            b, n = use[key]
            return bank_read[b], n + 1 + i

        def is_full(key):
            return bank_full[use[key][0]], 1

        def is_read(key):
            return bank_read[use[key][0]], 1

        NORM_ORDER = ["mix", "mem", ("ffn", 0), ("ffn", 1), "sgu", ("ffn", 2), ("ffn", 3), "nsa", ("ffn", 4)]
        RES = {name: 4 * i for i, name in enumerate(NORM_ORDER)}
        XN = {name: 4 * i for i, name in enumerate(["mix", "mem", "merged", "memq", "ffn0"])}
        GB0 = {name: 16 * (i + 1) for i, name in enumerate(NORM_ORDER)}
        GB1 = {name: 16 * (i + 1) for i, name in enumerate(["mix", "mem", "memq", "ffn0"] + NORM_ORDER[3:])}
        SQ_ORDER = [("mix", 0), ("mix", 1), ("mem", 0), ("mem", 1)]
        for y, x in (("ymix", "memq"), ("ymem", "ffn0")):
            SQ_ORDER += [(y, 0), (x, 0), (y, 1), (x, 1)]
        SQ_ORDER += [("yffn0", 0), ("yffn0", 1)]
        SQ = {key: i for i, key in enumerate(SQ_ORDER)}
        VAR_ORDER = [(name, tb) for name in (("ffn", 1), "zv", "sgu", ("ffn", 2), ("ffn", 3), "nsa", ("ffn", 4))
                     for tb in range(2)]
        VAR = {key: i for i, key in enumerate(VAR_ORDER)}
        RS = {key: i for i, key in enumerate(SQ_ORDER + VAR_ORDER)}
        BY_POOL = set()
        for name in ("sgv", ("ffn", 2), "v2", "k2", ("ffn", 4)):
            BY_POOL |= {first[name], first[name] + 1}

        def half_ready(name, tb, h):
            if name == "merged":
                return xn_ready, XN[name] + 2 * h + tb + 1
            if name in XN:
                return xn_ready, XN[name] + 2 * tb + h + 1
            n = {"b2": ("ffn", 0), "ln0": ("ffn", 1), "ln1": "sgu", "ln2": ("ffn", 2), "ln3": ("ffn", 3),
                 "ln4": "nsa", "out": ("ffn", 4)}[name]
            return res_ready, RES[n] + 2 * tb + h + 1

        ATT0 = {"self": 0, "mem": HEADS1, "nsa": HEADS1 + 4}

        block = ctx.enter_context(nc.Block())

        @block.sync
        def _(sp):
            for tb in range(2):
                sp.dma_start(res[:, tb, :], A["x"][0, tb * P:tb * P + P, :]).then_inc(x_loaded[tb], 16)
            sp.dma_start(ident, A["shape_consts"][:, K_ID:K_ID + P]).then_inc(ident_loaded, 16)

            def slot_free(u):
                sp.wait_ge(wlo_ready, u - 2)

            def load_up(n, i, half, u, s):
                slot_free(u)
                dst = raw[:, s, :].rearrange("p (k g c) -> p k g c", k=4, g=2)
                for g in range(2):
                    w = SWIGLU[n][g][512 * half:512 * half + 512, bass.ds(FC * i, FC)]
                    sp.dma_start(dst[:, :, g, :], w.rearrange("(k p) c -> p k c", p=P)).then_inc(raw_loaded[s], 16)

            def load_down(n, i, u, s):
                slot_free(u)
                dst = slot_view(s, 2)
                w = SWIGLU[n][2][bass.ds(FC * i, FC), :].rearrange("(k p) c -> p k c", p=P)
                for h in range(2):
                    sp.dma_start(dst[:, h:h + 1, :], w[:, h:h + 1, :]).then_inc(raw_loaded[s], 16)

            def step(n, i, u0):
                for half in range(2):
                    u, s, _ = at(u0 + 2 + half, i - 1)
                    load_up(n, i, half, u, s)
                u, s, _ = at(u0 + 4, i - 1)
                load_down(n, i - 1, u, s)

            u = 0
            ffn = 0
            while u < UNITS:
                if unit_loads[u] is not None:
                    if u >= RING:
                        slot_free(u)
                    for dst, src in unit_loads[u]:
                        sp.dma_start(dst, src).then_inc(raw_loaded[u % RING], 16)
                    if u == 1:
                        sp.dma_start(con[:, K_ID + P:], A["shape_consts"][:, K_ID + P:]).then_inc(const_loaded, 16)
                        sp.dma_start(vec[:, :], A["vectors"]).then_inc(const_loaded, 16)
                    u += 1
                    continue
                for half in range(2):
                    load_up(ffn, 0, half, u + half, (u + half) % RING)
                with sp.Fori(1, FSTEPS - 1) as i:
                    step(ffn, i, u)
                step(ffn, FSTEPS - 1, u)
                last = u + 3 * FSTEPS - 1
                load_down(ffn, FSTEPS - 1, last, last % RING)
                u += 3 * FSTEPS
                ffn += 1
            for tb in range(2):
                for h in range(2):
                    sp.wait_ge(*half_ready("out", tb, h))
                    sp.dma_start(out[0, tb * P:tb * P + P, 512 * h:512 * h + 512],
                                 res[:, tb, 512 * h:512 * h + 512]).then_inc(out_stored, 16)
            sp.wait_ge(out_stored, 64)

        @block.tensor
        def _(pe):
            def room(key):
                b, n = use[key]
                if n:
                    pe.wait_ge(bank_read[b], n)

            def product(o, a, b, start, stop):
                pe.matmul(o, a[0], b[0], start=start, stop=False)
                pe.matmul(o, a[0], b[1], start=False, stop=False)
                return pe.matmul(o, a[1], b[0], start=False, stop=stop)

            def weights(u, kt, cols):
                pe.wait_ge(wlo_ready, u + 1)
                s = u % RING
                n = kt * cols
                return [w[:, s, 0:n].rearrange("p (k c) -> p k c", k=kt) for w in (whi, wlo)]

            def features(u, tiles, k0=0, st=None):
                w = weights(u, KD, unit_len[u] // KD)
                for t, (c, o) in enumerate(tiles):
                    for k in range(KD):
                        if st is not None and t == 0 and k % 4 == 0:
                            wait_st(st, k // 4)
                        mm = product(o, [x[:, k, c:c + P] for x in w], [x[:, k0 + k, :] for x in (st_hi, st_lo)],
                                     k == 0, k == KD - 1)
                return mm

            def tokens(w, outs, kts, k0, start, stop):
                done = []
                for tb, o in enumerate(outs):
                    for k in range(kts):
                        mm = product(o, [x[:, k0 + k, tb * P:tb * P + P] for x in (st_hi, st_lo)],
                                     [x[:, k, :] for x in w], start and k == 0, stop and k == kts - 1)
                    done.append(mm)
                return done

            turned = set()

            def turn_st(name, src, tb, q):
                if name != "um":
                    pe.wait_ge(*half_ready(name, tb, q))
                key = ("st", name, tb, q)
                room(key)
                for k in range(4):
                    mm = pe.transpose(bank(key)[:, k * P:k * P + P],
                                      src[:, tb, (4 * q + k) * P:(4 * q + k + 1) * P], ident)
                mm.then_inc(*is_full(key))
                turned.add(key)

            def transpose_st(name, src, tb, tiles=KD):
                for q in range(tiles // 4):
                    if ("st", name, tb, q) not in turned:
                        turn_st(name, src, tb, q)

            def wait_st(name, q):
                for tb in range(2):
                    pe.wait_ge(*read(("st", name, tb, q)))

            def by_block(parts, st=None, src=None, ahead=None):
                for tb in range(2):
                    if st is not None:
                        transpose_st(st, src, tb)
                    for u, kt, cols, k0, outs, keys, start, stop in parts:
                        w = weights(u, kt, cols)
                        if start:
                            room(keys[tb])
                        for k in range(kt):
                            if (u, k) == (parts[-1][0], kt - 2):
                                if tb == 0 and st is not None:
                                    turn_st(st, src, 1, 0)
                                if tb == 1 and ahead is not None:
                                    ahead()
                            if st is not None and (k0 + k) % 4 == 0:
                                pe.wait_ge(*read(("st", st, tb, (k0 + k) // 4)))
                            mm = product(outs[tb], [x[:, k0 + k, tb * P:tb * P + P] for x in (st_hi, st_lo)],
                                         [x[:, k, :] for x in w], start and k == 0, stop and k == kt - 1)
                        if tb == 1:
                            mm.then_inc(w_used, 1)
                        elif stop and keys[0] != keys[1]:
                            mm.then_inc(*is_full(keys[0]))

            def chunk_part(u, q, per_chunk, keys, c, k0=0):
                ks = [keys(c, tb) for tb in range(2)]
                return (u, 4, 512, k0 + 4 * q, [bank(k) for k in ks], ks, q == 0, q == per_chunk - 1)

            def chunked(u0, chunks, kt, keys, k0=0, c0=0, st=None, src=None, tail=False, waits=None, ahead=None):
                per = kt // 4
                todo = [(c, q) for c in range(chunks) for q in range(per)]
                n = 0
                while n < len(todo):
                    pair = (st is not None and n == 0) or (tail and n == len(todo) - 2)
                    if pair:
                        by_block([chunk_part(u0 + n + x, todo[n + x][1], per, keys, c0 + todo[n + x][0], k0)
                                  for x in range(2)], st if n == 0 else None, src,
                                 ahead if n == len(todo) - 2 else None)
                        n += 2
                        continue
                    c, q = todo[n]
                    c += c0
                    if waits is not None and n < per:
                        waits(q)
                    if q == 0:
                        for tb in range(2):
                            room(keys(c, tb))
                    w = weights(u0 + n, 4, 512)
                    last = q == per - 1
                    mms = tokens(w, [bank(keys(c, tb)) for tb in range(2)], 4, k0 + 4 * q, q == 0, last)
                    if last:
                        mms[0].then_inc(*is_full(keys(c, 0)))
                    mms[1].then_inc(w_used, 1)
                    n += 1

            pe.wait_ge(ident_loaded, 16)
            chunked(first["gate0"], 1, KD, lambda c, tb: ("gate", 0, tb), st="mix", src=tmp)
            pe.wait_ge(const_loaded, 32)
            pe.wait_ge(table_loaded, 32)
            pe.wait_ge(zeros_ready, 1)
            room("rows")
            pe.matmul(bank("rows"), table[:, :], con[:, K_HOT:K_HOT + 512], start=True,
                      stop=True).then_inc(*is_full("rows"))
            room("kidx")
            u = first["kidx"]
            features(u, [(0, bank("kidx")[:, 0:S])]).then_inc(*is_full("kidx"))
            room("widx")
            w = weights(u, KD, P)
            mms = tokens([x[:, :, 64:68] for x in w], [bank("widx")[:, 4 * tb:4 * tb + 4] for tb in range(2)],
                         KD, 0, True, True)
            mms[1].then_inc(w_used, 1)
            room("qidx")
            u = first["qidx"]
            features(u, [(0, bank("qidx")[:, 0:S]), (P, bank("qidx")[:, S:2 * S])]).then_inc(w_used, 1)
            room("kv")
            u = first["kv"]
            features(u, [(0, bank("kv")[:, 0:S])])
            w = weights(u, KD, 256)
            mms = tokens([x[:, :, P:2 * P] for x in w],
                         [bank("kv")[:, S + tb * P:S + tb * P + P] for tb in range(2)], KD, 0, True, True)
            mms[1].then_inc(w_used, 1)

            pe.wait_ge(*read("kidx"))
            pe.wait_ge(*read("qidx"))
            room(("dots", 0))
            for j in range(2):
                mm = pe.matmul(bank(("dots", 0))[:, S * j:S * j + S].rearrange("p (a b) -> p a b", a=2),
                               qidx[:, j, 0:P], kidx[:, :, 0:P], start=True, stop=True)
            mm.then_inc(*is_full(("dots", 0)))
            for j in range(2):
                room(("dots", 1 + j))
                pe.matmul(bank(("dots", 1 + j)), qidx[:, j, P:2 * P], kidx[:, :, :].rearrange("p a b -> p (a b)"),
                          start=True, stop=True).then_inc(*is_full(("dots", 1 + j)))

            def feature_pairs(name, n, k0=0, st=None):
                for j in range(n):
                    key = (name, j)
                    room(key)
                    features(first[name] + j, [(0, bank(key)[:, 0:S]), (P, bank(key)[:, S:2 * S])],
                             k0, st if j == 0 else None).then_inc(w_used, 1)

            def reverse_rows(name, shifted, j):
                key = (name, j)
                room(key)
                pe.matmul(bank(key), reverse, shifted[:, 2 * j:2 * j + 2, :].rearrange("p a b -> p (a b)"),
                          start=True, stop=True).then_inc(*is_full(key))

            feature_pairs("q", 4)
            pe.wait_ge(bias1_loaded, 16)
            reverse_rows("rev1", shifted1, 0)
            reverse_rows("rev1", shifted1, 1)
            feature_pairs("u", 2)
            reverse_rows("rev1", shifted1, 2)
            reverse_rows("rev1", shifted1, 3)
            chunked(first["gate"], 2, KD, lambda c, tb: ("gate", c, tb), c0=1)

            pe.wait_ge(pooled, 1)
            pe.wait_ge(poolw_loaded, 16)
            for j in range(2):
                room(("pool", j))
                for g in (2 * j, 2 * j + 1):
                    src = (winA, winB)[g % 2]
                    mm = pe.matmul(bank(("pool", j))[:, (g % 2) * S:(g % 2 + 1) * S], poolw[:, g, :],
                                   src[:, g, 16:272], start=True, stop=True)
                mm.then_inc(*is_full(("pool", j)))
            chunked(first["gate"] + 4, 1, KD, lambda c, tb: ("gate", c, tb), c0=3)
            pe.wait_ge(*read(("pool", 0)))
            pe.wait_ge(*read(("pool", 1)))
            chunked(first["pp"], 2, 4, lambda c, tb: ("pp", c, tb), k0=8)

            for t in range(HEADS1 + 3):
                h = t
                if h < HEADS1:
                    if h == 0:
                        pe.wait_ge(*read(("q", 3)))
                        pe.wait_ge(*read("kv"))
                    room(("L1", h))
                    L = bank(("L1", h))
                    pe.matmul(L[:, 0:P], q1[:, h, 0:P], k1[:, 0:P], start=True, stop=True)
                    pe.matmul(L[:, P:3 * P], q1[:, h, P:S], k1[:, :], start=True,
                              stop=True).then_inc(*is_full(("L1", h)))
                h = t - 2
                if 0 <= h < HEADS1:
                    room(("T1", h))
                    pe.wait_ge(prob_ready, ATT0["self"] + h + 1)
                    T, pr = bank(("T1", h)), prob1[:, h % 3, :]
                    for c in range(3):
                        mm = pe.transpose(T[:, c * P:c * P + P], pr[:, c * P:c * P + P], ident)
                    mm.then_inc(*is_full(("T1", h)))
                h = t - 3
                if 0 <= h < HEADS1:
                    room(("O1", h))
                    pe.wait_ge(*read(("T1", h)))
                    O, pT = bank(("O1", h)), probT1[:, h % 2, :]
                    pe.matmul(O[:, 0:P], v1[:, 0, :], pT[:, 0:P], start=True, stop=True)
                    pe.matmul(O[:, P:S], v1[:, 0, :], pT[:, P:S], start=True, stop=False)
                    pe.matmul(O[:, P:S], v1[:, 1, :], pT[:, S:S + P], start=False,
                              stop=True).then_inc(*is_full(("O1", h)))
            def heads1(q):
                for h in range(4 * q + 2, 4 * q + 4):
                    pe.wait_ge(*read(("O1", h)))

            chunked(first["pa"], 2, KD, lambda c, tb: ("pa", c, tb), tail=True, waits=heads1,
                    ahead=lambda: turn_st("merged", tmp, 0, 0))
            chunked(first["out"], 1, KD, lambda c, tb: ("y", "mix", tb, c), st="merged", src=tmp,
                    ahead=lambda: transpose_st("mem", memx, 0))
            transpose_st("mem", memx, 1)
            chunked(first["out"] + 2, 1, KD, lambda c, tb: ("y", "mix", tb, c), c0=1, tail=True)

            feature_pairs("km", 2, 8, st="mem")
            chunked(first["vm"], 1, KD, lambda c, tb: ("vm", tb), 8, tail=True,
                    ahead=lambda: transpose_st("memq", tmp, 0))
            transpose_st("memq", tmp, 1)
            feature_pairs("qm", 2, st="memq")
            for t in range(4 + 3):
                h = t
                if h < 4:
                    if h == 0:
                        pe.wait_ge(*read(("qm", 0)))
                        pe.wait_ge(*read(("qm", 1)))
                    room(("Lm", h))
                    for tb in range(2):
                        mm = pe.matmul(bank(("Lm", h))[:, tb * S:tb * S + S], qm[:, h, tb * P:tb * P + P],
                                       km[:, h, :], start=True, stop=True)
                    mm.then_inc(*is_full(("Lm", h)))
                h = t - 2
                if 0 <= h < 4:
                    room(("Tm", h))
                    pe.wait_ge(prob_ready, ATT0["mem"] + h + 1)
                    for kb in range(2):
                        for tb in range(2):
                            c = (2 * kb + tb) * P
                            mm = pe.transpose(bank(("Tm", h))[:, c:c + P],
                                              probm[:, h % 3, tb * S + kb * P:tb * S + kb * P + P], ident)
                    mm.then_inc(*is_full(("Tm", h)))
                h = t - 3
                if 0 <= h < 4:
                    room(("Om", h))
                    pe.wait_ge(*read(("Tm", h)))
                    for kb in range(2):
                        mm = pe.matmul(bank(("Om", h))[:, 0:S], vm[:, kb, h * P:h * P + P],
                                       probTm[:, h % 2, kb * S:kb * S + S], start=kb == 0, stop=kb == 1)
                    mm.then_inc(*is_full(("Om", h)))
            for h in (2, 3):
                pe.wait_ge(*read(("Om", h)))
            chunked(first["om"], 2, 4, lambda c, tb: ("y", "mem", tb, c), k0=8, tail=True)

            def swiglu(n, name=None, src=None, ahead=None):
                u0 = first["ffn", n]
                up = [("up", n, tb) for tb in range(2)]
                hid = ("hid", n)
                ykeys = [[("y", ("ffn", n), tb, h) for h in range(2)] for tb in range(2)]

                def gate_up(i, base, j):
                    for half in range(2):
                        u, s, _ = at(base + half, j)
                        pe.wait_ge(wlo_ready, u + 1)
                        w = [x[:, s, :].rearrange("p (k c) -> p k c", k=4) for x in (whi, wlo)]
                        if half == 0:
                            for key in up:
                                b, c = use[key]
                                pe.wait_ge(bank_read[b], c + i)
                        mms = tokens(w, [bank(key) for key in up], 4, 4 * half, half == 0, half == 1)
                        if half == 1:
                            mms[0].then_inc(*is_full(up[0]))
                        mms[1].then_inc(w_used, 1)

                def down_block(w, x_hi, x_lo, tb, start=False, end=False, ahead=None):
                    for h in range(2):
                        for f in range(2):
                            if ahead is not None and (h, f) == (1, 1):
                                ahead()
                            mm = product(bank(ykeys[tb][h]), [x[:, f, tb * P:tb * P + P] for x in (x_hi, x_lo)],
                                         [x[:, f, 512 * h:512 * h + 512] for x in w], start and f == 0,
                                         end and f == 1)
                        if end and (tb, h) != (1, 1):
                            mm.then_inc(*is_full(ykeys[tb][h]))
                    return mm

                def down_weights(base, j):
                    u, s, _ = at(base, j)
                    pe.wait_ge(wlo_ready, u + 1)
                    return [x[:, s, :].rearrange("p (k c) -> p k c", k=2) for x in (whi, wlo)]

                def down(i, base, j, start=False):
                    pe.wait_ge(*read(hid, i))
                    w = down_weights(base, j)
                    down_block(w, hid_hi, hid_lo, 0, start)
                    down_block(w, hid_hi, hid_lo, 1, start).then_inc(w_used, 1)

                def turn(i):
                    for key in up:
                        pe.wait_ge(*read(key, i))
                    b, c = use[hid]
                    pe.wait_ge(bank_read[b], c + i)
                    for f in range(2):
                        for tb in range(2):
                            mm = pe.transpose(bank(hid)[:, (2 * f + tb) * P:(2 * f + tb + 1) * P],
                                              hidden[:, tb, f * P:f * P + P], ident)
                    mm.then_inc(*is_full(hid))

                def turn_last(tb):
                    key = ("hid_last", n, tb)
                    pe.wait_ge(*read(up[tb], FSTEPS - 1))
                    room(key)
                    for f in range(2):
                        mm = pe.transpose(bank(key)[:, f * P:f * P + P], hidden[:, tb, f * P:f * P + P], ident)
                    mm.then_inc(*is_full(key))

                by_block([(u0 + half, 4, 512, 4 * half, [bank(key) for key in up], up, half == 0, half == 1)
                          for half in range(2)], st=name, src=src)
                turn(0)
                gate_up(1, u0 + 2, 0)
                for key in (k for pair in ykeys for k in pair):
                    room(key)
                down(0, u0 + 4, 0, start=True)
                turn(1)
                with pe.Fori(2, FSTEPS - 1) as i:
                    gate_up(i, u0 + 2, i - 1)
                    down(i - 1, u0 + 4, i - 1)
                    turn(i)
                i = FSTEPS - 1
                gate_up(i, u0 + 2, i - 1)
                turn_last(0)
                pe.wait_ge(*read(hid, i - 1))
                w_before = down_weights(u0 + 4, i - 1)
                down_block(w_before, hid_hi, hid_lo, 0)
                turn_last(1)
                w_last = down_weights(u0 + 3 * FSTEPS - 1, 0)
                last = [x[:, 8:10, :] for x in (st_hi, st_lo)]
                pe.wait_ge(*read(("hid_last", n, 0)))
                down_block(w_last, *last, 0, end=True)
                down_block(w_before, hid_hi, hid_lo, 1).then_inc(w_used, 1)
                pe.wait_ge(*read(("hid_last", n, 1)))
                down_block(w_last, *last, 1, end=True, ahead=ahead).then_inc(w_used, 1)

            swiglu(0, "ffn0", tmp, ahead=lambda: turn_st("b2", res, 0, 0))

            swiglu(1, "b2", res, ahead=lambda: turn_st("ln0", res, 0, 0))
            chunked(first["sgv"], 1, KD, lambda c, tb: ("sgv", c, tb), st="ln0", src=res)
            pe.wait_ge(ws_masked, 1)
            for j in range(2):
                room(("wsT", j))
                for q in range(4):
                    mm = pe.transpose(bank(("wsT", j))[:, q * P:q * P + P], ws[:, 4 * j + q, :], ident)
                mm.then_inc(*is_full(("wsT", j)))
            chunked(first["sgv"] + 2, 3, KD, lambda c, tb: ("sgv", c, tb), c0=1)
            chunked(first["sgu"], 4, KD, lambda c, tb: ("sgu", c, tb))
            pe.wait_ge(zv_ready, 2)
            pe.wait_ge(*read(("wsT", 0)))
            pe.wait_ge(*read(("wsT", 1)))
            for tb in range(2):
                for gp in range(4):
                    key = ("mixed", tb, gp)
                    room(key)
                    for g in (2 * gp, 2 * gp + 1):
                        mm = pe.matmul(bank(key)[:, (g % 2) * S:(g % 2 + 1) * S], wsT[:, g, :],
                                       zv[:, tb, g * S:g * S + S], start=True, stop=True)
                    mm.then_inc(*is_full(key))
            for tb in range(2):
                for gp in range(4):
                    pe.wait_ge(*read(("mixed", tb, gp)))
                transpose_st("um", zu, tb, 16)
            chunked(first["sgo"], 2, 16, lambda c, tb: ("y", "sgu", tb, c),
                    waits=lambda q: wait_st("um", q), tail=True, ahead=lambda: turn_st("ln1", res, 0, 0))
            swiglu(2, "ln1", res, ahead=lambda: turn_st("ln2", res, 0, 0))

            by_block([(first[name], KD, 256, 0, [bank(name)[:, tb * S:tb * S + S] for tb in range(2)], [name, name],
                       True, True) for name in ("v2", "v2w")], st="ln2", src=res)
            pe.wait_ge(bias2_loaded, 16)
            def cmp_in(slot):
                key = ("cin", slot)
                room(key)
                features(first["cin", slot], [(0, bank(key)[:, 0:S]), (P, bank(key)[:, S:2 * S])]).then_inc(w_used, 1)

            def cmp_hidden(slot):
                pe.wait_ge(cmp_f_ready, 2 * slot + 2)
                key = ("cg", slot)
                room(key)
                x = [y[:, 8:12, :].rearrange("p a b -> p (a b)")[:, 0:960].rearrange("p (k c) -> p k c", k=16)
                     for y in (st_hi, st_lo)]
                for half in range(2):
                    w = weights(first["cw1", slot] + half, KD, 256)
                    for k in range(KD):
                        mm = product(bank(key)[0:60, 0:256], [y[:, 8 * half + k, :] for y in x],
                                     [y[:, k, :] for y in w], half == 0 and k == 0, half == 1 and k == KD - 1)
                    mm.then_inc(w_used, 1)

            def cmp_turn(slot):
                key = ("cgT", slot)
                pe.wait_ge(*read(("cg", slot)))
                room(key)
                for f in range(2):
                    mm = pe.transpose(bank(key)[:, 64 * f:64 * f + 60], cmp_x[0:60, slot, f * P:f * P + P],
                                      ident[0:60, 0:60])
                mm.then_inc(*is_full(key))

            cmp_in(0)
            for j in range(4):
                reverse_rows("rev2", shifted2, j)
            cmp_hidden(0)
            cmp_in(1)
            cmp_turn(0)
            for j in range(4, 8):
                reverse_rows("rev2", shifted2, j)
            pe.wait_ge(cmp_w2_loaded, 64)
            pe.wait_ge(*read(("cgT", 0)))
            room("kc")
            for f in range(2):
                mm = pe.matmul(bank("kc")[:, 0:P], cmp_w2[:, 0, f, :],
                               cmp_g[:, f, :, :].rearrange("p a b -> p (a b)"), start=f == 0, stop=f == 1)
            mm.then_inc(*is_full("kc"))
            cmp_hidden(1)
            swiglu(3)

            def keys2(name):
                room(name)
                features(first[name], [(0, bank(name)[:, 0:S]), (P, bank(name)[:, S:2 * S])]).then_inc(w_used, 1)

            keys2("k2")
            cmp_turn(1)
            keys2("k2w")
            for tb in range(2):
                transpose_st("ln3", res, tb)

            feature_pairs("q2", 4, 8, st="ln3")
            room("g2")
            w = weights(first["g2"], KD, 48)
            tokens(w, [bank("g2")[:, 48 * tb:48 * tb + 48] for tb in range(2)], KD, 8, True,
                   True)[1].then_inc(w_used, 1)
            pe.wait_ge(cmp_gr_ready, 1)
            room("vc")
            for g in range(4):
                for f in range(2):
                    mm = pe.matmul(bank("vc")[:, g * 64:g * 64 + 64], cmp_gr[:, f, g, :],
                                   cmp_w2[:, 1, f, 0:64], start=f == 0, stop=f == 1)
            mm.then_inc(*is_full("vc"))
            pT = cmp_pT

            def scores2(h):
                pair = h // 8
                for tb in range(2):
                    key = ("L2", h, tb)
                    room(key)
                    n = P * (tb + 1)
                    pe.matmul(bank(key)[:, 0:2 * n].rearrange("p (a b) -> p a b", a=2), q2[:, h, tb * P:tb * P + P],
                              k2[:, pair, :, 0:n], start=True, stop=True).then_inc(*is_full(key))

            def turn2(h):
                pe.wait_ge(prob_ready, ATT0["nsa"] + h + 1)
                pr = prob2[:, h % 3, :]
                room(("T2", h, 0))
                T = bank(("T2", h, 0))
                for br in range(2):
                    pe.transpose(T[:, 2 * br * P:2 * br * P + P], pr[:, br * P:br * P + P], ident)
                    mm = pe.transpose(T[:, (2 * br + 1) * P:(2 * br + 2) * P], pr[:, S + br * S:S + br * S + P], ident)
                mm.then_inc(*is_full(("T2", h, 0)))
                room(("T2", h, 1))
                T = bank(("T2", h, 1))
                for br in range(2):
                    mm = pe.transpose(T[:, br * P:br * P + P], pr[:, S + br * S + P:S + br * S + S], ident)
                mm.then_inc(*is_full(("T2", h, 1)))

            def values2(h):
                key = ("O2", h // 2)
                if h % 2 == 0:
                    room(key)
                pe.wait_ge(*read(("T2", h, 0)))
                pe.wait_ge(*read(("T2", h, 1)))
                r = 64 * (h % 2)
                O, g, p = bank(key)[r:r + 64, :], h // 4, probT2[:, h % 2, :]
                pe.matmul(O[:, 0:S], vc[:, g, h % 4, :], pT[:, g, :], start=True, stop=False)
                for br in range(2):
                    pe.matmul(O[:, P:S], v2[:, 1, br, g * 64:g * 64 + 64],
                              p[:, 512 + br * P:512 + br * P + P], start=False, stop=False)
                for br in range(2):
                    mm = pe.matmul(O[:, 0:S], v2[:, 0, br, g * 64:g * 64 + 64], p[:, br * S:br * S + S], start=False,
                                   stop=br == 1)
                if h % 2:
                    mm.then_inc(*is_full(key))

            for j in range(4):
                pe.wait_ge(*read(("q2", j)))
            def cmp_scores(heads):
                for h in heads:
                    g, j = h // 4, h % 4
                    for tb in range(2):
                        c = ((g * 2 + tb) * 4 + j) * 16
                        mm = pe.matmul(bank("Lc")[:, c:c + 16], q2[:, h, tb * P:tb * P + P], kc[:, g, 0:16],
                                       start=True, stop=True)
                return mm

            scores2(0)
            scores2(1)
            room("Lc")
            cmp_scores(range(0, HEADS2 // 2))
            for t in range(2, HEADS2 + 3):
                if t < HEADS2:
                    scores2(t)
                if t - 2 < HEADS2:
                    turn2(t - 2)
                if t == 2:
                    cmp_scores(range(HEADS2 // 2, HEADS2)).then_inc(*is_full("Lc"))
                if t == 3:
                    pe.wait_ge(cmp_p_ready, 1)
                    for q in range(2):
                        room(("Tc", q))
                        for g in (2 * q, 2 * q + 1):
                            for tb in range(2):
                                c = ((g % 2) * 2 + tb) * P
                                x = (g * 2 + tb) * 4
                                mm = pe.transpose(bank(("Tc", q))[:, c:c + P],
                                                  cmp_p[:, x:x + 4, :].rearrange("p a b -> p (a b)"), ident)
                        mm.then_inc(*is_full(("Tc", q)))
                    pe.wait_ge(*read(("Tc", 0)))
                    pe.wait_ge(*read(("Tc", 1)))
                if 0 <= t - 3:
                    values2(t - 3)
            def heads2(q):
                for j in range(4 * q + 2, 4 * q + 4):
                    pe.wait_ge(*read(("O2", j)))

            chunked(first["o2"], 2, KD, lambda c, tb: ("y", "nsa", tb, c), tail=True, waits=heads2,
                    ahead=lambda: turn_st("ln4", res, 0, 0))
            swiglu(4, "ln4", res)

        @block.scalar
        def _(act):
            nxt = [0]
            chain = [0]

            def link(ins):
                chain[0] += 1
                ins.then_inc(act_step, 1)
                act.wait_ge(act_step, chain[0])

            def split(u, s, q, n=UNIT):
                act.wait_ge(raw_loaded[s], 32 * (q + 1))
                if not isinstance(u, int) or u >= RING:
                    act.wait_ge(w_used, u - 2)
                act.copy(whi[:, s, 0:n], raw[:, s, 0:n]).then_inc(whi_ready, 1)

            def upto(u):
                while nxt[0] <= min(u, UNITS - 1):
                    n = nxt[0]
                    split(*at(n), unit_len[n])
                    nxt[0] += 1

            def beside(u):
                upto(u + 2)

            def st_out(name, tb, tiles=KD, k0=0):
                for q in range(tiles // 4):
                    key = ("st", name, tb, q)
                    act.wait_ge(*full(key))
                    act.copy(st_hi[:, k0 + 4 * q:k0 + 4 * q + 4, tb * P:tb * P + P],
                             bank(key).rearrange("p (k t) -> p k t", k=4)).then_inc(hi_rounded, 1)

            def square(name, src, tb, junk):
                c = SQ[name, tb]
                act.activation(junk, src, ACT.Square, accum_out=sumsq[:, c:c + 1]).then_inc(sumsq_ready, 1)

            warmed = [0]

            def warm_up(func):
                act.wait_ge(zeros_ready, 1)
                act.activation(warm[:, warmed[0]:warmed[0] + 1], minus_half[:, :], func)
                warmed[0] += 1

            for tb in range(2):
                act.wait_ge(x_loaded[tb], 16)
                square("mix", res[:, tb, :], tb, tmp[:, tb, :])
            st_out("mix", 0)
            upto(0)
            upto(1)
            st_out("mix", 1)
            warm_up(ACT.Sigmoid)
            upto(2)

            def gate_out(c):
                for tb in range(2):
                    act.wait_ge(*full(("gate", c, tb)))
                    act.activation(gate[:, c // 2, tb, 512 * (c % 2):512 * (c % 2) + 512], bank(("gate", c, tb)),
                                   ACT.Sigmoid).then_inc(*is_read(("gate", c, tb)))

            gate_out(0)
            act.wait_ge(*full("rows"))
            act.copy(gb[:, 0, 0:512], bank("rows")).then_inc(*is_read("rows"))
            act.wait_ge(*read("rows"))
            act.dma_start(bias_rows[:, :], gb[:, 0, 0:512]).then_inc(rows_stored, 16)
            u = first["kidx"]
            beside(u)
            act.wait_ge(*full("kidx"))
            act.wait_ge(zeros_ready, 1)
            link(act.copy(kidx[0:64, 0, :], bank("kidx")[0:64, 0:S]))
            act.copy(kidx[64:128, 1, :], bank("kidx")[0:64, 0:S]).then_inc(*is_read("kidx"))
            act.wait_ge(*full("widx"))
            act.mul(widx[:, :, :], bank("widx")[:, 0:8].rearrange("p (a b) -> p a b", a=2),
                    1.0 / 16).then_inc(*is_read("widx"))
            beside(first["qidx"])
            beside(first["kv"])
            act.wait_ge(*full("kv"))
            link(act.copy(k1[:, :], bank("kv")[:, 0:S]))
            act.copy(v1[:, :, :].rearrange("p a b -> p (a b)"), bank("kv")[:, S:2 * S]).then_inc(*is_read("kv"))
            for j in range(4):
                beside(first["q"] + j)
                act.wait_ge(*full(("q", j)))
                act.mul(q1[:, 2 * j:2 * j + 2, :].rearrange("p a b -> p (a b)"), bank(("q", j)),
                        float(P) ** -0.5).then_inc(*is_read(("q", j)))
            def bias_out(key, dst):
                act.wait_ge(*full(key))
                act.copy(dst, bank(key).rearrange("p (a b) -> p a b", a=2)).then_inc(*is_read(key))

            for j in range(2):
                bias_out(("rev1", j), bias1[:, 2 * j:2 * j + 2, P:384])
            for j in range(2):
                beside(first["u"] + j)
                act.wait_ge(*full(("u", j)))
                act.copy(upad[:, 2 * j:2 * j + 2, 16:272],
                         bank(("u", j)).rearrange("p (a b) -> p a b", a=2)).then_inc(*is_read(("u", j)))
            for j in range(2, 4):
                bias_out(("rev1", j), bias1[:, 2 * j:2 * j + 2, P:384])
            for c in range(3):
                beside(first["gate"] + 2 * c)
                beside(first["gate"] + 2 * c + 1)
                gate_out(1 + c)
                if c == 1:
                    for j in range(2):
                        act.wait_ge(*full(("pool", j)))
                        for g in (2 * j, 2 * j + 1):
                            mm = act.mul(st_hi[:, 8 + g, :], bank(("pool", j))[:, (g % 2) * S:(g % 2 + 1) * S],
                                         vec[:, V_PSCALE + g:V_PSCALE + g + 1])
                        mm.then_inc(hi_rounded, 1)
            warm_up(ACT.Exp)
            beside(first["pp"])
            beside(first["pp"] + 1)

            for t in range(HEADS1 + 4):
                h = t - 4
                if 0 <= h < HEADS1:
                    act.wait_ge(*full(("O1", h)))
                    act.copy(st_hi[:, h, :], bank(("O1", h))[:, 0:S]).then_inc(hi_rounded, 1)
                if t < HEADS1:
                    b = t % 3
                    act.wait_ge(max_ready, ATT0["self"] + t + 1)
                    act.activation(prob1[:, b, 0:P], prob1[:, b, 0:P], ACT.Exp, bias=negmax[:, b, 0:1],
                                   accum_out=rowsum[:, b, 0:1])
                    act.activation(prob1[:, b, P:384], prob1[:, b, P:384], ACT.Exp, bias=negmax[:, b, 1:2],
                                   accum_out=rowsum[:, b, 1:2]).then_inc(exp_ready, 1)
                h = t - 2
                if 0 <= h < HEADS1:
                    act.wait_ge(*full(("T1", h)))
                    act.copy(probT1[:, h % 2, :], bank(("T1", h))[:, 0:384]).then_inc(*is_read(("T1", h)))
            beside(first["pa"])
            beside(first["pa"] + 1)
            act.wait_ge(memx_loaded, 16)
            for tb in range(2):
                square("mem", memx[:, tb, :], tb, carve(11648, D) if tb == 0 else carve(12672, D))
            last = first["out"] - 1
            upto(last + 2)
            st_out("merged", 0)
            upto(last + 3)
            st_out("merged", 1)
            beside(last + 2)
            for tb in range(2):
                st_out("mem", tb, k0=8)
            last = first["km"] - 1
            upto(last + 1)

            def square_y(n, name, tb):
                for h in range(2):
                    act.wait_ge(*full(("y", n, tb, h)))
                square(name, ps[:, 2 * tb:2 * tb + 2, :], tb, tmp[:, tb, :].rearrange("p (a b) -> p a b", a=2))

            def square_res(n, name, tb):
                for h in range(2):
                    act.wait_ge(res_ready, RES[n] + 2 * tb + h + 1)
                square(name, res[:, tb, :], tb, tmp[:, tb, :])

            square_y("mix", "ymix", 0)
            upto(last + 2)
            square_res("mix", "memq", 0)
            square_y("mix", "ymix", 1)
            beside(first["km"])
            act.wait_ge(*full(("km", 0)))
            act.copy(km[:, 0:2, :].rearrange("p a b -> p (a b)"), bank(("km", 0))).then_inc(*is_read(("km", 0)))
            square_res("mix", "memq", 1)
            beside(first["km"] + 1)
            act.wait_ge(*full(("km", 1)))
            act.copy(km[:, 2:4, :].rearrange("p a b -> p (a b)"), bank(("km", 1))).then_inc(*is_read(("km", 1)))
            beside(first["vm"])
            beside(first["vm"] + 1)
            for tb in range(2):
                act.wait_ge(*full(("vm", tb)))
                act.copy(vm[:, tb, :], bank(("vm", tb))).then_inc(*is_read(("vm", tb)))
            for tb in range(2):
                st_out("memq", tb)
            for j in range(2):
                beside(first["qm"] + j)
                act.wait_ge(*full(("qm", j)))
                act.mul(qm[:, 2 * j:2 * j + 2, :].rearrange("p a b -> p (a b)"), bank(("qm", j)),
                        float(P) ** -0.5).then_inc(*is_read(("qm", j)))
            for t in range(4 + 4):
                h = t - 4
                if 0 <= h < 4:
                    act.wait_ge(*full(("Om", h)))
                    act.copy(st_hi[:, 8 + h, :], bank(("Om", h))[:, 0:S]).then_inc(hi_rounded, 1)
                if t < 4:
                    b = t % 3
                    act.wait_ge(max_ready, ATT0["mem"] + t + 1)
                    for tb in range(2):
                        mm = act.activation(probm[:, b, tb * S:tb * S + S], bank(("Lm", t))[:, tb * S:tb * S + S],
                                            ACT.Exp, bias=negmax[:, b, tb:tb + 1], accum_out=rowsum[:, b, tb:tb + 1])
                    mm.then_inc(*is_read(("Lm", t)))
                h = t - 2
                if 0 <= h < 4:
                    act.wait_ge(*full(("Tm", h)))
                    act.copy(probTm[:, h % 2, :], bank(("Tm", h))).then_inc(*is_read(("Tm", h)))
            last = first["om"] + 1
            upto(last + 1)
            square_y("mem", "ymem", 0)
            square_res("mem", "ffn0", 0)
            upto(last + 2)

            def swiglu(n, name=None, between=None):
                u0 = first["ffn", n]

                def gate_out(i, blocks=(0, 1)):
                    for tb in blocks:
                        if tb == 0:
                            act.wait_ge(*full(("up", n, 0), i))
                        elif isinstance(i, int) and i == 0:
                            act.wait_ge(*full(("up", n, 1)))
                        else:
                            act.wait_ge(w_used, u0 + 1 + 3 * i)
                        act.activation(silu[:, tb, :], bank(("up", n, tb))[:, 0:FC], ACT.Silu).then_inc(silu_ready, 1)

                def hidden_last(tb):
                    key = ("hid_last", n, tb)
                    act.wait_ge(*full(key))
                    act.copy(st_hi[:, 8:10, tb * P:tb * P + P],
                             bank(key)[:, 0:2 * P].rearrange("p (f t) -> p f t", f=2)).then_inc(hi_rounded, 1)

                def hidden_out(i):
                    act.wait_ge(*full(("hid", n), i))
                    act.copy(hid_hi[:, :, :].rearrange("p a b -> p (a b)"), bank(("hid", n))).then_inc(hi_rounded, 1)

                upto(u0 + 1)
                if name is not None:
                    st_out(name, 0)
                    if between is not None:
                        between()
                upto(u0 + 2)
                if name is not None:
                    st_out(name, 1)
                warm_up(ACT.Silu)
                gate_out(0, (0,))
                upto(u0 + 3)
                gate_out(0, (1,))
                hidden_out(0)
                with act.Fori(1, FSTEPS - 1) as i:
                    split(*at(u0 + 4, i - 1))
                    split(*at(u0 + 5, i - 1))
                    gate_out(i)
                    split(*at(u0 + 6, i - 1))
                    hidden_out(i)
                nxt[0] = u0 + 3 * FSTEPS - 2
                last = u0 + 3 * FSTEPS - 1
                upto(last)
                gate_out(FSTEPS - 1)
                hidden_last(0)
                upto(last + 1)
                hidden_last(1)

            def second_block():
                square_y("mem", "ymem", 1)
                square_res("mem", "ffn0", 1)

            swiglu(0, "ffn0", second_block)
            last = first["ffn", 1] - 1
            square_y(("ffn", 0), "yffn0", 0)
            upto(last + 2)
            swiglu(1, "b2", lambda: square_y(("ffn", 0), "yffn0", 1))
            last = first["sgv"] - 1
            warm_up(ACT.Gelu)
            upto(last + 2)
            st_out("ln0", 0)
            upto(last + 3)
            st_out("ln0", 1)
            for j in range(2):
                act.wait_ge(*full(("wsT", j)))
                act.copy(wsT[:, 4 * j:4 * j + 4, :].rearrange("p a b -> p (a b)"),
                         bank(("wsT", j))).then_inc(*is_read(("wsT", j)))
            for part, z in (("sgv", zv), ("sgu", zu)):
                for c in range(4):
                    beside(first[part] + 2 * c)
                    beside(first[part] + 2 * c + 1)
                    for tb in range(2):
                        act.wait_ge(*full((part, c, tb)))
                        act.activation(z[:, tb, 512 * c:512 * c + 512], bank((part, c, tb)),
                                       ACT.Gelu).then_inc(*is_read((part, c, tb)))
            for tb in range(2):
                st_out("um", tb, 16)
            for k in range(8):
                beside(first["sgo"] + k)
            swiglu(2, "ln1")
            last = first["v2"] - 1
            upto(last + 2)
            st_out("ln2", 0)
            upto(last + 3)
            st_out("ln2", 1)

            def kv_out(name):
                br = int(name[-1] == "w")
                act.wait_ge(*full(name))
                dst = (k2 if name[0] == "k" else v2)[:, :, br, :]
                act.copy(dst, bank(name).rearrange("p (a b) -> p a b", a=2)).then_inc(*is_read(name))

            for name in ("v2", "v2w"):
                beside(first[name])
                kv_out(name)

            def cmp_in(slot):
                key = ("cin", slot)
                act.wait_ge(*full(key))
                src = bank(key).rearrange("p (a m r) -> p a m r", a=2, r=2)
                for half in range(2):
                    for par in range(2):
                        mm = act.copy(cmp_e[64 * par:64 * par + 64, half::2, :], src[64 * half:64 * half + 64, :, :, par])
                        if (half, par) != (1, 1):
                            link(mm)
                mm.then_inc(*is_read(key))

            def cmp_round(slot):
                act.wait_ge(cmp_f_ready, 2 * slot + 1)
                fh = st_hi[:, 8:12, :].rearrange("p a b -> p (a b)")[:, 0:960]
                act.copy(fh, cmp_f[:, :, :].rearrange("p a b -> p (a b)")).then_inc(hi_rounded, 1)

            def cmp_hidden(slot):
                key = ("cg", slot)
                act.wait_ge(*full(key))
                act.copy(cmp_x[0:60, slot, :], bank(key)[0:60, 0:256]).then_inc(*is_read(key))

            def cmp_gelu(slot):
                key = ("cgT", slot)
                act.wait_ge(*full(key))
                act.wait_ge(zeros_ready, 2)
                for f in range(2):
                    mm = act.activation(cmp_g[:, f, :, 0:NCMP],
                                        bank(key)[:, 64 * f:64 * f + 60].rearrange("p (g n) -> p g n", g=4),
                                        ACT.Gelu, bias=vec[:, V_B1 + 2 * slot + f:V_B1 + 2 * slot + f + 1])
                mm.then_inc(*is_read(key))

            beside(first["cin", 0])
            cmp_in(0)
            cmp_round(0)
            for j in range(4):
                bias_out(("rev2", j), bias2[:, 2 * j:2 * j + 2, :])
            beside(first["cw1", 0])
            beside(first["cw1", 0] + 1)
            warm_up(ACT.Gelu)
            cmp_hidden(0)
            beside(first["cin", 1])
            cmp_in(1)
            cmp_gelu(0)
            cmp_round(1)
            for j in range(4, 8):
                bias_out(("rev2", j), bias2[:, 2 * j:2 * j + 2, :])
            act.wait_ge(*full("kc"))
            act.copy(kc[:, :, :].rearrange("p a b -> p (a b)"), bank("kc")[:, 0:P]).then_inc(*is_read("kc"))
            beside(first["cw1", 1])
            beside(first["cw1", 1] + 1)
            cmp_hidden(1)
            swiglu(3)
            warm_up(ACT.Gelu)
            beside(first["k2"])
            kv_out("k2")
            cmp_gelu(1)
            beside(first["k2w"])
            kv_out("k2w")
            st_out("ln3", 0, k0=8)
            st_out("ln3", 1, k0=8)
            warm_up(ACT.Sigmoid)

            act.wait_ge(zeros_ready, 3)
            for j in range(4):
                beside(first["q2"] + j)
                act.wait_ge(*full(("q2", j)))
                src = bank(("q2", j))
                r = 64 * (j % 2)
                for k in range(4):
                    mm = act.mul(q2[r:r + 64, 4 * j + k, :],
                                 src[64 * (k % 2):64 * (k % 2) + 64, (k // 2) * S:(k // 2 + 1) * S], 0.125)
                    if k < 3:
                        link(mm)
                mm.then_inc(*is_read(("q2", j)))
            beside(first["g2"])
            act.wait_ge(*full("g2"))
            act.activation(gate2[:, :, :].rearrange("p a b -> p (a b)"), bank("g2")[:, 0:96],
                           ACT.Sigmoid).then_inc(*is_read("g2"))
            warm_up(ACT.Exp)

            def exp2(h):
                b = h % 3
                act.wait_ge(max_ready, ATT0["nsa"] + h + 1)
                for x in range(4):
                    lo = (0, P, S, 2 * S)[x]
                    n = (P, P, S, S)[x]
                    mm = act.activation(prob2[:, b, lo:lo + n], prob2[:, b, lo:lo + n], ACT.Exp,
                                        bias=negmax[:, b, x:x + 1], accum_out=rowsum[:, b, x:x + 1])
                mm.then_inc(exp_ready, 1)

            exp2(0)
            exp2(1)
            for t in range(2, HEADS2 + 4):
                h = t - 4
                if h >= 0 and h % 2:
                    act.wait_ge(*full(("O2", h // 2)))
                    act.copy(st_hi[:, h // 2, :], bank(("O2", h // 2))[:, 0:S]).then_inc(hi_rounded, 1)
                if t < HEADS2:
                    exp2(t)
                h = t - 2
                if h < HEADS2:
                    act.wait_ge(*full(("T2", h, 0)))
                    act.copy(probT2[:, h % 2, 0:512], bank(("T2", h, 0))).then_inc(*is_read(("T2", h, 0)))
                if t == 2:
                    act.wait_ge(cmp_exp_in, 1)
                    act.activation(cmp_p[:, :, 0:16], cmp_p[:, :, 0:16], ACT.Exp).then_inc(cmp_exp_out, 1)
                if t == 3:
                    for q in range(2):
                        act.wait_ge(*full(("Tc", q)))
                        act.copy(cmp_pT[:, 2 * q:2 * q + 2, :].rearrange("p a b -> p (a b)"),
                                 bank(("Tc", q))).then_inc(*is_read(("Tc", q)))
            for k in range(4):
                beside(first["o2"] + k)
            swiglu(4, "ln4")

        @block.vector
        def _(dve):
            nxt = [0]
            chain = [0]

            def link(ins):
                chain[0] += 1
                ins.then_inc(dve_step, 1)
                dve.wait_ge(dve_step, chain[0])

            def split(u, s, q, n=UNIT):
                dve.wait_ge(whi_ready, u + 1)
                if isinstance(u, int) and u - 1 in BY_POOL:
                    dve.wait_ge(wlo_ready, u)
                dve.tensor_tensor(wlo[:, s, 0:n], raw[:, s, 0:n], whi[:, s, 0:n].bitcast(F32),
                                  ALU.subtract).then_inc(wlo_ready, 1)

            def upto(u):
                while nxt[0] <= min(u, UNITS - 1):
                    n = nxt[0]
                    if n not in BY_POOL:
                        split(*at(n), unit_len[n])
                    nxt[0] += 1

            def beside(u):
                upto(u + 2)

            def st_out(name, tb, tiles=KD, k0=0):
                for q in range(tiles // 4):
                    key = ("st", name, tb, q)
                    dve.wait_ge(hi_rounded, split_no[key] + 1)
                    hi, lo = (x[:, k0 + 4 * q:k0 + 4 * q + 4, tb * P:tb * P + P] for x in (st_hi, st_lo))
                    dve.tensor_tensor(lo, bank(key).rearrange("p (k t) -> p k t", k=4), hi.bitcast(F32),
                                      ALU.subtract).then_inc(*is_read(key))

            def root(name, tb):
                c = RS[name, tb]
                dve.wait_ge(rstd_ready, c + 1)
                return rstd[:, c:c + 1]

            def halves(x, tb):
                return [(h, x[:, tb, 512 * h:512 * h + 512]) for h in range(2)]

            def pre_norm(name, src, dst, tb):
                dve.wait_ge(gb_loaded[1], GB1[name])
                y = root(name, tb)
                for (h, a), (_, o) in zip(halves(src, tb), halves(dst, tb)):
                    dve.scalar_tensor_tensor(o, a, y, gb[:, 1, 512 * h:512 * h + 512], ALU.mult,
                                             ALU.mult).then_inc(xn_ready, 1)

            def post_norm_rms(n, name, tb):
                dve.wait_ge(gb_loaded[0], GB0[n])
                y = root(name, tb)
                for h, t in halves(tmp, tb):
                    key = ("y", n, tb, h)
                    dve.scalar_tensor_tensor(t, bank(key), y, gb[:, 0, 512 * h:512 * h + 512], ALU.mult,
                                             ALU.mult).then_inc(*is_read(key))
                for (h, t), (_, r) in zip(halves(tmp, tb), halves(res, tb)):
                    dve.wait_ge(*read(("y", n, tb, h)))
                    dve.tensor_tensor(r, r, t, ALU.add).then_inc(res_ready, 1)

            def variance(name, tb, parts, eps):
                c = RS[name, tb]
                link(dve.bn_aggr(mv[:, tb, :], stats[:, tb, 0:6 * parts]))
                dve.tensor_scalar(meansq[:, c:c + 1], mv[:, tb, 1:2], eps, None, ALU.add).then_inc(var_ready, 1)

            def sum_out(n, tb, h, halved):
                f = 2.0 if halved else 1.0
                key = ("y", n, tb, h)
                dve.wait_ge(*full(key))
                part = tmp[:, tb, 512 * h:512 * h + 512]
                dve.scalar_tensor_tensor(part, res[:, tb, 512 * h:512 * h + 512], f * ALPHA, bank(key),
                                         ALU.mult, ALU.add).then_inc(*is_read(key))
                dve.wait_ge(*read(key))
                link(dve.bn_stats(stats[:, tb, 6 * h:6 * h + 6], part))

            def norm_out(n, tb):
                for r in range(2):
                    dve.wait_ge(gb_loaded[r], (GB0, GB1)[r][n])
                for h, t in halves(tmp, tb):
                    link(dve.scalar_tensor_tensor(t, t, mv[:, tb, 0:1], gb[:, 0, 512 * h:512 * h + 512],
                                                  ALU.subtract, ALU.mult))
                y = root(n, tb)
                for (h, t), (_, r) in zip(halves(tmp, tb), halves(res, tb)):
                    dve.scalar_tensor_tensor(r, t, y, gb[:, 1, 512 * h:512 * h + 512], ALU.mult,
                                             ALU.add).then_inc(res_ready, 1)

            def post_norm_ln(n, name, halved, early=False):
                eps = EPS2 * (4.0 if halved else 1.0)
                if not early:
                    sum_out(n, 0, 0, halved)
                sum_out(n, 0, 1, halved)
                variance(n, 0, 2, eps)
                norm_out(n, 0)
                if name is None:
                    sum_out(n, 1, 0, halved)
                else:
                    if not early:
                        sum_out(n, 1, 0, halved)
                    st_out(name, 0)
                sum_out(n, 1, 1, halved)
                variance(n, 1, 2, eps)
                norm_out(n, 1)
                if name is not None:
                    st_out(name, 1)

            for tb in range(2):
                dve.wait_ge(x_loaded[tb], 16)
                pre_norm("mix", res, tmp, tb)
            st_out("mix", 0)
            upto(0)
            upto(1)
            st_out("mix", 1)
            upto(2)
            dve.wait_ge(const_loaded, 32)
            beside(first["kidx"])
            beside(first["qidx"])
            dve.wait_ge(*full("qidx"))
            dve.tensor_copy(qidx[:, :, :].rearrange("p a b -> p (a b)"), bank("qidx")).then_inc(*is_read("qidx"))
            beside(first["kv"])
            dve.wait_ge(*read("widx"))
            for tb in range(2):
                n = P * (tb + 1)
                acc = score[:, 0:P] if tb == 0 else score[:, P:384]
                for h in range(4):
                    key = ("dots", 0 if tb == 0 else 1 + h // 2)
                    c = S * (h // 2) + P * (h % 2) if tb == 0 else S * (h % 2)
                    if h == 0 or (tb and h == 2):
                        dve.wait_ge(*full(key))
                    mm = dve.tensor_scalar(relu_w[:, 0:n], bank(key)[:, c:c + n], 0.0, widx[:, tb, h:h + 1],
                                           ALU.max, ALU.mult)
                    if h == 3 or (tb and h == 1):
                        mm.then_inc(*is_read(key))
                        dve.wait_ge(*read(key))
                    else:
                        link(mm)
                    other = con[:, K_TRI + P:K_TRI + 2 * P] if tb == 0 else con[:, K_TRI:K_TRI + 2 * P]
                    link(dve.tensor_tensor(acc, relu_w[:, 0:n], other if h == 0 else acc, ALU.add))

            def top_round(r):
                if r < TOPK // 4:
                    acc = score[:, 0:P] if r < TOPK // 8 else score[:, P:384]
                    link(dve.max(top8[:, :], acc))
                    link(dve.match_replace(acc, top8[:, :], acc, TAKEN))
                if r == TOPK // 4:
                    dve.tensor_scalar(selmask[:, :], score[:, :], TAKEN / 1.5, BIG_NEG, ALU.is_gt,
                                      ALU.mult).then_inc(selected, 1)

            def pool_out():
                for j in range(2):
                    key = ("pool", j)
                    dve.wait_ge(hi_rounded, split_no[key] + 1)
                    for g in (2 * j, 2 * j + 1):
                        mm = dve.scalar_tensor_tensor(st_lo[:, 8 + g, :], bank(key)[:, (g % 2) * S:(g % 2 + 1) * S],
                                                      vec[:, V_PSCALE + g:V_PSCALE + g + 1],
                                                      st_hi[:, 8 + g, :].bitcast(F32), ALU.mult, ALU.subtract)
                    mm.then_inc(*is_read(key))

            r = 0
            for name, n in (("q", 4), ("u", 2), ("gate", 6)):
                for j in range(n):
                    beside(first[name] + j)
                    for _ in range(2 if name == "q" else 3):
                        top_round(r)
                        r += 1
                    if (name, j) == ("gate", 3):
                        pool_out()
            for c in range(2):
                beside(first["pp"] + c)
                for tb in range(2):
                    dve.wait_ge(*full(("pp", c, tb)))
                    g = gate[:, 0, tb, 512 * c:512 * c + 512]
                    dve.wait_ge(*read(("gate", c, tb)))
                    dve.tensor_tensor(g, bank(("pp", c, tb)), g, ALU.mult).then_inc(*is_read(("pp", c, tb)))

            def normalize(b, segments):
                link(dve.reciprocal(factor[:, b, 0:len(segments)], rowsum[:, b, 0:len(segments)]))
                for x, seg in enumerate(segments):
                    mm = dve.tensor_scalar(seg, seg, factor[:, b, x:x + 1], None, ALU.mult)
                    if x < len(segments) - 1:
                        link(mm)
                mm.then_inc(prob_ready, 1)

            dve.wait_ge(bias_masked, 1)
            for t in range(HEADS1 + 4):
                if t < HEADS1:
                    b = t % 3
                    dve.wait_ge(*full(("L1", t)))
                    L = bank(("L1", t))
                    if t >= 3:
                        dve.wait_ge(*full(("T1", t - 3)))
                    link(dve.tensor_tensor_reduce(prob1[:, b, 0:P], L[:, 0:P], bias1[:, t, 0:P], 1.0, -3e38,
                                                  ALU.add, ALU.max, rowmax[:, b, 0:1]))
                    dve.tensor_tensor_reduce(prob1[:, b, P:384], L[:, P:384], bias1[:, t, P:384], 1.0, -3e38,
                                             ALU.add, ALU.max, rowmax[:, b, 1:2]).then_inc(*is_read(("L1", t)))
                    dve.wait_ge(*read(("L1", t)))
                    dve.tensor_scalar(negmax[:, b, 0:2], rowmax[:, b, 0:2], -1.0, None,
                                      ALU.mult).then_inc(max_ready, 1)
                h = t - 1
                if 0 <= h < HEADS1:
                    b = h % 3
                    dve.wait_ge(exp_ready, h + 1)
                    normalize(b, [prob1[:, b, 0:P], prob1[:, b, P:384]])
                h = t - 4
                if 0 <= h < HEADS1:
                    dve.wait_ge(hi_rounded, split_no["O1", h] + 1)
                    dve.tensor_tensor(st_lo[:, h, :], bank(("O1", h))[:, 0:S], st_hi[:, h, :].bitcast(F32),
                                      ALU.subtract).then_inc(*is_read(("O1", h)))
            def merge(c, tb):
                dve.wait_ge(*full(("pa", c, tb)))
                dve.wait_ge(*read(("gate", 2 + c, tb)))
                dve.wait_ge(*read(("gate", c, tb)))
                g = gate[:, 1, tb, 512 * c:512 * c + 512]
                dve.tensor_tensor(g, bank(("pa", c, tb)), g, ALU.mult).then_inc(*is_read(("pa", c, tb)))
                dve.wait_ge(*read(("pa", c, tb)))
                dve.wait_ge(*read(("pp", c, tb)))
                dve.tensor_tensor(tmp[:, tb, 512 * c:512 * c + 512], gate[:, 0, tb, 512 * c:512 * c + 512],
                                  g, ALU.add).then_inc(xn_ready, 1)

            beside(first["pa"])
            beside(first["pa"] + 1)
            dve.wait_ge(memx_loaded, 16)
            for tb in range(2):
                pre_norm("mem", memx, memx, tb)
            merge(0, 0)
            merge(0, 1)
            last = first["out"] - 1
            upto(last + 1)
            merge(1, 0)
            st_out("merged", 0)
            upto(last + 2)
            merge(1, 1)
            st_out("merged", 1)
            upto(last + 3)
            beside(last + 2)
            for tb in range(2):
                st_out("mem", tb, k0=8)
            last = first["km"] - 1
            upto(last + 1)
            post_norm_rms("mix", "ymix", 0)
            upto(last + 2)
            pre_norm("memq", res, tmp, 0)
            post_norm_rms("mix", "ymix", 1)
            beside(first["km"])
            pre_norm("memq", res, tmp, 1)
            beside(first["km"] + 1)
            beside(first["vm"])
            beside(first["vm"] + 1)
            for tb in range(2):
                st_out("memq", tb)
            beside(first["qm"])
            beside(first["qm"] + 1)
            for t in range(4 + 4):
                if t < 4:
                    b = t % 3
                    dve.wait_ge(*full(("Lm", t)))
                    link(dve.tensor_reduce(rowmax[:, b, 0:2], bank(("Lm", t)).rearrange("p (a b) -> p a b", a=2),
                                           AX_X, ALU.max))
                    dve.tensor_scalar(negmax[:, b, 0:2], rowmax[:, b, 0:2], -1.0, None,
                                      ALU.mult).then_inc(max_ready, 1)
                h = t - 1
                if 0 <= h < 4:
                    b = h % 3
                    dve.wait_ge(*read(("Lm", h)))
                    link(dve.reciprocal(factor[:, b, 0:2], rowsum[:, b, 0:2]))
                    link(dve.tensor_scalar(probm[:, b, 0:S], probm[:, b, 0:S], factor[:, b, 0:1], None, ALU.mult))
                    dve.tensor_scalar(probm[:, b, S:512], probm[:, b, S:512], factor[:, b, 1:2], None,
                                      ALU.mult).then_inc(prob_ready, 1)
                h = t - 4
                if 0 <= h < 4:
                    dve.wait_ge(hi_rounded, split_no["Om", h] + 1)
                    dve.tensor_tensor(st_lo[:, 8 + h, :], bank(("Om", h))[:, 0:S], st_hi[:, 8 + h, :].bitcast(F32),
                                      ALU.subtract).then_inc(*is_read(("Om", h)))
            last = first["om"] + 1
            upto(last + 1)
            post_norm_rms("mem", "ymem", 0)
            pre_norm("ffn0", res, tmp, 0)
            st_out("ffn0", 0)
            upto(last + 2)
            post_norm_rms("mem", "ymem", 1)
            pre_norm("ffn0", res, tmp, 1)
            st_out("ffn0", 1)

            def swiglu(n):
                u0 = first["ffn", n]

                def hidden_in(i):
                    for tb in range(2):
                        dve.wait_ge(silu_ready, 2 * FSTEPS * n + tb + 1 + 2 * i)
                        dve.tensor_tensor(hidden[:, tb, :], bank(("up", n, tb))[:, FC:2 * FC], silu[:, tb, :],
                                          ALU.mult).then_inc(*is_read(("up", n, tb)))

                def hidden_last(tb):
                    key = ("hid_last", n, tb)
                    dve.wait_ge(hi_rounded, split_no[key] + 1)
                    hi, lo = (x[:, 8:10, tb * P:tb * P + P] for x in (st_hi, st_lo))
                    dve.tensor_tensor(lo, bank(key)[:, 0:2 * P].rearrange("p (f t) -> p f t", f=2), hi.bitcast(F32),
                                      ALU.subtract).then_inc(*is_read(key))

                def hidden_out(i):
                    dve.wait_ge(hi_rounded, split_no["hid", n] + 1 + i)
                    dve.tensor_tensor(hid_lo[:, :, :].rearrange("p a b -> p (a b)"), bank(("hid", n)),
                                      hid_hi[:, :, :].rearrange("p a b -> p (a b)").bitcast(F32),
                                      ALU.subtract).then_inc(*is_read(("hid", n)))

                upto(u0 + 2)
                hidden_in(0)
                upto(u0 + 3)
                hidden_out(0)
                with dve.Fori(1, FSTEPS - 1) as i:
                    split(*at(u0 + 4, i - 1))
                    split(*at(u0 + 5, i - 1))
                    hidden_in(i)
                    split(*at(u0 + 6, i - 1))
                    hidden_out(i)
                nxt[0] = u0 + 3 * FSTEPS - 2
                last = u0 + 3 * FSTEPS - 1
                upto(last)
                hidden_in(FSTEPS - 1)
                hidden_last(0)
                upto(last + 1)
                hidden_last(1)

            swiglu(0)
            last = first["ffn", 1] - 1
            post_norm_rms(("ffn", 0), "yffn0", 0)
            st_out("b2", 0)
            upto(last + 2)
            post_norm_rms(("ffn", 0), "yffn0", 1)
            st_out("b2", 1)
            swiglu(1)
            post_norm_ln(("ffn", 1), "ln0", True)
            for c in range(4):
                beside(first["sgv"] + 2 * c)
                beside(first["sgv"] + 2 * c + 1)
                for tb in range(2):
                    dve.wait_ge(*read(("sgv", c, tb)))
                    link(dve.bn_stats(stats[:, tb, 6 * c:6 * c + 6], zv[:, tb, 512 * c:512 * c + 512]))
            for tb in range(2):
                variance("zv", tb, 4, EPS2)
            for tb in range(2):
                y = root("zv", tb)
                dve.tensor_scalar(zv[:, tb, :], zv[:, tb, :], mv[:, tb, 0:1], y, ALU.subtract,
                                  ALU.mult).then_inc(zv_normed, 1)
            for k in range(8):
                beside(first["sgu"] + k)
            for tb in range(2):
                for gp in range(4):
                    key = ("mixed", tb, gp)
                    dve.wait_ge(*full(key))
                    if gp == 0:
                        dve.wait_ge(*read(("sgu", 3, tb)))
                    for g in (2 * gp, 2 * gp + 1):
                        z = zu[:, tb, g * S:g * S + S]
                        mm = dve.scalar_tensor_tensor(z, bank(key)[:, (g % 2) * S:(g % 2 + 1) * S],
                                                      vec[:, V_BS + g:V_BS + g + 1], z, ALU.add, ALU.mult)
                        if g % 2 == 0:
                            link(mm)
                    mm.then_inc(*is_read(key))
            for tb in range(2):
                st_out("um", tb, 16)
            for k in range(5):
                beside(first["sgo"] + k)
            for tb in range(2):
                sum_out("sgu", tb, 0, False)
            upto(first["ffn", 2])
            post_norm_ln("sgu", "ln1", False, early=True)
            swiglu(2)
            post_norm_ln(("ffn", 2), "ln2", True)
            beside(first["v2"])
            beside(first["v2w"])

            def cmp_in(slot):
                dve.wait_ge(*read(("cin", slot)))
                e = cmp_e[:, :, :]
                pe_vec = vec[:, V_PE + 16 * slot:V_PE + 16 * slot + 16]
                dve.tensor_tensor(view(cmp_f[:, 0, 0:1], (60, 16), (15, 4), (1, 15)),
                                  view(e[:, 0, 0:1], (1, 16), (P, 4), (8, 15)),
                                  view(pe_vec, (1, 16), (0, 4), (0, 15)), ALU.add).then_inc(cmp_f_ready, 1)
                fh, fl = (x[:, 8:12, :].rearrange("p a b -> p (a b)")[:, 0:960] for x in (st_hi, st_lo))
                dve.wait_ge(hi_rounded, split_no["cf", slot] + 1)
                dve.tensor_tensor(fl, cmp_f[:, :, :].rearrange("p a b -> p (a b)"), fh.bitcast(F32),
                                  ALU.subtract).then_inc(cmp_f_ready, 1)

            for slot in range(2):
                beside(first["cin", slot])
                cmp_in(slot)
                beside(first["cw1", slot])
                beside(first["cw1", slot] + 1)
            swiglu(3)
            post_norm_ln(("ffn", 3), None, True)
            dve.wait_ge(*read(("cgT", 1)))
            for f in range(2):
                mm = dve.tensor_copy(cmp_gr[:, f, :, :].rearrange("p g (j n) -> p g j n", j=4),
                                     view(cmp_g[:, f, 0, 0:1], (32, 4), (0, 4), (1, 32)))
            mm.then_inc(cmp_gr_ready, 1)
            beside(first["k2"])
            st_out("ln3", 0, k0=8)
            st_out("ln3", 1, k0=8)
            beside(first["k2w"])

            for j in range(4):
                beside(first["q2"] + j)
            beside(first["g2"])
            dve.wait_ge(*full("vc"))
            for j in range(4):
                mm = dve.tensor_scalar(vc[:, :, j, :], bank("vc")[:, 0:256].rearrange("p (g d) -> p g d", g=4),
                                       con[:, K_BLK + j:K_BLK + j + 1], None, ALU.mult)
            mm.then_inc(*is_read("vc"))
            for j in range(4, 8):
                dve.wait_ge(*read(("rev2", j)))
            flat = cmp_p[:, :, :]
            link(dve.memset(flat[:, :, 0:16], BIG_NEG))
            link(dve.memset(flat[:, :, 16:32], 0.0))
            def max2(h):
                b = h % 3
                if h >= 3:
                    dve.wait_ge(*full(("T2", h - 3, 1)))
                for tb in range(2):
                    dve.wait_ge(*full(("L2", h, tb)))
                    L = bank(("L2", h, tb))
                    n = P * (tb + 1)
                    for br in range(2):
                        lo = S * tb + n * br
                        mm = dve.tensor_tensor_reduce(prob2[:, b, lo:lo + n], L[:, n * br:n * br + n],
                                                      bias2[:, h, S - n:S], 1.0, -3e38, ALU.add, ALU.max,
                                                      rowmax[:, b, 2 * tb + br:2 * tb + br + 1])
                    mm.then_inc(*is_read(("L2", h, tb)))
                dve.wait_ge(*read(("L2", h, 1)))
                dve.tensor_scalar(negmax[:, b, :], rowmax[:, b, :], -1.0, None, ALU.mult).then_inc(max_ready, 1)

            def normalize2(h):
                b = h % 3
                dve.wait_ge(exp_ready, HEADS1 + h + 1)
                link(dve.reciprocal(factor[:, b, :], rowsum[:, b, :]))
                link(dve.tensor_tensor(factor[:, b, :].rearrange("p (a c) -> p a c", a=2),
                                       factor[:, b, :].rearrange("p (a c) -> p a c", a=2),
                                       gate2[:, :, 3 * h + 1:3 * h + 3], ALU.mult))
                for x in range(4):
                    seg = prob2[:, b, (0, P, S, 2 * S)[x]:(P, S, 2 * S, 3 * S)[x]]
                    mm = dve.tensor_scalar(seg, seg, factor[:, b, x:x + 1], None, ALU.mult)
                mm.then_inc(prob_ready, 1)

            def cmp_exponents():
                dve.wait_ge(*full("Lc"))
                for tb in range(2):
                    n, c0 = ((7, P + 31), (NCMP, 31))[tb]
                    mm = dve.tensor_tensor(view(flat[:, 4 * tb, 0:1], (256, 4), (32, 4), (1, n)),
                                           view(bank("Lc")[:, 64 * tb:64 * tb + 1], (128, 4), (16, 4), (1, n)),
                                           view(bias2[:, 0, c0:c0 + 1], (4 * S, 4), (S, 4), (16, n)), ALU.add)
                    if tb == 0:
                        link(mm)
                mm.then_inc(*is_read("Lc"))
                dve.wait_ge(*read("Lc"))
                link(dve.tensor_reduce(cmp_stat[:, 0, :], flat[:, :, 0:16], AX_X, ALU.max))
                dve.tensor_tensor(flat[:, :, 0:16], flat[:, :, 0:16], view(cmp_stat[:, 0, 0:1], (1, 32), (0, 16)),
                                  ALU.subtract).then_inc(cmp_exp_in, 1)

            def cmp_weights():
                dve.wait_ge(cmp_exp_out, 1)
                link(dve.tensor_reduce(cmp_stat[:, 1, :], flat[:, :, 0:16], AX_X, ALU.add))
                link(dve.reciprocal(cmp_stat[:, 2, :], cmp_stat[:, 1, :]))
                fac = view(cmp_stat[:, 2, 0:1], (8, 4), (4, 2), (1, 4))
                link(dve.tensor_tensor(fac, fac, view(gate2[:, 0, 0:1], (12, 4), (48, 2), (3, 4)), ALU.mult))
                link(dve.tensor_tensor(flat[:, :, 0:16], flat[:, :, 0:16], view(cmp_stat[:, 2, 0:1], (1, 32), (0, 16)),
                                       ALU.mult))
                for tb in range(2):
                    part = view(flat[:, 4 * tb, 0:1], (256, 4), (32, 4), (1, 16))
                    mm = dve.tensor_tensor(part, part, view(con[:, K_CMASK + 16 * tb:K_CMASK + 16 * tb + 1], (0, 4), (0, 4),
                                                            (1, 16)), ALU.mult)
                mm.then_inc(cmp_p_ready, 1)

            dve.wait_ge(*read("g2"))
            max2(0)
            max2(1)
            normalize2(0)
            normalize2(1)
            for t in range(2, HEADS2 + 4):
                if t < HEADS2:
                    max2(t)
                if t == 3:
                    cmp_weights()
                if 2 < t <= HEADS2:
                    normalize2(t - 1)
                h = t - 2
                if h < HEADS2:
                    dve.wait_ge(*full(("T2", h, 1)))
                    dve.tensor_copy(probT2[:, h % 2, 512:768],
                                    bank(("T2", h, 1))[:, 0:S]).then_inc(*is_read(("T2", h, 1)))
                if t == 2:
                    cmp_exponents()
                h = t - 4
                if h >= 0 and h % 2:
                    key = ("O2", h // 2)
                    dve.wait_ge(hi_rounded, split_no[key] + 1)
                    dve.tensor_tensor(st_lo[:, h // 2, :], bank(key)[:, 0:S], st_hi[:, h // 2, :].bitcast(F32),
                                      ALU.subtract).then_inc(*is_read(key))
            beside(first["o2"])
            beside(first["o2"] + 1)
            for tb in range(2):
                sum_out("nsa", tb, 0, False)
            upto(first["ffn", 4])
            post_norm_ln("nsa", "ln4", False, early=True)
            swiglu(4)
            post_norm_ln(("ffn", 4), None, True)

        @block.gpsimd
        def _(pool):
            chain = [0]

            def link(ins):
                chain[0] += 1
                ins.then_inc(pool_step, 1)
                pool.wait_ge(pool_step, chain[0])

            def rms_root(name, tb):
                c = RS[name, tb]
                pool.wait_ge(sumsq_ready, SQ[name, tb] + 1)
                link(pool.tensor_scalar(meansq[:, c:c + 1], sumsq[:, SQ[name, tb]:SQ[name, tb] + 1], 1.0 / D, EPS1,
                                        ALU.mult, ALU.add))
                pool.tensor_tensor(rstd[:, c:c + 1], meansq[:, c:c + 1], minus_half[:, :],
                                   ALU.pow).then_inc(rstd_ready, 1)

            def var_root(name, tb):
                c = RS[name, tb]
                pool.wait_ge(var_ready, VAR[name, tb] + 1)
                pool.tensor_tensor(rstd[:, c:c + 1], meansq[:, c:c + 1], minus_half[:, :],
                                   ALU.pow).then_inc(rstd_ready, 1)

            def split(u):
                s = u % RING
                pool.wait_ge(whi_ready, u + 1)
                pool.wait_ge(wlo_ready, u)
                n = unit_len[u]
                pool.tensor_tensor(wlo[:, s, 0:n], raw[:, s, 0:n], whi[:, s, 0:n].bitcast(F32),
                                   ALU.subtract).then_inc(wlo_ready, 1)

            def norm_done(n):
                pool.wait_ge(res_ready, RES[n] + 4)

            def prenorm_done(name):
                pool.wait_ge(xn_ready, XN[name] + 4)

            def load_row(dst, row, signal):
                pool.dma_start(dst, bass.AP(row.tensor, row.offset, [[0, P], [1, row.shape[-1]]])).then_inc(signal, 16)

            load_row(gb[:, 1, :], A["norm_mix_pre"], gb_loaded[1])
            link(pool.memset(minus_half[:, :], -0.5))
            link(pool.memset(table[:, :], 0.0))
            link(pool.memset(table[32:33, :], BIG_NEG))
            pool.dma_start(table[0:32, 0:HEADS1], A["rel_bias_table"]).then_inc(table_loaded, 16)
            pool.dma_start(table[0:32, HEADS1:HEADS1 + HEADS2], A["rel_table_2"]).then_inc(table_loaded, 16)
            pool.dma_start(poolw[:, :, :], A["pool_w"].rearrange("g c d -> c g d")).then_inc(poolw_loaded, 16)
            pool.memset(kidx[:, :, :], 0.0)
            pool.memset(upad[:, :, 0:16], 0.0).then_inc(zeros_ready, 1)
            for tb in range(2):
                rms_root("mix", tb)
            pool.wait_ge(rows_stored, 16)
            pool.dma_start(shifted1[:, :, :], bass.AP(bias_rows, 0, [[1, P], [512, HEADS1], [1, S]]))\
                .then_inc(bias1_loaded, 16)
            load_row(gb[:, 0, :], A["norm_mix_post"], gb_loaded[0])
            prenorm_done("mix")
            load_row(gb[:, 1, :], A["norm_mem_kv"], gb_loaded[1])

            pool.wait_ge(const_loaded, 32)
            for j in range(2):
                pool.wait_ge(*read(("u", j)))
            link(pool.tensor_tensor(winA[:, :, 1:272], upad[:, :, 1:272], upad[:, :, 0:271], ALU.add))
            link(pool.tensor_tensor(winB[:, 1:4, 3:272], winA[:, 1:4, 3:272], winA[:, 1:4, 1:270], ALU.add))
            link(pool.tensor_tensor(winA[:, 2:4, 7:272], winB[:, 2:4, 7:272], winB[:, 2:4, 3:268], ALU.add))
            link(pool.tensor_tensor(winB[:, 3, 15:272], winA[:, 3, 15:272], winA[:, 3, 7:264], ALU.add))
            for g in range(4):
                win = (winA, winB)[g % 2]
                link(pool.tensor_tensor(win[:, g, 16:32], win[:, g, 16:32],
                                        con[:, K_ICNT + 16 * g:K_ICNT + 16 * g + 16], ALU.mult))
                link(pool.tensor_scalar(win[:, g, 32:272], win[:, g, 32:272], 1.0 / (2 << g), None, ALU.mult))
                mm = pool.tensor_tensor(win[:, g, 16:272], win[:, g, 16:272], upad[:, g, 16:272], ALU.subtract)
                if g < 3:
                    link(mm)
            mm.then_inc(pooled, 1)
            pool.wait_ge(selected, 1)
            for j in range(4):
                pool.wait_ge(*read(("rev1", j)))
            for lo, src, n in ((0, S, P), (P, P, S)):
                mm = pool.tensor_tensor(bias1[:, :, lo:lo + n], bias1[:, :, src:src + n],
                                        view(selmask[:, lo:lo + 1], (0, HEADS1), (1, n)), ALU.add)
                if lo == 0:
                    link(mm)
            mm.then_inc(bias_masked, 1)
            pool.wait_ge(*read(("O1", HEADS1 - 1)))
            pool.dma_start(memx[:, :, :], A["mem"][0].rearrange("(t p) d -> p t d", p=P)).then_inc(memx_loaded, 16)
            for tb in range(2):
                rms_root("mem", tb)
            prenorm_done("mem")
            load_row(gb[:, 1, :], A["norm_mem_pre"], gb_loaded[1])
            for tb in range(2):
                rms_root("ymix", tb)
                rms_root("memq", tb)
            norm_done("mix")
            load_row(gb[:, 0, :], A["norm_mem_post"], gb_loaded[0])
            prenorm_done("memq")
            load_row(gb[:, 1, :], A["norm_ffn_pre"], gb_loaded[1])
            for tb in range(2):
                rms_root("ymem", tb)
                rms_root("ffn0", tb)
            norm_done("mem")
            load_row(gb[:, 0, :], A["norm_ffn_post"], gb_loaded[0])
            prenorm_done("ffn0")
            load_row(gb[:, 1, :], A["ln_b_2"][0, 0], gb_loaded[1])
            load_row(sgu_gb[:, 0, :], A["sgu_ln_g_2"][0], sgu_gb_loaded)
            load_row(sgu_gb[:, 1, :], A["sgu_ln_b_2"][0], sgu_gb_loaded)
            pool.dma_start(ws[:, :, :], A["sgu_w_s_2"][0].rearrange("g t s -> t g s")).then_inc(ws_loaded, 16)
            pool.wait_ge(ws_loaded, 16)
            pool.affine_select(out=ws[:, :, :], in_=ws[:, :, :], compare_op=ALU.is_ge, fill=0.0, base=0,
                               pattern=[[0, 8], [-1, P]], channel_multiplier=1).then_inc(ws_masked, 1)

            def load_norm(i):
                load_row(gb[:, 0, :], A["ln_g_2"][i // 3, i % 3], gb_loaded[0])
                load_row(gb[:, 1, :], A["ln_b_2"][i // 3, i % 3], gb_loaded[1])

            def layer_norm(n, unit):
                split(unit)
                var_root(n, 0)
                split(unit + 1)
                var_root(n, 1)
                norm_done(n)

            for tb in range(2):
                rms_root("yffn0", tb)
            norm_done(("ffn", 0))
            load_row(gb[:, 0, :], A["ln_g_2"][0, 0], gb_loaded[0])
            layer_norm(("ffn", 1), first["sgv"])
            load_norm(1)
            pool.wait_ge(sgu_gb_loaded, 32)
            for tb in range(2):
                var_root("zv", tb)
            for tb in range(2):
                pool.wait_ge(zv_normed, tb + 1)
                link(pool.tensor_tensor(zv[:, tb, :], zv[:, tb, :], sgu_gb[:, 0, :], ALU.mult))
                pool.tensor_tensor(zv[:, tb, :], zv[:, tb, :], sgu_gb[:, 1, :], ALU.add).then_inc(zv_ready, 1)
            pool.wait_ge(*full(("st", "um", 1, 3)))
            pool.dma_start(shifted2[:, :, :], bass.AP(bias_rows, HEADS1 * 512,
                                                      [[1, P], [512, HEADS2], [1, S]])).then_inc(bias2_loaded, 16)
            layer_norm("sgu", first["ffn", 2])
            load_norm(2)
            for slot in range(2):
                for dup in range(2):
                    pool.dma_start(cmp_w2[:, slot, :, 64 * dup:64 * dup + 64],
                                   A["cmp_w2_2"][slot].rearrange("(f p) d -> p f d", p=P)).then_inc(cmp_w2_loaded, 16)
            pool.memset(cmp_g[:, :, :, :], 0.0).then_inc(zeros_ready, 1)
            layer_norm(("ffn", 2), first["v2"])
            load_norm(3)
            pool.wait_ge(*full(("rev2", 7)))
            pool.memset(q2[:, :, :], 0.0).then_inc(zeros_ready, 1)
            layer_norm(("ffn", 3), first["k2"])
            load_norm(4)
            layer_norm("nsa", first["ffn", 4])
            load_norm(5)
            for tb in range(2):
                var_root(("ffn", 4), tb)


_MATRICES = ["x", "mem", "norm_mix_pre", "norm_mem_kv", "norm_mem_pre", "norm_ffn_pre", "norm_mix_post", "w_in", "pool_w", "w_proj_pool", "w_proj_attn", "rel_bias_table",
             "w_out", "norm_mem_post", "w_q_mem", "w_kv_mem", "w_o_mem", "norm_ffn_post", "w_gate_up", "w_down",
             "rel_table_2", "ln_g_2", "ln_b_2", "ffn_w1_2", "ffn_w3_2", "ffn_w2_2", "sgu_w_in_2", "sgu_ln_g_2",
             "sgu_ln_b_2", "sgu_w_s_2", "sgu_w_out_2", "kv_w_2", "cmp_w1_2", "cmp_w2_2", "nsa_w_qg_2", "nsa_w_o_2"]


def _columns(v):
    return np.ascontiguousarray(np.asarray(v).reshape(-1, P).T)


def kernel(**inputs):
    import concourse.bacc as _bacc
    from concourse.bass_utils import run_bass_kernel_spmd as _run

    nc = _bacc.Bacc("TRN2", target_bir_lowering=False, num_devices=1)
    arrays = {name: np.ascontiguousarray(inputs[name]) for name in _MATRICES}
    parts = [_columns(inputs["pool_scale"])]
    parts += [_columns(row) for row in np.asarray(inputs["cmp_b1_2"])]
    parts += [_columns(row) for row in np.asarray(inputs["cmp_pe_2"]).reshape(2, 32 * 64)]
    parts += [np.asarray(inputs["sgu_b_s_2"])[0].T]
    arrays["vectors"] = np.ascontiguousarray(np.concatenate(parts, axis=1))
    arrays["shape_consts"] = shape_constants()
    A = {name: nc.dram_tensor(f"in_{name}", a.shape, mybir.dt.from_np(a.dtype), kind="ExternalInput").ap()
         for name, a in arrays.items()}
    out = nc.dram_tensor("out_0", (1, S, D), F32, kind="ExternalOutput").ap()
    build(nc, A, out)
    r = _run(nc, [{f"in_{name}": a for name, a in arrays.items()}], core_ids=[0])
    return r.results[0]["out_0"]
```
